# Optimizing a Trainium2 kernel written in Bass

```python
import math
import jax, jax.numpy as jnp
from jax import lax
import numpy as np

D_MODEL = 1024
BATCH = 1
SEQ = 256
DEPTH = 2

HEAD_DIM = 64
NSA_Q_HEADS = 6
NSA_KV_HEADS = 2
NSA_HPG = NSA_Q_HEADS // NSA_KV_HEADS
NSA_WIDTH = NSA_Q_HEADS * HEAD_DIM
N_BRANCH = 3
NSA_KV_COLS = N_BRANCH * 2 * NSA_KV_HEADS * HEAD_DIM
CMP_BLOCK = 32
CMP_STRIDE = 16
CMP_HIDDEN = 64
SEL_BLOCK = 64
SEL_TOP_N = 16
WINDOW = 512
FORCE_SCORE = 1.0e4
GLA_HEADS = 6
GLA_DK = 32
GLA_DV = 64
GLA_WIDTH = GLA_HEADS * GLA_DV
GLA_GATE_RANK = 16
GLA_GATE_NORM = 16.0
GLA_CHUNK = 64
POOL_WINDOWS = (2, 4, 8, 16)
POOL_GROUPS = 4
POOL_GROUP = 64
POOL_WIDTH = POOL_GROUPS * POOL_GROUP
MIX_WIDTH = NSA_WIDTH + GLA_WIDTH + POOL_WIDTH
SPLIT_SIZES = (NSA_WIDTH, NSA_KV_COLS, NSA_Q_HEADS * N_BRANCH,
               GLA_HEADS * GLA_DK, GLA_HEADS * GLA_DK, GLA_WIDTH, GLA_GATE_RANK, GLA_WIDTH,
               POOL_WIDTH)
P_IN = sum(SPLIT_SIZES)
D_FF = 4 * D_MODEL
ROPE_THETA = 500000.0
ROPE_DIM = HEAD_DIM // 4
Q_BLOCK = 128
SEL_Q_BLOCK = 32
LN_EPS = 1e-5
RMS_EPS = 1e-6
DEEPNORM_ALPHA = (2 * DEPTH) ** 0.25
DEEPNORM_BETA = (8 * DEPTH) ** -0.25


def partial_rope(x, pos):
    half = ROPE_DIM // 2
    inv = ROPE_THETA ** (-jnp.arange(half, dtype=jnp.float32) * 2.0 / ROPE_DIM)
    ang = pos.astype(jnp.float32)[:, None] * inv[None, :]
    cos = jnp.cos(ang).astype(x.dtype)
    sin = jnp.sin(ang).astype(x.dtype)
    x1, x2, xp = x[..., :half], x[..., half:ROPE_DIM], x[..., ROPE_DIM:]
    return jnp.concatenate([x1 * cos - x2 * sin, x1 * sin + x2 * cos, xp], axis=-1)

def layer_norm(x, g, b):
    xf = x.astype(jnp.float32)
    mu = jnp.mean(xf, -1, keepdims=True)
    var = jnp.mean(jnp.square(xf - mu), -1, keepdims=True)
    return ((xf - mu) * lax.rsqrt(var + LN_EPS)).astype(x.dtype) * g + b

def masked_softmax(s, mask):
    s = jnp.where(mask, s.astype(jnp.float32), -jnp.inf)
    m = jnp.max(s, -1, keepdims=True)
    m = jnp.where(jnp.isfinite(m), m, 0.0)
    e = jnp.exp(s - m)
    return e / jnp.maximum(jnp.sum(e, -1, keepdims=True), 1e-30)

def nsa_mixer(q, kv, gates, cmp_pos, cmp_w1, cmp_w2):
    B, S, _ = q.shape
    G, H, Dh = NSA_KV_HEADS, NSA_HPG, HEAD_DIM
    pos = jnp.arange(S)
    q = q.reshape(B, S, G, H, Dh).transpose(0, 2, 3, 1, 4)
    q = partial_rope(q, pos) * (Dh ** -0.5)
    kv = kv.reshape(B, S, N_BRANCH, 2, G, Dh).transpose(2, 3, 0, 4, 1, 5)

    n_cmp = (S - CMP_BLOCK) // CMP_STRIDE + 1
    blk_idx = CMP_STRIDE * jnp.arange(n_cmp)[:, None] + jnp.arange(CMP_BLOCK)[None, :]

    def compress(t, p, w1, w2):
        tb = t[:, :, blk_idx] + p
        hid = jax.nn.gelu(tb.reshape(B, G, n_cmp, CMP_BLOCK * Dh) @ w1)
        return hid @ w2

    kc = compress(partial_rope(kv[0, 0], pos), cmp_pos[0], cmp_w1[0], cmp_w2[0])
    vc = compress(kv[0, 1], cmp_pos[1], cmp_w1[1], cmp_w2[1])
    s_cmp = jnp.einsum('bghsd,bgnd->bghsn', q, kc)
    cmp_mask = blk_idx[:, -1][None, :] <= pos[:, None]
    p_cmp = masked_softmax(s_cmp, cmp_mask)
    o_cmp = jnp.einsum('bghsn,bgnd->bghsd', p_cmp.astype(vc.dtype), vc)

    n_sel = S // SEL_BLOCK
    n_top = min(SEL_TOP_N, n_sel)
    c_lo = blk_idx[:, 0:1]
    s_lo = (SEL_BLOCK * jnp.arange(n_sel))[None, :]
    overlap = jnp.clip(jnp.minimum(c_lo + CMP_BLOCK, s_lo + SEL_BLOCK) - jnp.maximum(c_lo, s_lo), 0, None)
    cmp_to_sel = overlap.astype(jnp.float32) / CMP_BLOCK
    imp = jnp.einsum('bghsn,nj->bgsj', p_cmp, cmp_to_sel)
    cur = (pos // SEL_BLOCK)[:, None]
    jb = jnp.arange(n_sel)[None, :]
    imp = jnp.where((jb == 0) | (jb == cur) | (jb == cur - 1), FORCE_SCORE, imp)
    imp = jnp.where(jb > cur, -FORCE_SCORE, imp)
    _, sel_idx = lax.top_k(imp, n_top)

    k_slc = partial_rope(kv[1, 0], pos).reshape(B, G, n_sel, SEL_BLOCK, Dh)
    v_slc = kv[1, 1].reshape(B, G, n_sel, SEL_BLOCK, Dh)
    nqb = S // SEL_Q_BLOCK
    q_blk = q.reshape(B, G, H, nqb, SEL_Q_BLOCK, Dh).transpose(3, 0, 1, 2, 4, 5)
    idx_blk = sel_idx.reshape(B, G, nqb, SEL_Q_BLOCK, n_top).transpose(2, 0, 1, 3, 4)
    t_blk = pos.reshape(nqb, SEL_Q_BLOCK)
    bi = jnp.arange(B)[:, None, None, None]
    gi = jnp.arange(G)[None, :, None, None]

    def sel_block(args):
        qb, ib, tb = args
        kb = k_slc[bi, gi, ib]
        vb = v_slc[bi, gi, ib]
        s = jnp.einsum('bghqd,bgqnkd->bghqnk', qb, kb)
        kpos = ib[..., None] * SEL_BLOCK + jnp.arange(SEL_BLOCK)
        m = (kpos <= tb[None, None, :, None, None])[:, :, None]
        s = s.reshape(B, G, H, SEL_Q_BLOCK, n_top * SEL_BLOCK)
        m = m.reshape(B, G, 1, SEL_Q_BLOCK, n_top * SEL_BLOCK)
        p = masked_softmax(s, m).reshape(B, G, H, SEL_Q_BLOCK, n_top, SEL_BLOCK)
        return jnp.einsum('bghqnk,bgqnkd->bghqd', p.astype(vb.dtype), vb)

    o_slc = lax.map(sel_block, (q_blk, idx_blk, t_blk))
    o_slc = o_slc.transpose(1, 2, 3, 0, 4, 5).reshape(B, G, H, S, Dh)

    pad = ((0, 0), (0, 0), (WINDOW, 0), (0, 0))
    k_win = jnp.pad(partial_rope(kv[2, 0], pos), pad)
    v_win = jnp.pad(kv[2, 1], pad)
    nwb = S // Q_BLOCK
    span = WINDOW + Q_BLOCK
    q_wb = q.reshape(B, G, H, nwb, Q_BLOCK, Dh).transpose(3, 0, 1, 2, 4, 5)
    starts = jnp.arange(nwb) * Q_BLOCK

    def win_block(args):
        qb, s0 = args
        kb = lax.dynamic_slice_in_dim(k_win, s0, span, axis=2)
        vb = lax.dynamic_slice_in_dim(v_win, s0, span, axis=2)
        s = jnp.einsum('bghqd,bgkd->bghqk', qb, kb)
        tq = s0 + jnp.arange(Q_BLOCK)
        tk = s0 - WINDOW + jnp.arange(span)
        diff = tq[:, None] - tk[None, :]
        m = (diff >= 0) & (diff < WINDOW) & (tk[None, :] >= 0)
        p = masked_softmax(s, m)
        return jnp.einsum('bghqk,bgkd->bghqd', p.astype(vb.dtype), vb)

    o_win = lax.map(win_block, (q_wb, starts))
    o_win = o_win.transpose(1, 2, 3, 0, 4, 5).reshape(B, G, H, S, Dh)

    gt = jax.nn.sigmoid(gates.reshape(B, S, G, H, N_BRANCH).transpose(0, 2, 3, 1, 4))
    o = gt[..., 0:1] * o_cmp + gt[..., 1:2] * o_slc + gt[..., 2:3] * o_win
    return o.transpose(0, 3, 1, 2, 4).reshape(B, S, NSA_WIDTH)

def gla_mixer(q, k, v, g_lr, og, w_gate2, b_gate, norm_g):
    B, S, _ = q.shape
    Hh, dk, dv, C = GLA_HEADS, GLA_DK, GLA_DV, GLA_CHUNK
    N = S // C
    f32 = jnp.float32
    gk = jax.nn.log_sigmoid((g_lr @ w_gate2 + b_gate).astype(f32)) / GLA_GATE_NORM

    def chunks(t, d):
        return t.astype(f32).reshape(B, N, C, Hh, d).transpose(0, 3, 1, 2, 4)

    qc = chunks(q, dk) * (dk ** -0.5)
    kc = chunks(k, dk)
    vc = chunks(v, dv)
    bcum = jnp.cumsum(chunks(gk, dk), axis=3)
    blast = bcum[:, :, :, -1:]
    q_dec = qc * jnp.exp(bcum)
    k_inv = kc * jnp.exp(-bcum)
    k_end = kc * jnp.exp(blast - bcum)
    causal = jnp.tril(jnp.ones((C, C), bool))
    a = jnp.where(causal, jnp.einsum('bhnid,bhnjd->bhnij', q_dec, k_inv), 0.0)
    o_intra = jnp.einsum('bhnij,bhnjv->bhniv', a, vc)
    d_state = jnp.einsum('bhncd,bhncv->bhndv', k_end, vc)
    decay = jnp.exp(blast[:, :, :, 0])

    def step(s_prev, inp):
        dcy, ds = inp
        return s_prev * dcy[..., None] + ds, s_prev

    _, s_in = lax.scan(step, jnp.zeros((B, Hh, dk, dv), f32),
                       (decay.transpose(2, 0, 1, 3), d_state.transpose(2, 0, 1, 3, 4)))
    s_in = s_in.transpose(1, 2, 0, 3, 4)
    o = o_intra + jnp.einsum('bhncd,bhndv->bhncv', q_dec, s_in)
    o = o * lax.rsqrt(jnp.mean(o * o, -1, keepdims=True) + RMS_EPS)
    o = o.transpose(0, 2, 3, 1, 4).reshape(B, S, GLA_WIDTH).astype(og.dtype)
    return o * norm_g * jax.nn.silu(og)

def pool_mixer(u, w_pool, scale):
    B, S, Cw = u.shape
    uf = u.astype(jnp.float32)
    cs = jnp.pad(jnp.cumsum(uf, axis=1), ((0, 0), (1, 0), (0, 0)))
    win = jnp.repeat(jnp.array(POOL_WINDOWS, jnp.int32), POOL_GROUP)
    t = jnp.arange(S)[:, None]
    lo = jnp.maximum(t + 1 - win[None, :], 0)
    cnt = jnp.minimum(t + 1, win[None, :]).astype(jnp.float32)
    lo_sum = jnp.take_along_axis(cs, jnp.broadcast_to(lo[None], (B, S, Cw)), axis=1)
    pooled = (cs[:, 1:] - lo_sum) / cnt - uf
    y = jnp.einsum('bsgc,gcd->bsgd', pooled.reshape(B, S, POOL_GROUPS, POOL_GROUP).astype(u.dtype), w_pool)
    return y.reshape(B, S, POOL_WIDTH) * scale

def first_inputs(seed: int = 0) -> dict:
    key = jax.random.key(seed)
    ks = jax.random.split(key, 20)
    L, D = DEPTH, D_MODEL
    nrm = lambda k, shape, s: jax.random.normal(k, shape, jnp.float32) * s
    return {
        "x": nrm(ks[0], (BATCH, SEQ, D), 1.0),
        "w_in": nrm(ks[1], (L, D, P_IN), D ** -0.5),
        "cmp_pos": nrm(ks[2], (L, 2, CMP_BLOCK, HEAD_DIM), 0.1),
        "cmp_w1": nrm(ks[3], (L, 2, CMP_BLOCK * HEAD_DIM, CMP_HIDDEN), (CMP_BLOCK * HEAD_DIM) ** -0.5),
        "cmp_w2": nrm(ks[4], (L, 2, CMP_HIDDEN, HEAD_DIM), CMP_HIDDEN ** -0.5),
        "gla_w_gate2": nrm(ks[5], (L, GLA_GATE_RANK, GLA_HEADS * GLA_DK), GLA_GATE_RANK ** -0.5),
        "gla_b_gate": nrm(ks[6], (L, GLA_HEADS * GLA_DK), 0.01),
        "gla_norm_g": 1.0 + nrm(ks[7], (L, GLA_WIDTH), 0.02),
        "pool_w": nrm(ks[8], (L, POOL_GROUPS, POOL_GROUP, POOL_GROUP), POOL_GROUP ** -0.5),
        "pool_scale": 1.0 + nrm(ks[9], (L, POOL_WIDTH), 0.02),
        "w_out": nrm(ks[10], (L, MIX_WIDTH, D), MIX_WIDTH ** -0.5 * DEEPNORM_BETA),
        "ln1_g": 1.0 + nrm(ks[11], (L, D), 0.02),
        "ln1_b": nrm(ks[12], (L, D), 0.02),
        "w_up": nrm(ks[13], (L, D, D_FF), D ** -0.5),
        "w_down": nrm(ks[14], (L, D_FF, D), D_FF ** -0.5 * DEEPNORM_BETA),
        "ln2_g": 1.0 + nrm(ks[15], (L, D), 0.02),
        "ln2_b": nrm(ks[16], (L, D), 0.02),
    }

def first_block(x, w_in, cmp_pos, cmp_w1, cmp_w2, gla_w_gate2, gla_b_gate, gla_norm_g, pool_w, pool_scale,
              w_out, ln1_g, ln1_b, w_up, w_down, ln2_g, ln2_b):
    split_points = []
    acc = 0
    for sz in SPLIT_SIZES[:-1]:
        acc += sz
        split_points.append(acc)
    h = x
    for l in range(DEPTH):
        proj = h @ w_in[l]
        nq, nkv, ngate, gq, gk, gv, glr, gog, pu = jnp.split(proj, split_points, axis=-1)
        mixed = jnp.concatenate([
            nsa_mixer(nq, nkv, ngate, cmp_pos[l], cmp_w1[l], cmp_w2[l]),
            gla_mixer(gq, gk, gv, glr, gog, gla_w_gate2[l], gla_b_gate[l], gla_norm_g[l]),
            pool_mixer(pu, pool_w[l], pool_scale[l]),
        ], axis=-1)
        h = layer_norm(DEEPNORM_ALPHA * h + mixed @ w_out[l], ln1_g[l], ln1_b[l])
        ff = jnp.square(jax.nn.relu(h @ w_up[l])) @ w_down[l]
        h = layer_norm(DEEPNORM_ALPHA * h + ff, ln2_g[l], ln2_b[l])
    return h


N_META = 16
BLOCK = 128
PAD = BLOCK - N_META

D_RNN = D_MODEL
LRU_BLOCKS = 8
LRU_BS = D_RNN // LRU_BLOCKS
LRU_C = 8.0
CONV_A = 4

N_Q_HEADS = 16
N_KV_HEADS = 2
Q_PER_KV = N_Q_HEADS // N_KV_HEADS
WINDOW_2 = 128
Q_DIM = N_Q_HEADS * HEAD_DIM
KV_DIM = N_KV_HEADS * HEAD_DIM

EVEN_IN = 2 * D_RNN + Q_DIM + 2 * KV_DIM
EVEN_MIX = D_RNN + Q_DIM

D_SSM = 2 * D_MODEL
SSD_HEADDIM = 64
SSD_HEADS = D_SSM // SSD_HEADDIM
SSD_GROUPS = 8
SSD_HPG = SSD_HEADS // SSD_GROUPS
SSD_STATE = 128
CONV_C = 4
SSD_CONV_DIM = D_SSM + 2 * SSD_GROUPS * SSD_STATE
ODD_IN = D_SSM + SSD_CONV_DIM + SSD_HEADS

D_FF_2 = 2816
CONV_F = 3

EPS = 1e-6


def rms_norm(x, w):
    x32 = x.astype(jnp.float32)
    y = x32 * lax.rsqrt(jnp.mean(x32 * x32, axis=-1, keepdims=True) + EPS)
    return (y * w.astype(jnp.float32)).astype(x.dtype)

def causal_dwconv(x, w, b):
    k = w.shape[0]
    y = lax.conv_general_dilated(
        x, w[:, None, :].astype(x.dtype), window_strides=(1,), padding=[(k - 1, 0)],
        dimension_numbers=("NWC", "WIO", "NWC"), feature_group_count=x.shape[-1])
    return y + b.astype(x.dtype)

def alibi_slopes(n_heads):
    return 2.0 ** (-8.0 * jnp.arange(1, n_heads + 1, dtype=jnp.float32) / n_heads)

def rg_lru(x, w_a, b_a, w_x, b_x, lam):
    bsz, L, _ = x.shape
    x32 = x.astype(jnp.float32)
    xb = x32.reshape(bsz, L, LRU_BLOCKS, LRU_BS)
    r = jax.nn.sigmoid(jnp.einsum("blni,nij->blnj", xb, w_a.astype(jnp.float32)).reshape(bsz, L, D_RNN) + b_a)
    i = jax.nn.sigmoid(jnp.einsum("blni,nij->blnj", xb, w_x.astype(jnp.float32)).reshape(bsz, L, D_RNN) + b_x)
    log_a = -LRU_C * r * jax.nn.softplus(-lam.astype(jnp.float32))
    a = jnp.exp(log_a)
    u = jnp.sqrt(-jnp.expm1(2.0 * log_a)) * (i * x32)

    def combine(c1, c2):
        a1, b1 = c1
        a2, b2 = c2
        return a1 * a2, a2 * b1 + b2

    _, h = lax.associative_scan(combine, (a, u), axis=1)
    return h.astype(x.dtype)

def swa_sink_alibi(q, k, v, sinks):
    bsz, L = q.shape[:2]
    Lp = L + PAD
    nblk = Lp // BLOCK
    q = q.astype(jnp.float32)
    k = k.astype(jnp.float32)
    v = v.astype(jnp.float32)
    padw = ((0, 0), (PAD, 0), (0, 0), (0, 0))
    qb = jnp.pad(q, padw).reshape(bsz, nblk, BLOCK, N_KV_HEADS, Q_PER_KV, HEAD_DIM)
    kb = jnp.pad(k, padw).reshape(bsz, nblk, BLOCK, N_KV_HEADS, HEAD_DIM)
    vb = jnp.pad(v, padw).reshape(bsz, nblk, BLOCK, N_KV_HEADS, HEAD_DIM)
    shift = ((0, 0), (1, 0), (0, 0), (0, 0), (0, 0))
    k_band = jnp.concatenate([jnp.pad(kb, shift)[:, :-1], kb], axis=2)
    v_band = jnp.concatenate([jnp.pad(vb, shift)[:, :-1], vb], axis=2)
    k_meta = k[:, :N_META]
    v_meta = v[:, :N_META]
    scale = HEAD_DIM ** -0.5
    s_band = jnp.einsum("bnqkgd,bnskd->bnkgqs", qb, k_band) * scale
    s_meta = jnp.einsum("bnqkgd,bmkd->bnkgqm", qb, k_meta) * scale

    blk = jnp.arange(nblk)
    t = blk[:, None] * BLOCK + jnp.arange(BLOCK)[None, :] - PAD
    s = (blk[:, None] - 1) * BLOCK + jnp.arange(2 * BLOCK)[None, :] - PAD
    dist_band = t[:, :, None] - s[:, None, :]
    band_ok = (s[:, None, :] >= N_META) & (dist_band >= 0) & (dist_band < WINDOW_2)
    dist_meta = t[:, :, None] - jnp.arange(N_META)[None, None, :]
    meta_ok = dist_meta >= 0

    slopes = alibi_slopes(N_Q_HEADS).reshape(N_KV_HEADS, Q_PER_KV)[:, :, None, None]
    pen_band = slopes * dist_band[:, None, None].astype(jnp.float32)
    pen_meta = slopes * jnp.minimum(dist_meta, WINDOW_2)[:, None, None].astype(jnp.float32)
    s_band = jnp.where(band_ok[:, None, None], s_band - pen_band, -jnp.inf)
    s_meta = jnp.where(meta_ok[:, None, None], s_meta - pen_meta, -jnp.inf)

    sink = sinks.astype(jnp.float32).reshape(N_KV_HEADS, Q_PER_KV)[:, :, None, None]
    mx = jnp.maximum(jnp.maximum(s_band.max(-1, keepdims=True), s_meta.max(-1, keepdims=True)), sink)
    p_band = jnp.exp(s_band - mx)
    p_meta = jnp.exp(s_meta - mx)
    denom = p_band.sum(-1, keepdims=True) + p_meta.sum(-1, keepdims=True) + jnp.exp(sink - mx)
    p_band = p_band / denom
    p_meta = p_meta / denom
    o = (jnp.einsum("bnkgqs,bnskd->bnqkgd", p_band, v_band)
         + jnp.einsum("bnkgqm,bmkd->bnqkgd", p_meta, v_meta))
    return o.reshape(bsz, Lp, Q_DIM)[:, PAD:]

def griffin_swa_mixer(u, w_in, conv_w, conv_b, w_a, b_a, w_x, b_x, lam, sinks, w_out):
    bsz, L, _ = u.shape
    proj = u @ w_in
    gate, xr, q, k, v = jnp.split(
        proj, [D_RNN, 2 * D_RNN, 2 * D_RNN + Q_DIM, 2 * D_RNN + Q_DIM + KV_DIM], axis=-1)
    xr = causal_dwconv(xr, conv_w, conv_b)
    y_a = jax.nn.gelu(gate, approximate=True) * rg_lru(xr, w_a, b_a, w_x, b_x, lam)
    y_b = swa_sink_alibi(q.reshape(bsz, L, N_Q_HEADS, HEAD_DIM),
                         k.reshape(bsz, L, N_KV_HEADS, HEAD_DIM),
                         v.reshape(bsz, L, N_KV_HEADS, HEAD_DIM), sinks).astype(u.dtype)
    return jnp.concatenate([y_a, y_b], axis=-1) @ w_out

def ssd_chunked(x, dt, a, b_in, c_in):
    bsz, Lp = x.shape[:2]
    nc = Lp // BLOCK
    x = x.reshape(bsz, nc, BLOCK, SSD_GROUPS, SSD_HPG, SSD_HEADDIM)
    dt = dt.reshape(bsz, nc, BLOCK, SSD_GROUPS, SSD_HPG)
    bc = b_in.reshape(bsz, nc, BLOCK, SSD_GROUPS, SSD_STATE)
    cc = c_in.reshape(bsz, nc, BLOCK, SSD_GROUPS, SSD_STATE)
    cs = jnp.cumsum(dt * a.reshape(SSD_GROUPS, SSD_HPG), axis=2)
    xdt = x * dt[..., None]
    cs_t = jnp.moveaxis(cs, 2, -1)
    seg = cs_t[..., :, None] - cs_t[..., None, :]
    tril = jnp.tril(jnp.ones((BLOCK, BLOCK), dtype=bool))
    decay_in = jnp.exp(jnp.where(tril, seg, -jnp.inf))
    cb = jnp.einsum("bclgn,bcsgn->bcgls", cc, bc)
    y_diag = jnp.einsum("bcgls,bcghls,bcsghp->bclghp", cb, decay_in, xdt)
    cs_last = cs[:, :, -1:]
    chunk_states = jnp.einsum("bclgn,bclgh,bclghp->bcghpn", bc, jnp.exp(cs_last - cs), xdt)
    chunk_decay = jnp.exp(cs_last[:, :, 0])

    def step(state, inp):
        dec, st = inp
        return state * dec[..., None, None] + st, state

    init = jnp.zeros_like(chunk_states[:, 0])
    _, prev = lax.scan(step, init, (jnp.moveaxis(chunk_decay, 1, 0), jnp.moveaxis(chunk_states, 1, 0)))
    prev = jnp.moveaxis(prev, 0, 1)
    y_off = jnp.einsum("bclgn,bcghpn,bclgh->bclghp", cc, prev, jnp.exp(cs))
    return (y_diag + y_off).reshape(bsz, Lp, SSD_HEADS, SSD_HEADDIM)

def mamba2_mixer(u, w_in, conv_w, conv_b, dt_bias, a_log, d_skip, gate_norm, w_out):
    bsz, L, _ = u.shape
    proj = u @ w_in
    z, xbc, dt = jnp.split(proj, [D_SSM, D_SSM + SSD_CONV_DIM], axis=-1)
    xbc = jax.nn.silu(causal_dwconv(xbc, conv_w, conv_b))
    xs, bs, cs = jnp.split(xbc, [D_SSM, D_SSM + SSD_GROUPS * SSD_STATE], axis=-1)
    xs = xs.reshape(bsz, L, SSD_HEADS, SSD_HEADDIM).astype(jnp.float32)
    bs = bs.reshape(bsz, L, SSD_GROUPS, SSD_STATE).astype(jnp.float32)
    cs = cs.reshape(bsz, L, SSD_GROUPS, SSD_STATE).astype(jnp.float32)
    dt = jax.nn.softplus(dt.astype(jnp.float32) + dt_bias.astype(jnp.float32))
    a = -jnp.exp(a_log.astype(jnp.float32))

    def front_pad(t):
        return jnp.pad(t, ((0, 0), (PAD, 0)) + ((0, 0),) * (t.ndim - 2))

    y = ssd_chunked(front_pad(xs), front_pad(dt), a, front_pad(bs), front_pad(cs))[:, PAD:]
    y = y + d_skip.astype(jnp.float32)[:, None] * xs
    y = y.reshape(bsz, L, D_SSM) * jax.nn.silu(z.astype(jnp.float32))
    yg = y.reshape(bsz, L, SSD_GROUPS, D_SSM // SSD_GROUPS)
    yg = yg * lax.rsqrt(jnp.mean(yg * yg, axis=-1, keepdims=True) + EPS)
    y = yg.reshape(bsz, L, D_SSM) * gate_norm.astype(jnp.float32)
    return y.astype(u.dtype) @ w_out

def conv_ffn(u, w_up, conv_w, conv_b, w_down):
    h = causal_dwconv(u @ w_up, conv_w, conv_b)
    g, up = jnp.split(h, 2, axis=-1)
    return (jax.nn.gelu(g, approximate=True) * up) @ w_down

def second_inputs(seed: int = 0) -> dict:
    key = jax.random.key(seed)
    k = jax.random.split(key, 36)

    def normal(kk, shape, scale):
        return jax.random.normal(kk, shape, jnp.float32) * scale

    def gain(kk, n):
        return 1.0 + 0.05 * jax.random.normal(kk, (n,), jnp.float32)

    u = jax.random.uniform(k[11], (D_RNN,), jnp.float32, 0.9, 0.999)
    a0 = u ** (1.0 / LRU_C)
    lru_lambda = jnp.log(a0) - jnp.log1p(-a0)
    dt0 = jnp.exp(jax.random.uniform(k[25], (SSD_HEADS,), jnp.float32, math.log(1e-3), math.log(1e-1)))
    dt_bias = dt0 + jnp.log(-jnp.expm1(-dt0))
    a_log = jnp.log(jax.random.uniform(k[26], (SSD_HEADS,), jnp.float32, 1.0, 16.0))

    return {
        "x": normal(k[0], (BATCH, SEQ, D_MODEL), 1.0),
        "meta_tokens": normal(k[1], (N_META, D_MODEL), 1.0),
        "l0_mix_pre_norm": gain(k[2], D_MODEL),
        "l0_mix_post_norm": gain(k[3], D_MODEL),
        "l0_w_in": normal(k[4], (D_MODEL, EVEN_IN), D_MODEL ** -0.5),
        "l0_lru_conv_w": normal(k[5], (CONV_A, D_RNN), CONV_A ** -0.5),
        "l0_lru_conv_b": normal(k[6], (D_RNN,), 0.01),
        "l0_lru_w_a": normal(k[7], (LRU_BLOCKS, LRU_BS, LRU_BS), LRU_BS ** -0.5),
        "l0_lru_b_a": normal(k[8], (D_RNN,), 0.01),
        "l0_lru_w_x": normal(k[9], (LRU_BLOCKS, LRU_BS, LRU_BS), LRU_BS ** -0.5),
        "l0_lru_b_x": normal(k[10], (D_RNN,), 0.01),
        "l0_lru_lambda": lru_lambda,
        "l0_attn_sinks": normal(k[12], (N_Q_HEADS,), 0.5),
        "l0_w_out": normal(k[13], (EVEN_MIX, D_MODEL), EVEN_MIX ** -0.5),
        "l0_ffn_pre_norm": gain(k[14], D_MODEL),
        "l0_ffn_post_norm": gain(k[15], D_MODEL),
        "l0_ffn_w_up": normal(k[16], (D_MODEL, 2 * D_FF_2), D_MODEL ** -0.5),
        "l0_ffn_conv_w": normal(k[17], (CONV_F, 2 * D_FF_2), CONV_F ** -0.5),
        "l0_ffn_conv_b": normal(k[18], (2 * D_FF_2,), 0.01),
        "l0_ffn_w_down": normal(k[19], (D_FF_2, D_MODEL), D_FF_2 ** -0.5),
        "l1_mix_pre_norm": gain(k[20], D_MODEL),
        "l1_mix_post_norm": gain(k[21], D_MODEL),
        "l1_w_in": normal(k[22], (D_MODEL, ODD_IN), D_MODEL ** -0.5),
        "l1_ssm_conv_w": normal(k[23], (CONV_C, SSD_CONV_DIM), CONV_C ** -0.5),
        "l1_ssm_conv_b": normal(k[24], (SSD_CONV_DIM,), 0.01),
        "l1_dt_bias": dt_bias,
        "l1_a_log": a_log,
        "l1_d_skip": 1.0 + 0.1 * jax.random.normal(k[27], (SSD_HEADS,), jnp.float32),
        "l1_gate_norm": gain(k[28], D_SSM),
        "l1_w_out": normal(k[29], (D_SSM, D_MODEL), D_SSM ** -0.5),
        "l1_ffn_pre_norm": gain(k[30], D_MODEL),
        "l1_ffn_post_norm": gain(k[31], D_MODEL),
        "l1_ffn_w_up": normal(k[32], (D_MODEL, 2 * D_FF_2), D_MODEL ** -0.5),
        "l1_ffn_conv_w": normal(k[33], (CONV_F, 2 * D_FF_2), CONV_F ** -0.5),
        "l1_ffn_conv_b": normal(k[34], (2 * D_FF_2,), 0.01),
        "l1_ffn_w_down": normal(k[35], (D_FF_2, D_MODEL), D_FF_2 ** -0.5),
    }

def second_block(x, meta_tokens,
              l0_mix_pre_norm, l0_mix_post_norm, l0_w_in, l0_lru_conv_w, l0_lru_conv_b,
              l0_lru_w_a, l0_lru_b_a, l0_lru_w_x, l0_lru_b_x, l0_lru_lambda, l0_attn_sinks, l0_w_out,
              l0_ffn_pre_norm, l0_ffn_post_norm, l0_ffn_w_up, l0_ffn_conv_w, l0_ffn_conv_b, l0_ffn_w_down,
              l1_mix_pre_norm, l1_mix_post_norm, l1_w_in, l1_ssm_conv_w, l1_ssm_conv_b,
              l1_dt_bias, l1_a_log, l1_d_skip, l1_gate_norm, l1_w_out,
              l1_ffn_pre_norm, l1_ffn_post_norm, l1_ffn_w_up, l1_ffn_conv_w, l1_ffn_conv_b, l1_ffn_w_down):
    bsz = x.shape[0]
    meta = jnp.broadcast_to(meta_tokens.astype(x.dtype)[None], (bsz, N_META, D_MODEL))
    h = jnp.concatenate([meta, x], axis=1)
    layers = [
        (l0_mix_pre_norm, l0_mix_post_norm,
         (l0_w_in, l0_lru_conv_w, l0_lru_conv_b, l0_lru_w_a, l0_lru_b_a, l0_lru_w_x, l0_lru_b_x,
          l0_lru_lambda, l0_attn_sinks, l0_w_out),
         (l0_ffn_pre_norm, l0_ffn_post_norm, l0_ffn_w_up, l0_ffn_conv_w, l0_ffn_conv_b, l0_ffn_w_down)),
        (l1_mix_pre_norm, l1_mix_post_norm,
         (l1_w_in, l1_ssm_conv_w, l1_ssm_conv_b, l1_dt_bias, l1_a_log, l1_d_skip, l1_gate_norm, l1_w_out),
         (l1_ffn_pre_norm, l1_ffn_post_norm, l1_ffn_w_up, l1_ffn_conv_w, l1_ffn_conv_b, l1_ffn_w_down)),
    ]
    for i in range(DEPTH):
        pre, post, mix, ffn = layers[i]
        mixer = griffin_swa_mixer if i % 2 == 0 else mamba2_mixer
        h = h + rms_norm(mixer(rms_norm(h, pre), *mix), post)
        f_pre, f_post, w_up, c_w, c_b, w_down = ffn
        h = h + rms_norm(conv_ffn(rms_norm(h, f_pre), w_up, c_w, c_b, w_down), f_post)
    return h[:, N_META:]


def setup_inputs(seed=0):
    out = dict(first_inputs(seed))
    for name, value in second_inputs(seed + 1).items():
        if name != "x":
            out[name + "_2"] = value
    return out


def reference(
    x, w_in, cmp_pos, cmp_w1, cmp_w2, gla_w_gate2, gla_b_gate, gla_norm_g, pool_w, pool_scale,
    w_out, ln1_g, ln1_b, w_up, w_down, ln2_g, ln2_b, meta_tokens_2, l0_mix_pre_norm_2,
    l0_mix_post_norm_2, l0_w_in_2, l0_lru_conv_w_2, l0_lru_conv_b_2, l0_lru_w_a_2, l0_lru_b_a_2,
    l0_lru_w_x_2, l0_lru_b_x_2, l0_lru_lambda_2, l0_attn_sinks_2, l0_w_out_2, l0_ffn_pre_norm_2,
    l0_ffn_post_norm_2, l0_ffn_w_up_2, l0_ffn_conv_w_2, l0_ffn_conv_b_2, l0_ffn_w_down_2,
    l1_mix_pre_norm_2, l1_mix_post_norm_2, l1_w_in_2, l1_ssm_conv_w_2, l1_ssm_conv_b_2,
    l1_dt_bias_2, l1_a_log_2, l1_d_skip_2, l1_gate_norm_2, l1_w_out_2, l1_ffn_pre_norm_2,
    l1_ffn_post_norm_2, l1_ffn_w_up_2, l1_ffn_conv_w_2, l1_ffn_conv_b_2, l1_ffn_w_down_2,
):
    x = first_block(
        x, w_in, cmp_pos, cmp_w1, cmp_w2, gla_w_gate2, gla_b_gate, gla_norm_g, pool_w,
        pool_scale, w_out, ln1_g, ln1_b, w_up, w_down, ln2_g, ln2_b,
    )
    return second_block(
        x, meta_tokens_2, l0_mix_pre_norm_2, l0_mix_post_norm_2, l0_w_in_2, l0_lru_conv_w_2,
        l0_lru_conv_b_2, l0_lru_w_a_2, l0_lru_b_a_2, l0_lru_w_x_2, l0_lru_b_x_2,
        l0_lru_lambda_2, l0_attn_sinks_2, l0_w_out_2, l0_ffn_pre_norm_2, l0_ffn_post_norm_2,
        l0_ffn_w_up_2, l0_ffn_conv_w_2, l0_ffn_conv_b_2, l0_ffn_w_down_2, l1_mix_pre_norm_2,
        l1_mix_post_norm_2, l1_w_in_2, l1_ssm_conv_w_2, l1_ssm_conv_b_2, l1_dt_bias_2,
        l1_a_log_2, l1_d_skip_2, l1_gate_norm_2, l1_w_out_2, l1_ffn_pre_norm_2,
        l1_ffn_post_norm_2, l1_ffn_w_up_2, l1_ffn_conv_w_2, l1_ffn_conv_b_2, l1_ffn_w_down_2,
    )


_drawn_inputs = setup_inputs


def setup_inputs(seed=0):
    import zlib

    import numpy as np

    out = dict(_drawn_inputs(seed))
    spreads = {}
    factors = {'gla_b_gate': 8.0,
     'gla_norm_g': 8.0,
     'pool_scale': 8.0,
     'l0_lru_b_a_2': 39.829,
     'l0_lru_b_x_2': 8.0,
     'l0_ffn_conv_b_2': 5.399,
     'l1_ssm_conv_b_2': 7.753,
     'l1_ffn_conv_b_2': 8.0,
     'cmp_pos': 4.088}
    for name, (base, spread) in spreads.items():
        noise = np.random.default_rng([zlib.crc32(name.encode()), seed]).standard_normal(out[name].shape)
        drawn = base * np.exp(spread * noise) if base else spread * noise
        out[name] = __import__('jax').numpy.asarray(drawn.astype(out[name].dtype))
    for name, factor in factors.items():
        out[name] = (out[name] * factor).astype(out[name].dtype)
    return out
```

```python
from contextlib import ExitStack

import numpy as np
import concourse.bass as bass
from concourse import mybir

P = 128
F32 = mybir.dt.float32
ALU = mybir.AluOpType
ACT = mybir.ActivationFunctionType
AX_X = mybir.AxisListType.X

D = 1024
KT = D // P
S = 256
DEPTH = 2
META = 16
T = S + META
HD = 64
NSA_J = 3
CMP_N, CMP_BLOCK, CMP_STRIDE = 15, 32, 16
GLA_H, GLA_DK, GLA_DV, GLA_C = 6, 32, 64, 64
D_FF = 4096
FT1 = D_FF // P
D_FF2 = 2816
FT2 = D_FF2 // P
SWA_J = 8
SWA_WINDOW = 128
SSM_TILES = 16
SSM_G = 8
SSM_HEADS = 32
CHUNKS = [(0, META), (META, P), (META + P, P)]
ALPHA = float((2 * DEPTH) ** 0.25)
LN_EPS, RMS_EPS = 1e-5, 1e-6
MASKED = -1.0e30
MAX_FLOOR = -1.0e29
SLOT = 2048
RING = 8
GLA_BANKS = [4, 7, 2, 3]
GB = 4


def nsa_gla_pool_tiles():
    q0, kv0, gate0 = 0, 384, 384 + 768
    gq0 = gate0 + 18
    gk0, gv0 = gq0 + 192, gq0 + 384
    glr0 = gv0 + 384
    og0 = glr0 + 16
    pu0 = og0 + 384
    kv = lambda branch, which: [kv0 + (branch * 2 + which) * 128 + i for i in range(128)]
    q = lambda j: [q0 + (g * NSA_J + j) * HD + i for g in range(2) for i in range(HD)]
    run = lambda a, n: list(range(a, a + n))
    tiles = [kv(0, 0), kv(1, 0), kv(2, 0), q(0), q(1), q(2), kv(0, 1), kv(1, 1), kv(2, 1)]
    tiles.append(run(glr0, 16) + [None] * 16 + run(gate0, 18))
    tiles += [run(gq0, 128), run(gq0 + 128, 64) + [None] * 64, run(gk0, 128), run(gk0 + 128, 64) + [None] * 64]
    tiles += [run(gv0 + 128 * i, 128) for i in range(3)]
    tiles += [run(og0 + 128 * i, 128) for i in range(3)]
    tiles += [run(pu0 + 128 * i, 128) for i in range(2)]
    return tiles


T_KC, T_KS, T_KW, T_Q, T_VC, T_VS, T_VW, T_LR, T_GQ, T_GK, T_GV, T_OG, T_PU = 0, 1, 2, 3, 6, 7, 8, 9, 10, 12, 14, 17, 20
N_IN1 = 22


def griffin_tiles():
    run = lambda a, n: list(range(a, a + n))
    gate0, xr0, q0, k0, v0 = 0, D, 2 * D, 3 * D, 3 * D + 128
    tiles = [run(xr0 + 128 * i, 128) for i in range(8)]
    tiles += [run(gate0 + 128 * i, 128) for i in range(8)]
    tiles += [[q0 + (g * SWA_J + j) * HD + i for g in range(2) for i in range(HD)] for j in range(SWA_J)]
    return tiles + [run(k0, 128), run(v0, 128)]


def mamba_tiles():
    run = lambda a, n: list(range(a, a + n))
    z0, x0, b0, c0, dt0 = 0, 2048, 4096, 5120, 6144
    tiles = [run(dt0, 32)]
    tiles += [run(x0 + 128 * i, 128) for i in range(16)]
    tiles += [run(b0 + 128 * i, 128) for i in range(8)]
    tiles += [run(c0 + 128 * i, 128) for i in range(8)]
    return tiles + [run(z0 + 128 * i, 128) for i in range(16)]


def straight_tiles(n):
    return [list(range(P * i, P * i + P)) for i in range(n)]


def ffn2_up_tiles():
    out = []
    for i in range(FT2):
        out += [list(range(P * i, P * i + P)), list(range(D_FF2 + P * i, D_FF2 + P * i + P))]
    return out


def nsa_mix_rows():
    rows = [(g * NSA_J + j) * HD + i for j in range(NSA_J) for g in range(2) for i in range(HD)]
    return rows + list(range(384, 1024))


def griffin_mix_rows():
    rows = list(range(D))
    return rows + [D + (g * SWA_J + j) * HD + i for j in range(SWA_J) for g in range(2) for i in range(HD)]


def stream_items():
    items = []
    for l in range(DEPTH):
        items.append(("product", f"in1_{l}", KT, [len(t) for t in nsa_gla_pool_tiles()]))
        items.append(("matrix", f"cmp_{l}_0", 2048))
        items.append(("matrix", f"cmp_{l}_1", 2048))
        items.append(("matrix", f"misc_{l}", 512))
        items.append(("product", f"out1_{l}", KT, [P] * KT))
        items.append(("product", f"up1_{l}", KT, [P] * FT1))
        items.append(("product", f"down1_{l}", FT1, [P] * KT))
    items.append(("product", "in_g", KT, [P] * 26))
    items.append(("matrix", "lru", 2048))
    items.append(("product", "out_g", 16, [P] * KT))
    items.append(("product", "up2_0", KT, [P] * (2 * FT2)))
    items.append(("product", "down2_0", FT2, [P] * KT))
    items.append(("product", "in_m", KT, [len(t) for t in mamba_tiles()]))
    items.append(("product", "out_m", SSM_TILES, [P] * KT))
    items.append(("product", "up2_1", KT, [P] * (2 * FT2)))
    items.append(("product", "down2_1", FT2, [P] * KT))
    return items


def plan_stream():
    slots, products, matrices = [], {}, {}
    at, tile = 0, 0

    def slot(name, width, first_k=0, ks=0, tiles=()):
        nonlocal at
        slots.append(dict(name=name, at=at, width=width, first_k=first_k, ks=ks, tiles=tiles, release=None))
        at += width
        return len(slots) - 1

    for kind, name, *rest in stream_items():
        if kind == "matrix":
            matrices[name] = slot(name, rest[0])
            continue
        kt, widths = rest
        steps = []
        i = 0
        while i < len(widths):
            pair = [i]
            if i + 1 < len(widths):
                pair.append(i + 1)
            cols = sum(widths[j] for j in pair)
            for k0 in range(0, kt, 8):
                ks = min(8, kt - k0)
                steps.append((slot(name, ks * cols, k0, ks, tuple(pair)), pair, k0, ks))
            i += len(pair)
        products[name] = dict(first=tile, kt=kt, widths=widths, steps=steps)
        tile += len(widths)
    return slots, products, matrices, at


class Columns:

    def __init__(self):
        self.n, self.at = 0, {}

    def add(self, name, width):
        self.at[name] = self.n
        self.n += width

    def __getitem__(self, name):
        return self.at[name]


def parameter_columns():
    c = Columns()
    for l in range(DEPTH):
        for name, w in (("pos", 64), ("b_gate", 2), ("norm_g", 3), ("pool_scale", 2),
                        ("ln1_g", 8), ("ln1_b", 8), ("ln2_g", 8), ("ln2_b", 8)):
            c.add(f"{name}{l}", w)
    for l in range(2):
        for name in ("mix_pre", "mix_post", "ffn_pre", "ffn_post"):
            c.add(f"{name}{l}", 8)
        c.add(f"ffn_w{l}", 3 * 2 * FT2)
        c.add(f"ffn_b{l}", 2 * FT2)
    c.add("lru_w", 32)
    for name in ("lru_b", "lru_ba", "lru_bx", "lru_lam"):
        c.add(name, 8)
    c.add("sinks", 16)
    c.add("sinks_last", 2)
    c.add("ssm_w", 4 * 32)
    c.add("ssm_b", 32)
    c.add("dt_bias", 1)
    c.add("a_log", 1)
    c.add("d_skip", 16)
    c.add("gate_norm", 16)
    return c


def constant_columns():
    c = Columns()
    for name, w in (("ident", P), ("mean", P), ("head_mean", P), ("rope_swap", P), ("cos", S), ("sin", S),
                    ("tri", P), ("cmp_mask", 12 * 16), ("pool_inv", 2 * S), ("gla_causal", P),
                    ("gla_reset", 2 * S), ("dist0", P), ("dist1", 2 * P), ("dist2", T), ("slope_last", 2),
                    ("ssd_reset", T), ("ssd_causal", P), ("eps", 2)):
        c.add(name, w)
    return c


PAR = parameter_columns()
CON = constant_columns()
SLOPES = [2.0 ** (-8.0 * (h + 1) / (2 * SWA_J)) for h in range(2 * SWA_J)]


def constants():
    c = np.zeros((P, CON.n), np.float32)

    def put(name, a):
        a = np.asarray(a, np.float32).reshape(a.shape[0], -1)
        c[:a.shape[0], CON[name]:CON[name] + a.shape[1]] = a

    put("ident", np.eye(P))
    put("mean", np.full((P, P), 1.0 / D))
    put("head_mean", np.kron(np.eye(2), np.full((HD, HD), 1.0 / GLA_DV)))
    half = HD // 8
    swap = np.zeros((P, P))
    for g in range(2):
        for i in range(half):
            swap[g * HD + half + i, g * HD + i] = 1.0
            swap[g * HD + i, g * HD + half + i] = 1.0
    put("rope_swap", swap)
    inv = np.float32(500000.0) ** (-np.arange(half, dtype=np.float32) * np.float32(2.0) / np.float32(2 * half))
    ang = np.arange(S, dtype=np.float32)[None, :] * inv.astype(np.float32)[:, None]
    cos, sin = np.ones((P, S), np.float32), np.zeros((P, S), np.float32)
    for g in range(2):
        b = g * HD
        cos[b:b + half] = cos[b + half:b + 2 * half] = np.cos(ang)
        sin[b:b + half] = -np.sin(ang)
        sin[b + half:b + 2 * half] = np.sin(ang)
    put("cos", cos)
    put("sin", sin)
    r = np.arange(P)
    put("tri", np.where(r[None, :] <= r[:, None], 0.0, MASKED))
    cm = np.full((P, 2, 2, 3, 16), MASKED)
    last = CMP_STRIDE * np.arange(CMP_N) + CMP_BLOCK - 1
    for ch in range(2):
        cm[:, :, ch, :, :CMP_N] = np.where(last[None, :] <= (ch * P + r)[:, None], 0.0, MASKED)[:, None, None, :]
    put("cmp_mask", cm)
    win = np.array([[2, 4], [8, 16]])
    t = np.arange(S)
    pi = np.zeros((P, 2, S))
    for i in range(2):
        for h in range(2):
            pi[h * HD:(h + 1) * HD, i] = 1.0 / np.minimum(t + 1, win[i, h]).astype(np.float32)
    put("pool_inv", pi)
    same = (r[:, None] // GLA_C) == (r[None, :] // GLA_C)
    put("gla_causal", np.where(same & (r[None, :] >= r[:, None]), 1.0, 0.0))
    put("gla_reset", np.tile(np.where(np.arange(2 * S) % GLA_C == 0, 0.0, 1.0), (P, 1)))
    far = 1.0e32

    def dist(tq, key):
        d = tq[:, None] - key[None, :]
        meta = key[None, :] < META
        ok = (d >= 0) & (meta | (d < SWA_WINDOW))
        return np.where(ok, np.where(meta, np.minimum(d, SWA_WINDOW), d), far)

    put("dist0", dist(r, r))
    put("dist1", dist(P + r, np.arange(2 * P)))
    put("dist2", dist(2 * P + np.tile(np.arange(META), SWA_J), np.arange(T)))
    put("slope_last", np.stack([-np.repeat([SLOPES[g * SWA_J + j] for j in range(SWA_J)], META) for g in range(2)], 1))
    reset = np.ones(T)
    reset[[t0 for t0, _ in CHUNKS]] = 0.0
    put("ssd_reset", np.tile(reset, (P, 1)))
    put("ssd_causal", np.where(r[None, :] >= r[:, None], 0.0, MASKED))
    put("eps", np.tile([LN_EPS, RMS_EPS], (P, 1)))
    return c


def two_stacks(nc, stream, params, consts, x_t, meta_t, out_t):
    slots, products, matrices, stream_width = plan_stream()

    freed = 0
    for s in slots:
        prod = products.get(s["name"])
        if prod and s["first_k"] + s["ks"] == prod["kt"]:
            s["release"] = ("tile", prod["first"] + s["tiles"][-1] + 1)
        else:
            freed += 1
            s["release"] = ("free", freed)

    with ExitStack() as ctx:
        def sb(name, cols):
            return ctx.enter_context(nc.sbuf_tensor(name, [P, cols], F32))[:, :]

        def sem(name):
            return ctx.enter_context(nc.semaphore(name))

        ring = sb("ring", RING * SLOT)
        par = sb("par", PAR.n)
        con = sb("con", CON.n)
        h_all = sb("h", KT * T).rearrange("p (k t) -> p k t", t=T)
        u_all = sb("u", KT * T).rearrange("p (k t) -> p k t", t=T)
        m_all = sb("m", KT * T).rearrange("p (k t) -> p k t", t=T)
        sq_all = sb("sq", KT * T).rearrange("p (k t) -> p k t", t=T)
        rstd = sb("rstd", T)
        lnv = sb("lnv", T)
        ARENA = 23100
        arena = sb("arena", ARENA)
        psum = ctx.enter_context(nc.psum_tensor("psum", [P, 8, 512], F32))

        def bank(b, lo=0, hi=512, rows=slice(0, P)):
            return psum[rows, b, lo:hi]

        def shaped(ap, *dims):
            if len(dims) == 1:
                return ap
            names = "abc"[:len(dims)]
            return ap.rearrange(f"p ({' '.join(names)}) -> p {' '.join(names)}", **dict(zip(names, dims)))

        def carve(sizes):
            at, out = 0, []
            for dims in sizes:
                n = int(np.prod(dims))
                out.append(shaped(arena[:, at:at + n], *dims))
                at += n
            assert at <= ARENA, at
            return out

        def C(name, lo, hi, rows=slice(0, P)):
            return con[rows, CON[name] + lo:CON[name] + hi]

        def pcol(name, i, rows=slice(0, P)):
            return par[rows, PAR[name] + i:PAR[name] + i + 1]

        ident = C("ident", 0, P)
        h1 = h_all[:, :, META:T]
        eps_ln, eps_rms = C("eps", 0, 1), C("eps", 1, 2)

        def over(ap, n):
            return ap.unsqueeze(1).to_broadcast([ap.shape[0], n] + list(ap.shape[1:]))

        def along(ap, n):
            return ap.unsqueeze(len(ap.shape)).to_broadcast(list(ap.shape) + [n])

        (p1, rope_cos, roped, tb, hid, kc, vc, v_tok, gv_tok, gates_t, sc, sc_s, e_at, pt_at, ptc, nm, gk_x, gk_l, bc,
         ep, en, qd, kinv, kend, kend_tok, gmix) = carve([
             (N_IN1, S), (6, S), (6, S), (2, 32, 15), (2, 16), (16,), (2, HD), (4, P), (6, P), (2, 18), (12, 16), (5, 12),
             (2, 2, S), (2, 512), (12, P), (2, 8), (2 * S,), (2 * S,), (2 * S,),
             (2 * S,), (2 * S,), (2 * S,), (2 * S,), (2 * S,), (4, P), (KT, S)])
        at_gla = shaped(sq_all.rearrange("p k t -> p (k t)")[:, 0:2048], 4, 4, P)
        u_flat = u_all.rearrange("p k t -> p (k t)")
        s_gla = shaped(u_flat[:, 0:384], 3, 2, HD)
        o_sq = shaped(u_flat[:, 384:384 + 768], 3, S)
        o_rs = shaped(u_flat[:, 1152:1152 + 768], 3, S)
        m_flat = m_all.rearrange("p k t -> p (k t)")
        pool_u = shaped(m_flat[:, 0:544], 2, 272)
        pool_a = shaped(m_flat[:, 544:1088], 2, 272)
        pool_b = shaped(m_flat[:, 1088:1632], 2, 272)
        pool_d = shaped(m_flat[:, 1632:2144], 2, S)
        og_silu = roped[:, 0:3, :]
        (ff1,) = carve([(FT1, S)])
        (xr, gg, qt, kv_t, rg, ig, la, a_sc, th, gmix_a, v_swa) = carve(
            [(8, T), (8, T), (8, T), (3, T), (8, T), (8, T), (8, T), (8, T), (8, T), (8, T), (3, P)])
        gmix_b = rg
        s_at = [shaped(ig.rearrange("p k t -> p (k t)")[:, 0:1024], 4, S), shaped(ig.rearrange("p k t -> p (k t)")[:, 1024:2048], 4, S)]
        pt_sw = shaped(la.rearrange("p k t -> p (k t)")[:, 0:2048], 4, 512)
        sm = shaped(th.rearrange("p k t -> p (k t)")[:, 0:96], 2, 6, 8)
        ff2, cg, cu = carve([(FT2, T), (2, T), (2, T)])
        (xbc, z_t, b_tok, prev, seg, e2, cd, dtt, dts, y_rs, aneg) = carve(
            [(32, T), (SSM_TILES, T), (SSM_G, P), (2048,), (2, 4, P), (2, 4, P), (2, 4, P), (3, 3, 32), (6, T), (2, T), (2,)])
        xdt = m_flat[:, 0:2048]
        xw = sq_all.rearrange("p k t -> p (k t)")[:, 0:2048]

        def gla_out(buf, q):
            rows = slice(64 * (q % 2), 64 * (q % 2) + 64)
            if q < 2:
                return buf[rows, 0:3:2, :], shaped(bank(GLA_BANKS[q], rows=rows), 2, S)
            return buf[rows, 1, :], bank(GLA_BANKS[q], 0, S, rows)

        slot_full = [sem(f"slot_full{i}") for i in range(RING)]
        slot_free = sem("slot_free")
        tile_done = sem("tile_done")
        evacuated = [sem(f"evacuated{i}") for i in range(GB)]
        tables_in, x_in = sem("tables_in"), sem("x_in")
        out_stored = sem("out_stored")
        act_chain, dve_chain, pool_chain = sem("act_chain"), sem("dve_chain"), sem("pool_chain")
        sq_ready, sums_done, rstd_ready = sem("sq_ready"), sem("sums_done"), sem("rstd_ready")
        mean_done, centred, ln_scaled, h_ready = sem("mean_done"), sem("centred"), sem("ln_scaled"), sem("h_ready")
        u_ready, h2_ready = sem("u_ready"), sem("h2_ready")
        rope_done, cos_ready, roped_ready = sem("rope_done"), sem("cos_ready"), sem("roped_ready")
        tb_ready, hid_done, hid_ready, kcvc_done, kcvc_ready = sem("tb_ready"), sem("hid_done"), sem("hid_ready"), sem("kcvc_done"), sem("kcvc_ready")
        gate_sig, v_turned, gv_turned, gates_turned, toks_ready = sem("gate_sig"), sem("v_turned"), sem("gv_turned"), sem("gates_turned"), sem("toks_ready")
        cmp_scored, cmp_shifted, cmp_exped, cmp_ready, cmp_turned, ptc_ready = (
            sem("cmp_scored"), sem("cmp_shifted"), sem("cmp_exped"), sem("cmp_ready"), sem("cmp_turned"), sem("ptc_ready"))
        scores_done, scores_max, attn_exp, attn_p, p_turned, pt_ready, pv_done, mix_out = (
            sem("scores_done"), sem("scores_max"), sem("attn_exp"), sem("attn_p"), sem("p_turned"), sem("pt_ready"), sem("pv_done"), sem("mix_out"))
        gk_done, gk_biased, gk_logged, bcum_ready, decays_ready, gla_in, kend_ready = (
            sem("gk_done"), sem("gk_biased"), sem("gk_logged"), sem("bcum_ready"), sem("decays_ready"), sem("gla_in"), sem("kend_ready"))
        kend_turned, kend_tok_ready, a_done, a_masked, ds_done, s_ready, o_done, o_squared, o_sums, o_rstd, gla_mixed = (
            sem("kend_turned"), sem("kend_tok_ready"), sem("a_done"), sem("a_masked"), sem("ds_done"), sem("s_ready"),
            sem("o_done"), sem("o_squared"), sem("o_sums"), sem("o_rstd"), sem("gla_mixed"))
        pool_in, pooled, pool_done, pool_mixed = sem("pool_in"), sem("pooled"), sem("pool_done"), sem("pool_mixed")
        relu_ready, f_ready = sem("relu_ready"), sem("f_ready")
        conv_acc, conv_done, conv_act = sem("conv_acc"), sem("conv_done"), sem("conv_act")
        lru_softplus, ssd_end = sem("lru_softplus"), sem("ssd_end")
        lru_done, lru_gated, lru_log, lru_exp, lru_root, lru_a2, lru_out = (
            sem("lru_done"), sem("lru_gated"), sem("lru_log"), sem("lru_exp"), sem("lru_root"), sem("lru_a2"), sem("lru_out"))
        v2_turned, v2_ready = sem("v2_turned"), sem("v2_ready")
        sw_scored, sw_max, sw_exp, sw_p, sw_turned, sw_pt, sw_pv, sw_out = (
            sem("sw_scored"), sem("sw_max"), sem("sw_exp"), sem("sw_p"), sem("sw_turned"), sem("sw_pt"), sem("sw_pv"), sem("sw_out"))
        dt_logged, cs_ready, dt_w, dtt_done, dtt_ready = (
            sem("dt_logged"), sem("cs_ready"), sem("dt_w"), sem("dtt_done"), sem("dtt_ready"))
        x_turned, xdt_ready, b_turned, b_ready = sem("x_turned"), sem("xdt_ready"), sem("b_turned"), sem("b_ready")
        cs_spread, seg_ready, ssd_exp, mt_ready, cd_ready, y_done, y_out, prev_ready, zy_ready, zy_sq, zy_sums, zy_rstd, y_ready = (
            sem("cs_spread"), sem("seg_ready"), sem("ssd_exp"), sem("mt_ready"), sem("cd_ready"), sem("y_done"), sem("y_out"),
            sem("prev_ready"), sem("zy_ready"), sem("zy_sq"), sem("zy_sums"), sem("zy_rstd"), sem("y_ready"))
        block = ctx.enter_context(nc.Block())

        class Tell:

            def __init__(self, eng, chain):
                self.eng, self.chain, self.counts, self.last = eng, chain, {}, None

            def __call__(self, ins, sem=None, value=None):
                sem = self.chain if sem is None else sem
                ins.then_inc(sem, 1)
                self.counts[sem.name] = self.counts.get(sem.name, 0) + 1
                self.last = (sem, self.counts[sem.name] if value is None else value)

            def settle(self):
                self.eng.wait_ge(*self.last)

        def evac_value(g):
            return evacuated[g % GB], g // GB + 1

        @block.sync
        def _(sp):
            def load(i):
                s = slots[i]
                sp.dma_start(ring[:, (i % RING) * SLOT:(i % RING) * SLOT + s["width"]],
                             stream[:, s["at"]:s["at"] + s["width"]]).then_inc(slot_full[i % RING], 16)

            sp.dma_start(h1, x_t).then_inc(x_in, 16)
            load(0)
            sp.dma_start(con, consts).then_inc(tables_in, 16)
            sp.dma_start(par, params).then_inc(tables_in, 16)
            sp.dma_start(h_all[:, :, 0:META], meta_t).then_inc(x_in, 16)
            for i in range(1, len(slots)):
                if i >= RING:
                    kind, n = slots[i - RING]["release"]
                    sp.wait_ge(tile_done if kind == "tile" else slot_free, n)
                load(i)
            sp.wait_ge(h2_ready, 4)
            sp.dma_start(out_t, h1).then_inc(out_stored, 16)
            sp.wait_ge(out_stored, 16)

        @block.tensor
        def _(pe):
            def slot_at(i, lo, hi, rows=slice(0, P)):
                return ring[rows, (i % RING) * SLOT + lo:(i % RING) * SLOT + hi]

            def await_slot(i):
                pe.wait_ge(slot_full[i % RING], 16 * (i // RING + 1))

            def product(name, rhs, ready, n, after=None):
                prod = products[name]
                first, kt, widths = prod["first"], prod["kt"], prod["widths"]
                for i, pair, k0, ks in prod["steps"]:
                    await_slot(i)
                    cols = sum(widths[j] for j in pair)
                    off = 0
                    for j in pair:
                        g, w = first + j, widths[j]
                        if k0 == 0 and g >= GB:
                            pe.wait_ge(*evac_value(g - GB))
                        for k in range(k0, k0 + ks):
                            if j == 0:
                                ready(k)
                            at = (k - k0) * cols + off
                            mm = pe.matmul(bank(g % GB, 0, n, slice(0, w)), slot_at(i, at, at + w), rhs(k),
                                           start=(k == 0), stop=(k == kt - 1))
                        if k == kt - 1:
                            mm.then_inc(tile_done, 1)
                        elif j == pair[-1]:
                            mm.then_inc(slot_free, 1)
                        off += w
                        if after and k == kt - 1:
                            after(j)

            def sums(src, n, value, ones="mean"):
                pe.wait_ge(sq_ready, value)
                for k in range(KT):
                    mm = pe.matmul(bank(4, 0, n), C(ones, 0, P), src[:, k, 0:n], start=(k == 0), stop=(k == KT - 1))
                mm.then_inc(sums_done, 1)

            def layer_norm(name, m):
                first = products[name]["first"]
                for k in range(KT):
                    pe.wait_ge(*evac_value(first + k))
                    mm = pe.matmul(bank(5, 0, S), C("mean", 0, P), m_all[:, k, 0:S], start=(k == 0), stop=(k == KT - 1))
                mm.then_inc(mean_done, 1)
                sums(sq_all, S, m + 1)

            def first_layer(l):
                first = products[f"in1_{l}"]["first"]
                misc = matrices[f"misc_{l}"]

                def evac_wait(t):
                    pe.wait_ge(*evac_value(first + t))

                def hidden_ready(k):
                    if l == 0:
                        pe.wait_ge(x_in, 32)
                    else:
                        pe.wait_ge(h_ready, 8 * (2 * l - 1) + k + 1)

                def rope():
                    evac_wait(5)
                    pe.wait_ge(tables_in, 32)
                    for i in range(3):
                        pe.matmul(bank(4 + i), C("rope_swap", 0, P), p1[:, 2 * i:2 * i + 2, :], start=True,
                                  stop=True).then_inc(rope_done, 1)

                product(f"in1_{l}", lambda k: h1[:, k, :], hidden_ready, S, lambda j: rope() if j == 7 else None)

                await_slot(misc)
                evac_wait(T_LR)
                for i in range(2):
                    mm = pe.matmul(bank(7, i * S, i * S + S), slot_at(misc, P + P * i, 2 * P + P * i, slice(0, 16)),
                                   p1[0:16, T_LR, :], start=True, stop=True)
                mm.then_inc(gk_done, 1)
                evac_wait(N_IN1 - 1)
                evac_wait(N_IN1 - 2)
                evac_wait(N_IN1 - 3)
                evac_wait(N_IN1 - 4)
                for b in range(2):
                    for c in range(2):
                        n = 2 * b + c
                        mm = pe.transpose(bank(0, n * P, n * P + P), p1[:, T_VS + b, c * P:c * P + P], ident)
                mm.then_inc(v_turned, 1)
                for i in range(3):
                    for c in range(2):
                        n = 2 * i + c
                        mm = pe.transpose(bank(1 + n // 4, (n % 4) * P, (n % 4) * P + P), p1[:, T_GV + i, c * P:c * P + P], ident)
                mm.then_inc(gv_turned, 1)
                pe.wait_ge(gate_sig, l + 1)
                for c in range(2):
                    mm = pe.transpose(bank(3, c * 18, c * 18 + 18), p1[32:50, T_LR, c * P:c * P + P], C("ident", 32, 50, slice(32, 50)))
                mm.then_inc(gates_turned, 1)

                pe.wait_ge(roped_ready, 3 * l + 3)
                for which in range(2):
                    w1 = matrices[f"cmp_{l}_{which}"]
                    await_slot(w1)
                    pe.wait_ge(tb_ready, 2 * l + which + 1)
                    for j in range(CMP_BLOCK):
                        for g in range(2):
                            r = slice(g * HD, g * HD + HD)
                            mm = pe.matmul(bank(4 + g, 16 * which, 16 * which + CMP_N, r), slot_at(w1, j * HD, j * HD + HD, r),
                                           tb[r, which, j, :], start=(j == 0), stop=(j == CMP_BLOCK - 1))
                    mm.then_inc(slot_free, 1)
                pe.matmul(bank(6, 0, 1), ident, C("eps", 0, 1), start=True, stop=True).then_inc(hid_done, 1)
                pe.wait_ge(hid_ready, l + 1)
                pe.wait_ge(gk_biased, l + 1)
                for g in range(2):
                    r = slice(g * HD, g * HD + HD)
                    pe.matmul(bank(6 + g, 0, CMP_N, r), slot_at(misc, 0, HD, r), hid[r, 0, 0:CMP_N], start=True, stop=True)
                    mm = pe.matmul(bank(6 + g, 64, 64 + HD, slice(0, CMP_N)), hid[r, 1, 0:CMP_N], slot_at(misc, HD, 2 * HD, r),
                                   start=True, stop=True)
                mm.then_inc(kcvc_done, 1)

                pe.wait_ge(kcvc_ready, l + 1)
                for g in range(2):
                    r = slice(g * HD, g * HD + HD)
                    for c in range(2):
                        for j in range(NSA_J):
                            at = (c * NSA_J + j) * 16
                            mm = pe.matmul(bank(4 + g, at, at + CMP_N), roped[r, T_Q + j, c * P:c * P + P], kc[r, 0:CMP_N],
                                           start=True, stop=True)
                mm.then_inc(cmp_scored, 1)
                pe.wait_ge(cmp_ready, l + 1)
                pe.wait_ge(toks_ready, l + 1)
                for n in range(12):
                    mm = pe.transpose(bank(n // 4, (n % 4) * P, (n % 4) * P + P, slice(0, CMP_N)), sc[:, n, 0:CMP_N], ident)
                mm.then_inc(cmp_turned, 1)

                units = [(c, j, g) for c in range(2) for j in range(NSA_J) for g in range(2)]
                base = 12 * l

                def scores(u):
                    c, j, g = units[u]
                    r, nk = slice(g * HD, g * HD + HD), (c + 1) * P
                    if u >= 2:
                        pe.wait_ge(attn_exp, base + u - 1)
                    for b in range(2):
                        mm = pe.matmul(bank(6 + u % 2, b * nk, b * nk + nk), roped[r, T_Q + j, c * P:c * P + P],
                                       roped[r, T_KS + b, 0:nk], start=True, stop=True)
                    mm.then_inc(scores_done, 1)

                def turn(u):
                    c, j, g = units[u]
                    pe.wait_ge(attn_p, base + u + 1)
                    if u >= 2:
                        pe.wait_ge(pt_ready, base + u - 1)
                    else:
                        pe.wait_ge(ptc_ready, l + 1)
                    for b in range(2):
                        for k in range(c + 1):
                            n = b * (c + 1) + k
                            mm = pe.transpose(bank(u % 2, n * P, n * P + P), e_at[:, u % 2, b, k * P:k * P + P], ident)
                    mm.then_inc(p_turned, 1)

                def values(u):
                    c, j, g = units[u]
                    r = slice(g * HD, g * HD + HD)
                    pe.wait_ge(pt_ready, base + u + 1)
                    if u >= 2:
                        pe.wait_ge(mix_out, base + u - 1)
                    out = bank(2 + u % 2, 0, P, r)
                    pe.matmul(out, vc[0:CMP_N, g, :], ptc[0:CMP_N, (g * 2 + c) * NSA_J + j, :], start=True, stop=False)
                    for b in range(2):
                        for k in range(c + 1):
                            n = b * (c + 1) + k
                            last = b == 1 and k == c
                            mm = pe.matmul(out, v_tok[:, 2 * b + k, g * HD:g * HD + HD], pt_at[:, u % 2, n * P:n * P + P],
                                           start=False, stop=last)
                    mm.then_inc(pv_done, 1)

                for u in range(14):
                    if u < 12:
                        scores(u)
                    if 1 <= u < 13:
                        turn(u - 1)
                    if u >= 2:
                        values(u - 2)

                pe.wait_ge(kend_ready, l + 1)
                pe.wait_ge(cmp_shifted, l + 1)
                for i in range(2):
                    for c in range(2):
                        n = 2 * i + c
                        mm = pe.transpose(bank(4, n * P, n * P + P), shaped(kend, 2, S)[:, i, c * P:c * P + P], ident)
                mm.then_inc(kend_turned, 1)
                pe.wait_ge(gla_in, l + 1)
                pe.wait_ge(mix_out, base + 12)
                for h in range(GLA_H):
                    r, i = slice(32 * (h % 4), 32 * (h % 4) + 32), h // 4
                    for c in range(2):
                        n = 2 * i + c
                        mm = pe.matmul(bank(h % 4, n * P, n * P + P), shaped(kinv, 2, S)[r, i, c * P:c * P + P],
                                       shaped(qd, 2, S)[r, i, c * P:c * P + P], start=True, stop=True)
                mm.then_inc(a_done, 1)
                pe.wait_ge(kend_tok_ready, l + 1)
                pe.wait_ge(attn_exp, base + 12)
                for n in range(3):
                    t = slice(64 * (n % 2), 64 * (n % 2) + 64)
                    for h in range(GLA_H):
                        i = h // 4
                        r = slice(32 * (h % 4), 32 * (h % 4) + 32)
                        at = (n // 2) * P + i * HD
                        mm = pe.matmul(bank(5 + n % 2, at, at + HD, r), kend_tok[t, 2 * i + n // 2, r],
                                       gv_tok[t, 2 * (h // 2) + n // 2, 64 * (h % 2):64 * (h % 2) + 64], start=True, stop=True)
                mm.then_inc(ds_done, 1)
                pe.wait_ge(a_masked, l + 1)
                pe.wait_ge(s_ready, l + 1)
                for h in range(GLA_H):
                    r, i, m = slice(32 * (h % 4), 32 * (h % 4) + 32), h // 4, h // 2
                    o = slice(64 * (h % 2), 64 * (h % 2) + 64)
                    b, at = GLA_BANKS[h % 4], i * S
                    for c in range(2):
                        pe.matmul(bank(b, at + c * P, at + c * P + P, o), gv_tok[:, 2 * m + c, o],
                                  at_gla[:, h % 4, 2 * i + c, :], start=True, stop=False)
                        for n in range(max(1, 2 * c), 2 * c + 2):
                            mm = pe.matmul(bank(b, at + n * 64, at + n * 64 + 64, o), s_gla[r, n - 1, i, :],
                                           shaped(qd, 2, S)[r, i, n * 64:n * 64 + 64], start=False, stop=(n == 2 * c + 1))
                mm.then_inc(o_done, 1)
                pe.wait_ge(pooled, l + 1)
                for g in range(4):
                    r = slice(64 * (g % 2), 64 * (g % 2) + 64)
                    mm = pe.matmul(bank(g % 2, (g // 2) * S, (g // 2) * S + S, r),
                                   slot_at(misc, 384 + (g // 2) * HD, 384 + (g // 2) * HD + HD, r), pool_d[r, g // 2, :],
                                   start=True, stop=True)
                mm.then_inc(pool_done, 1)
                pe.wait_ge(o_squared, l + 1)
                pe.matmul(bank(5, 0, 1), ident, C("eps", 0, 1), start=True, stop=True).then_inc(slot_free, 1)
                pe.matmul(bank(5), C("head_mean", 0, P), o_sq[:, 0:2, :], start=True, stop=True)
                pe.matmul(bank(6, 0, S), C("head_mean", 0, P), o_sq[:, 2, :], start=True, stop=True).then_inc(o_sums, 1)

                def mixed_ready(k):
                    if k < 3:
                        pe.wait_ge(pool_mixed, 4 * l + 4)
                        pe.wait_ge(gla_mixed, 3 * l + 1)
                        pe.wait_ge(mix_out, base + 12)
                    elif k < 6:
                        pe.wait_ge(gla_mixed, 3 * l + k - 2)
                    else:
                        pe.wait_ge(pool_mixed, 4 * l + 4)

                product(f"out1_{l}", lambda k: gmix[:, k, :], mixed_ready, S)
                layer_norm(f"out1_{l}", 2 * l)
                product(f"up1_{l}", lambda k: h1[:, k, :], lambda k: pe.wait_ge(h_ready, 8 * 2 * l + k + 1), S)
                product(f"down1_{l}", lambda k: ff1[:, k, :], lambda k: pe.wait_ge(f_ready, FT1 * l + k + 1), S)
                layer_norm(f"down1_{l}", 2 * l + 1)

            def norm2(n):
                sums(sq_all, T, 4 + n + 1)

            def normed_ready(p):
                return lambda k: pe.wait_ge(u_ready, 8 * p + k + 1)

            def second_ffn(l):
                product(f"up2_{l}", lambda k: u_all[:, k, :], normed_ready(2 * l + 1), T)
                product(f"down2_{l}", lambda k: ff2[:, k, :], lambda k: pe.wait_ge(f_ready, 2 * FT1 + FT2 * l + k + 1), T)

            def griffin():
                product("in_g", lambda k: u_all[:, k, :], normed_ready(0), T)
                first = products["in_g"]["first"]
                w = matrices["lru"]
                await_slot(w)
                pe.wait_ge(conv_done, 1)
                for n in range(16):
                    if n >= 4:
                        pe.wait_ge(lru_gated, n - 3)
                    mm = pe.matmul(bank(4 + n % 4, 0, T), slot_at(w, n * P, n * P + P), xr[:, n % 8, :], start=True, stop=True)
                    mm.then_inc(lru_done, 1)
                for t in range(GB):
                    pe.wait_ge(*evac_value(first + 25 - t))
                for c in range(3):
                    n = min(P, T - c * P)
                    mm = pe.transpose(bank(0, c * P, c * P + P, slice(0, n)), kv_t[:, 1, c * P:c * P + n], ident)
                mm.then_inc(v2_turned, 1)
                pe.matmul(bank(1, 0, 1), ident, C("eps", 0, 1), start=True, stop=True).then_inc(slot_free, 1)
                for b, (c, g, half) in enumerate(SWA_BATCHES):
                    r = slice(g * HD, g * HD + HD)
                    nk = SWA_KEYS[c]
                    if b >= 2:
                        pe.wait_ge(sw_max, b - 1)
                    else:
                        pe.wait_ge(lru_gated, 16)
                    s0 = 4 + 2 * (b % 2)
                    for j in range(4 if c < 2 else 1):
                        if c < 2:
                            lhs = qt[r, 4 * half + j, c * P:c * P + P]
                            per = 512 // nk
                            out = bank(s0 + j // per, (j % per) * nk, (j % per) * nk + nk)
                        else:
                            lhs = kv_t[r, 2, 0:P]
                            out = bank(s0, 0, nk)
                        mm = pe.matmul(out, lhs, kv_t[r, 0, 0:nk], start=True, stop=True)
                    mm.then_inc(sw_scored, 1)
                    if b >= 1:
                        swa_values(b - 1)
                swa_values(len(SWA_BATCHES) - 1)

                def mixed_ready(k):
                    pe.wait_ge(lru_out, 1)
                    pe.wait_ge(sw_out, len(SWA_BATCHES))

                product("out_g", lambda k: gmix_a[:, k, :] if k < 8 else gmix_b[:, k - 8, :], mixed_ready, T)

            def swa_values(b):
                c, g, half = SWA_BATCHES[b]
                nk = SWA_KEYS[c]
                chunks = [(k * P, min(P, nk - k * P)) for k in range((nk + P - 1) // P)]
                heads = 4 if c < 2 else 1
                pe.wait_ge(sw_p, b + 1)
                if b >= 1:
                    pe.wait_ge(sw_pt, b)
                else:
                    pe.wait_ge(v2_ready, 1)
                for k, (k0, kn) in enumerate(chunks):
                    for j in range(heads):
                        mm = pe.transpose(bank(1 + k, j * P, j * P + P, slice(0, kn)), s_at[b % 2][:, j, k0:k0 + kn] if c < 2
                                          else s_at[b % 2].rearrange("p a b -> p (a b)")[:, k0:k0 + kn], ident)
                mm.then_inc(sw_turned, 1)
                pe.wait_ge(sw_pt, b + 1)
                if b >= 1:
                    pe.wait_ge(sw_out, b)
                for k, (k0, kn) in enumerate(chunks):
                    mm = pe.matmul(bank(0, 0, heads * P, slice(g * HD, g * HD + HD)), v_swa[0:kn, k, g * HD:g * HD + HD],
                                   pt_sw[0:kn, k, 0:heads * P], start=(k == 0), stop=(k == len(chunks) - 1))
                mm.then_inc(sw_pv, 1)

            def mamba():
                product("in_m", lambda k: u_all[:, k, :], normed_ready(2), T)
                first = products["in_m"]["first"]
                for t in range(GB):
                    pe.wait_ge(*evac_value(first + 48 - t))
                pe.wait_ge(dt_w, 1)
                for ci, (t0, n) in enumerate(CHUNKS):
                    for v in range(3):
                        at = (3 * ci + v) * 32
                        mm = pe.transpose(bank(7, at, at + 32, slice(0, n)), dts[0:32, v, t0:t0 + n], C("ident", 0, 32, slice(0, 32)))
                mm.then_inc(dtt_done, 1)
                pe.wait_ge(conv_act, FT2 + 32)
                for ci, (t0, n) in enumerate(CHUNKS):
                    if ci == 0:
                        pe.wait_ge(dtt_ready, 1)
                    else:
                        pe.wait_ge(y_out, 8 * ci)
                    for i in range(4):
                        for t in range(4):
                            mm = pe.transpose(bank(4 + i, t * P, t * P + P, slice(0, n)), xbc[:, 4 * i + t, t0:t0 + n], ident)
                        mm.then_inc(x_turned, 1)
                    if ci < 2:
                        for g in range(SSM_G):
                            mm = pe.transpose(bank(g // 4, (g % 4) * P, (g % 4) * P + P, slice(0, n)), xbc[:, 16 + g, t0:t0 + n], ident)
                        mm.then_inc(b_turned, 1)
                        pe.wait_ge(b_ready, ci + 1)
                    pe.wait_ge(xdt_ready, ci + 1)

                    def spread(g):
                        q = 8 * ci + g
                        if g >= 2:
                            pe.wait_ge(mt_ready, q - 1)
                        pe.matmul(bank(q % 2, 0, n, slice(0, n)), xbc[:, 16 + g, t0:t0 + n], xbc[:, 24 + g, t0:t0 + n], start=True, stop=True)
                        for h in range(4):
                            mm = pe.matmul(bank(2 + q % 2, h * n, h * n + n), C("ident", 4 * g + h, 4 * g + h + 1, slice(0, 32)).to_broadcast([32, P]),
                                           dts[0:32, 1, t0:t0 + n], start=True, stop=True)
                        mm.then_inc(cs_spread, 1)

                    def outputs(g):
                        q = 8 * ci + g
                        pe.wait_ge(mt_ready, q + 1)
                        if ci:
                            pe.wait_ge(cd_ready, q - 8 + 1)
                        if g >= 2:
                            pe.wait_ge(y_out, q - 1)
                        for h in range(4):
                            o = slice(64 * (h % 2), 64 * (h % 2) + 64)
                            head = 4 * g + h
                            out = bank(4 + q % 2, (h // 2) * n, (h // 2) * n + n, o)
                            mm = pe.matmul(out, xdt[0:n, head * HD:head * HD + HD], seg[0:n, q % 2, h, 0:n], start=True, stop=(ci == 0))
                            if ci:
                                mm = pe.matmul(out, prev[:, head * HD:head * HD + HD], cd[:, q % 2, h, 0:n], start=False, stop=True)
                        if ci < 2:
                            mm = pe.matmul(bank(6 + q % 2, 0, 256), b_tok[0:n, g, :], xw[0:n, g * 256:g * 256 + 256], start=True, stop=True)
                        mm.then_inc(y_done, 1)

                    for g in range(9):
                        if g < 8:
                            spread(g)
                        if g:
                            outputs(g - 1)
                for g in range(SSM_G):
                    pe.wait_ge(zy_sq, g + 1)
                    if g >= 4:
                        pe.wait_ge(zy_rstd, g - 3)
                    for i in range(2):
                        mm = pe.matmul(bank(g % 4, 0, T), C("mean", 0, P), (u_all if g < 4 else m_all)[:, 2 * (g % 4) + i, :], start=(i == 0), stop=(i == 1))
                    mm.then_inc(zy_sums, 1)
                pe.wait_ge(zy_rstd, 8)
                product("out_m", lambda k: xbc[:, k, :], lambda k: pe.wait_ge(y_ready, k + 1), T)

            for l in range(DEPTH):
                first_layer(l)
            norm2(0)
            griffin()
            norm2(1)
            norm2(2)
            second_ffn(0)
            norm2(3)
            norm2(4)
            mamba()
            norm2(5)
            norm2(6)
            second_ffn(1)
            norm2(7)

        @block.scalar
        def _(act):
            tell = Tell(act, act_chain)

            def done(g):
                act.wait_ge(tile_done, g + 1)

            def evacuate(dst, g, n, func=ACT.Copy, rows=slice(0, P), **kw):
                done(g)
                tell(act.activation(dst, bank(g % GB, 0, n, rows), func, **kw), evacuated[g % GB], g // GB + 1)

            def inverse_root(dst, tmp, src, eps, scale=1.0):
                tell(act.activation(tmp, src, ACT.Ln, bias=eps, scale=scale))
                tell.settle()
                return act.activation(dst, tmp, ACT.Exp, scale=-0.5)

            def finish_norm(value, n, eps):
                act.wait_ge(sums_done, value)
                tell(inverse_root(rstd[:, 0:n], lnv[:, 0:n], bank(4, 0, n), eps), rstd_ready)

            def layer_norm(m, which, l):
                act.wait_ge(centred, m + 1)
                tell(act.activation(sq_all[:, :, 0:S], m_all[:, :, 0:S], ACT.Square), sq_ready)
                finish_norm(m + 1, S, eps_ln)
                for k in range(KT):
                    act.wait_ge(ln_scaled, 8 * m + k + 1)
                    tell(act.activation(h1[:, k, :], m_all[:, k, 0:S], ACT.Identity, bias=pcol(f"ln{which}_b{l}", k)), h_ready)

            def first_layer(l):
                first = products[f"in1_{l}"]["first"]
                widths = products[f"in1_{l}"]["widths"]
                for t in range(N_IN1):
                    rows = slice(0, widths[t])
                    if T_Q <= t < T_Q + NSA_J:
                        evacuate(p1[:, t, :], first + t, S, scale=float(HD) ** -0.5)
                    elif t >= T_PU:
                        if t == T_PU:
                            act.wait_ge(pool_in, l + 1)
                        evacuate(pool_u[:, t - T_PU, 16:272], first + t, S)
                    else:
                        evacuate(p1[rows, t, :], first + t, S, rows=rows)
                tell.settle()
                tell(act.activation(p1[32:50, T_LR, :], p1[32:50, T_LR, :], ACT.Sigmoid), gate_sig)
                act.wait_ge(gk_biased, l + 1)
                tell(act.activation(gk_l, gk_x, ACT.Abs))
                tell.settle()
                tell(act.activation(gk_l, gk_l, ACT.Exp, scale=-1.0))
                tell.settle()
                tell(act.activation(gk_l, gk_l, ACT.Ln, bias=1.0), gk_logged)
                act.wait_ge(v_turned, l + 1)
                act.activation(v_tok, shaped(bank(0), 4, P), ACT.Copy)
                act.wait_ge(gv_turned, l + 1)
                act.activation(gv_tok[:, 0:4, :], shaped(bank(1), 4, P), ACT.Copy)
                act.activation(gv_tok[:, 4:6, :], shaped(bank(2, 0, 256), 2, P), ACT.Copy)
                act.wait_ge(gates_turned, l + 1)
                tell(act.activation(gates_t, shaped(bank(3, 0, 36), 2, 18), ACT.Copy), toks_ready)
                act.wait_ge(bcum_ready, l + 1)
                act.activation(ep, bc, ACT.Exp, scale=1.0 / 16.0)
                act.activation(en, bc, ACT.Exp, scale=-1.0 / 16.0)
                tell(act.activation(gk_x, gk_l, ACT.Exp, scale=1.0 / 16.0), decays_ready)
                act.wait_ge(hid_done, l + 1)
                for g in range(2):
                    r = slice(g * HD, g * HD + HD)
                    ins = act.activation(hid[r, :, 0:CMP_N], shaped(bank(4 + g, 0, 32, r), 2, 16)[:, :, 0:CMP_N], ACT.Gelu_apprx_tanh)
                tell(ins, hid_ready)
                act.wait_ge(kcvc_done, l + 1)
                for g in range(2):
                    r = slice(g * HD, g * HD + HD)
                    act.activation(kc[r, 0:CMP_N], bank(6 + g, 0, CMP_N, r), ACT.Copy)
                    ins = act.activation(vc[0:CMP_N, g, :], bank(6 + g, 64, 64 + HD, slice(0, CMP_N)), ACT.Copy)
                tell(ins, kcvc_ready)
                act.wait_ge(cmp_shifted, l + 1)
                tell(act.activation(sc[:, :, 0:CMP_N], sc[:, :, 0:CMP_N], ACT.Exp), cmp_exped)

                base = 12 * l

                def exps(u):
                    nk = (u // 6 + 1) * P
                    act.wait_ge(scores_max, base + u + 1)
                    if u >= 2:
                        act.wait_ge(p_turned, base + u - 1)
                    for b in range(2):
                        ins = act.activation(e_at[:, u % 2, b, 0:nk], bank(6 + u % 2, b * nk, b * nk + nk), ACT.Exp,
                                             bias=nm[:, u % 2, b:b + 1], accum_out=nm[:, u % 2, 2 + b:3 + b])
                    tell(ins, attn_exp)

                def copy_pt(u):
                    n = 2 * (u // 6 + 1) * P
                    act.wait_ge(p_turned, base + u + 1)
                    if u >= 2:
                        act.wait_ge(pv_done, base + u - 1)
                    tell(act.activation(pt_at[:, u % 2, 0:n], bank(u % 2, 0, n), ACT.Copy), pt_ready)

                def copy_out(u):
                    c, j, g = u // 6, (u % 6) // 2, u % 2
                    r = slice(g * HD, g * HD + HD)
                    act.wait_ge(pv_done, base + u + 1)
                    tell(act.activation(gmix[r, j, c * P:c * P + P], bank(2 + u % 2, 0, P, r), ACT.Copy), mix_out)

                for u in range(14):
                    if u < 12:
                        exps(u)
                    if u == 0:
                        act.wait_ge(cmp_turned, l + 1)
                        for n in range(3):
                            ins = act.activation(ptc[0:CMP_N, 4 * n:4 * n + 4, :], shaped(bank(n, rows=slice(0, CMP_N)), 4, P), ACT.Copy)
                        tell(ins, ptc_ready)
                    if 1 <= u < 13:
                        copy_pt(u - 1)
                    if u >= 2:
                        copy_out(u - 2)

                act.wait_ge(kend_turned, l + 1)
                tell(act.activation(kend_tok, shaped(bank(4), 4, P), ACT.Copy), kend_tok_ready)
                tell(act.activation(og_silu, p1[:, T_OG:T_OG + 3, :], ACT.Silu))
                act.wait_ge(o_done, l + 1)
                for q in range(4):
                    dst, src = gla_out(o_sq, q)
                    ins = act.activation(dst, src, ACT.Square)
                tell(ins, o_squared)
                act.wait_ge(pool_done, l + 1)
                for g in range(4):
                    r = slice(64 * (g % 2), 64 * (g % 2) + 64)
                    tell(act.activation(gmix[r, 6 + g // 2, :], bank(g % 2, (g // 2) * S, (g // 2) * S + S, r), ACT.Identity,
                                        scale=pcol(f"pool_scale{l}", g // 2, r)), pool_mixed)
                act.wait_ge(o_sums, l + 1)
                act.activation(o_rs[:, 0:2, :], shaped(bank(5), 2, S), ACT.Ln, bias=eps_rms)
                tell(act.activation(o_rs[:, 2, :], bank(6, 0, S), ACT.Ln, bias=eps_rms))
                tell.settle()
                tell(act.activation(o_rs, o_rs, ACT.Exp, scale=-0.5), o_rstd)

                layer_norm(2 * l, 1, l)
                up = products[f"up1_{l}"]["first"]
                for i in range(FT1):
                    evacuate(ff1[:, i, :], up + i, S, ACT.Relu)
                layer_norm(2 * l + 1, 2, l)

            def square_norm(n, src, wait):
                wait()
                tell(act.activation(sq_all, src, ACT.Square), sq_ready)
                finish_norm(4 + n + 1, T, eps_rms)

            def out_product(name):
                for k in range(KT):
                    evacuate(m_all[:, k, :], products[name]["first"] + k, T)

            def second_ffn(l):
                up = products[f"up2_{l}"]["first"]
                for i in range(FT2 + 1):
                    if i < FT2:
                        for half, buf in ((0, cg), (1, cu)):
                            g = up + 2 * i + half
                            done(g)
                            if i >= 2:
                                act.wait_ge(f_ready, 2 * FT1 + FT2 * l + i - 1)
                            tell(act.activation(buf[:, i % 2, :], bank(g % GB, 0, T), ACT.Identity, scale=pcol(f"ffn_w{l}", 2 * 2 * FT2 + 2 * i + half),
                                                bias=pcol(f"ffn_b{l}", 2 * i + half)), conv_acc)
                    if i:
                        act.wait_ge(evacuated[(up + 2 * i - 2) % GB], (up + 2 * i - 2) // GB + 1)
                        tell(act.activation(cg[:, (i - 1) % 2, :], cg[:, (i - 1) % 2, :], ACT.Gelu_apprx_tanh), conv_act)
                out_product(f"down2_{l}")

            def griffin():
                first = products["in_g"]["first"]
                for i in range(8):
                    done(first + i)
                    tell(act.activation(xr[:, i, :], bank((first + i) % GB, 0, T), ACT.Identity, scale=pcol("lru_w", 24 + i), bias=pcol("lru_b", i)), conv_acc)
                for i in range(8):
                    evacuate(gg[:, i, :], first + 8 + i, T, ACT.Gelu_apprx_tanh)
                for i in range(8):
                    done(first + 16 + i)
                    act.activation(kv_t[:, 2, META * i:META * i + META], bank((first + 16 + i) % GB, 2 * P, T), ACT.Copy, scale=float(HD) ** -0.5)
                    evacuate(qt[:, i, :], first + 16 + i, T, scale=float(HD) ** -0.5)
                for i in range(2):
                    evacuate(kv_t[:, i, :], first + 24 + i, T)
                act.wait_ge(conv_done, 1)
                tell(act.activation(lnv[:, 16:24], lnv[:, 8:16], ACT.Abs))
                tell.settle()
                tell(act.activation(lnv[:, 16:24], lnv[:, 16:24], ACT.Exp, scale=-1.0))
                tell.settle()
                tell(act.activation(lnv[:, 16:24], lnv[:, 16:24], ACT.Ln, bias=1.0), lru_softplus)
                for n in range(16):
                    act.wait_ge(lru_done, n + 1)
                    dst = (rg if n < 8 else ig)[:, n % 8, :]
                    tell(act.activation(dst, bank(4 + n % 4, 0, T), ACT.Sigmoid, bias=pcol("lru_ba" if n < 8 else "lru_bx", n % 8)), lru_gated)
                act.wait_ge(lru_log, 1)
                act.activation(a_sc, la, ACT.Exp)
                act.activation(th, la, ACT.Tanh, scale=-1.0)
                tell(act.activation(sq_all, la, ACT.Exp, scale=2.0), lru_exp)
                act.wait_ge(v2_turned, 1)
                act.activation(v_swa[:, 0:2, :], shaped(bank(0, 0, 256), 2, P), ACT.Copy)
                tell(act.activation(v_swa[0:16, 2, :], bank(0, 256, 384, slice(0, 16)), ACT.Copy), v2_ready)
                act.wait_ge(lru_a2, 1)
                tell(act.activation(th, th, ACT.Sqrt), lru_root)
                for b, (c, g, half) in enumerate(SWA_BATCHES):
                    nk = SWA_KEYS[c]
                    heads = 4 if c < 2 else 1
                    act.wait_ge(sw_max, b + 1)
                    st = sm[:, b % 2]
                    for j in range(heads):
                        s = s_at[b % 2][:, j, 0:nk] if c < 2 else s_at[b % 2].rearrange("p a b -> p (a b)")[:, 0:nk]
                        act.activation(s, s, ACT.Exp, bias=st[:, 1, j:j + 1], accum_out=st[:, 2, j:j + 1])
                    tell(act.activation(st[:, 3, 0:heads], st[:, 3, 0:heads], ACT.Exp), sw_exp)
                    if b:
                        swa_copies(b - 1)
                swa_copies(len(SWA_BATCHES) - 1)
                out_product("out_g")

            def swa_copies(b):
                c, g, half = SWA_BATCHES[b]
                nk = SWA_KEYS[c]
                heads = 4 if c < 2 else 1
                act.wait_ge(sw_turned, b + 1)
                if b:
                    act.wait_ge(sw_pv, b)
                for k in range((nk + P - 1) // P):
                    rows = slice(0, min(P, nk - k * P))
                    ins = act.activation(pt_sw[rows, k, 0:heads * P], bank(1 + k, 0, heads * P, rows), ACT.Copy)
                tell(ins, sw_pt)
                act.wait_ge(sw_pv, b + 1)
                r = slice(g * HD, g * HD + HD)
                if c < 2:
                    ins = act.activation(gmix_b[r, 4 * half:4 * half + 4, c * P:c * P + P], shaped(bank(0, rows=r), 4, P), ACT.Copy)
                else:
                    ins = act.activation(gmix_b[r, :, 2 * P:T], shaped(bank(0, 0, P, r), 8, META), ACT.Copy)
                tell(ins, sw_out)

            def mamba():
                first = products["in_m"]["first"]
                act.wait_ge(*evac_value(first))
                ab = dts[0:32, 3, :]
                tell(act.activation(ab, dts[0:32, 0, :], ACT.Abs))
                tell.settle()
                tell(act.activation(ab, ab, ACT.Exp, scale=-1.0))
                tell(act.activation(aneg[0:32, 0:1], pcol("a_log", 0, slice(0, 32)), ACT.Exp))
                tell.settle()
                tell(act.activation(ab, ab, ACT.Ln, bias=1.0), dt_logged)
                for i in range(33):
                    if i == 8:
                        act.wait_ge(cs_ready, 1)
                        tell(act.activation(dts[0:32, 4, :], dts[0:32, 4, :], ACT.Exp, scale=-1.0), ssd_end)
                    if i < 32:
                        g = first + 1 + i
                        done(g)
                        tell(act.activation(xbc[:, i, :], bank(g % GB, 0, T), ACT.Identity, scale=pcol("ssm_w", 96 + i), bias=pcol("ssm_b", i)), conv_acc)
                    if i:
                        act.wait_ge(evacuated[(first + i) % GB], (first + i) // GB + 1)
                        tell(act.activation(xbc[:, i - 1, :], xbc[:, i - 1, :], ACT.Silu), conv_act)
                for i in range(SSM_TILES):
                    evacuate(z_t[:, i, :], first + 33 + i, T, ACT.Silu)
                act.wait_ge(dtt_done, 1)
                act.activation(dtt[0:META, 0], shaped(bank(7, 0, 96, slice(0, META)), 3, 32), ACT.Copy)
                tell(act.activation(dtt[:, 1:3], shaped(bank(7, 96, 288), 2, 3, 32), ACT.Copy), dtt_ready)
                for ci, (t0, n) in enumerate(CHUNKS):
                    if ci < 2:
                        act.wait_ge(b_turned, ci + 1)
                        for i in range(2):
                            ins = act.activation(b_tok[0:n, 4 * i:4 * i + 4, :], shaped(bank(i, rows=slice(0, n)), 4, P), ACT.Copy)
                        tell(ins, b_ready)
                    for g in range(SSM_G):
                        q = 8 * ci + g
                        if ci:
                            act.wait_ge(seg_ready, q + 1)
                            if q - 8 >= 2:
                                act.wait_ge(cd_ready, q - 8 - 1)
                                act.wait_ge(prev_ready, min(q - 1, 16))
                            act.activation(e2[:, q % 2], shaped(bank(2 + q % 2), 4, P), ACT.Exp)
                        act.wait_ge(seg_ready, q + 1)
                        s = seg[0:n, q % 2, :, 0:n]
                        tell(act.activation(s, s, ACT.Exp), ssd_exp)
                for g in range(SSM_G):
                    act.wait_ge(zy_ready, g + 1)
                    dst = (u_all if g < 4 else m_all)[:, 2 * (g % 4):2 * (g % 4) + 2, :]
                    tell(act.activation(dst, xbc[:, 2 * g:2 * g + 2, :], ACT.Square), zy_sq)
                for g in range(SSM_G):
                    act.wait_ge(zy_sums, g + 1)
                    if g >= 2:
                        act.wait_ge(y_ready, 2 * (g - 1))
                    tell(inverse_root(y_rs[:, g % 2, :], y_rs[:, g % 2, :], bank(g % 4, 0, T), eps_rms, scale=float(D) / 256.0), zy_rstd)
                out_product("out_m")

            act.wait_ge(tables_in, 32)
            act.wait_ge(x_in, 32)
            for l in range(DEPTH):
                first_layer(l)

            square_norm(0, h_all, lambda: tell.settle())
            griffin()
            square_norm(1, m_all, lambda: tell.settle())
            square_norm(2, h_all, lambda: act.wait_ge(h2_ready, 1))
            second_ffn(0)
            square_norm(3, m_all, lambda: tell.settle())
            square_norm(4, h_all, lambda: act.wait_ge(h2_ready, 2))
            mamba()
            square_norm(5, m_all, lambda: tell.settle())
            square_norm(6, h_all, lambda: act.wait_ge(h2_ready, 3))
            second_ffn(1)
            square_norm(7, m_all, lambda: tell.settle())

        @block.vector
        def _(dve):
            tell = Tell(dve, dve_chain)

            def residual(name):
                first = products[name]["first"]
                for k in range(KT):
                    g = first + k
                    dve.wait_ge(tile_done, g + 1)
                    tell(dve.scalar_tensor_tensor(m_all[:, k, 0:S], h1[:, k, :], ALPHA, bank(g % GB, 0, S), ALU.mult, ALU.add),
                         evacuated[g % GB], g // GB + 1)

            def layer_norm(m, which, l):
                dve.wait_ge(mean_done, m + 1)
                tell.settle()
                tell(dve.tensor_tensor(m_all[:, :, 0:S], m_all[:, :, 0:S], over(bank(5, 0, S), KT), ALU.subtract), centred)
                dve.wait_ge(rstd_ready, m + 1)
                tell.settle()
                for k in range(KT):
                    tell(dve.scalar_tensor_tensor(m_all[:, k, 0:S], m_all[:, k, 0:S], pcol(f"ln{which}_g{l}", k), rstd[:, 0:S],
                                                  ALU.mult, ALU.mult), ln_scaled)

            def first_layer(l):
                first = products[f"in1_{l}"]["first"]

                def evac_wait(t):
                    dve.wait_ge(*evac_value(first + t))

                dve.wait_ge(tables_in, 32)
                for i in range(3):
                    pair = roped[:, 2 * i:2 * i + 2, :]
                    dve.wait_ge(rope_done, 3 * l + i + 1)
                    tell(dve.tensor_tensor(pair, shaped(bank(4 + i), 2, S), over(C("sin", 0, S), 2), ALU.mult))
                    tell.settle()
                    dve.wait_ge(cos_ready, l + 1)
                    tell(dve.tensor_tensor(pair, pair, rope_cos[:, 2 * i:2 * i + 2, :], ALU.add), roped_ready)
                tell.settle()
                evac_wait(T_VC)
                for which, src in ((0, roped[:, T_KC, :]), (1, p1[:, T_VC, :])):
                    windows = bass.AP(src.tensor, src.offset, [list(src.ap[0]), [1, CMP_BLOCK], [CMP_STRIDE, CMP_N]])
                    pos = par[:, PAR[f"pos{l}"] + 32 * which:PAR[f"pos{l}"] + 32 * which + 32]
                    tell(dve.tensor_tensor(tb[:, which], windows, along(pos, CMP_N), ALU.add), tb_ready)
                dve.wait_ge(gk_done, l + 1)
                for i in range(2):
                    ins = dve.tensor_scalar(shaped(gk_x, 2, S)[:, i, :], bank(7, i * S, i * S + S), pcol(f"b_gate{l}", i), None, ALU.add)
                tell(ins, gk_biased)
                tell.settle()
                dve.wait_ge(gk_logged, l + 1)
                tell(dve.scalar_tensor_tensor(gk_l, gk_x, 0.0, gk_l, ALU.min, ALU.subtract))
                tell.settle()
                tell(dve.tensor_tensor_scan(bc, C("gla_reset", 0, 2 * S), gk_l, 0.0, ALU.mult, ALU.add))
                tell.settle()
                chunked = shaped(bc, 8, GLA_C)
                tell(dve.tensor_tensor(shaped(gk_l, 8, GLA_C), chunked[:, :, GLA_C - 1:GLA_C].to_broadcast([P, 8, GLA_C]), chunked, ALU.subtract), bcum_ready)
                dve.wait_ge(decays_ready, l + 1)
                p1q = p1[:, T_GQ:T_GQ + 2, :].rearrange("p a b -> p (a b)")
                p1k = p1[:, T_GK:T_GK + 2, :].rearrange("p a b -> p (a b)")
                dve.scalar_tensor_tensor(qd, p1q, float(np.float32(GLA_DK ** -0.5)), ep, ALU.mult, ALU.mult)
                tell(dve.tensor_tensor(kinv, p1k, en, ALU.mult), gla_in)
                tell(dve.tensor_tensor(kend, p1k, gk_x, ALU.mult), kend_ready)
                dve.wait_ge(cmp_scored, l + 1)
                s15 = sc[:, :, 0:CMP_N]
                mask = shaped(C("cmp_mask", 0, 192), 12, 16)
                for g in range(2):
                    ins = dve.tensor_tensor(sc[:, 6 * g:6 * g + 6, 0:CMP_N], shaped(bank(4 + g, 0, 96), 6, 16)[:, :, 0:CMP_N],
                                            mask[:, 6 * g:6 * g + 6, 0:CMP_N], ALU.add)
                tell(ins)
                tell.settle()
                tell(dve.tensor_reduce(sc_s[:, 0, :], s15, AX_X, ALU.max))
                tell.settle()
                tell(dve.tensor_scalar(sc_s[:, 1, :], sc_s[:, 0, :], MAX_FLOOR, None, ALU.max))
                tell.settle()
                tell(dve.tensor_tensor(s15, s15, along(sc_s[:, 1, :], CMP_N), ALU.subtract), cmp_shifted)
                dve.wait_ge(cmp_exped, l + 1)
                tell(dve.tensor_reduce(sc_s[:, 2, :], s15, AX_X, ALU.add))
                tell.settle()
                tell(dve.tensor_scalar(sc_s[:, 3, :], sc_s[:, 2, :], 1.0e-30, None, ALU.max))
                tell.settle()
                tell(dve.reciprocal(sc_s[:, 4, :], sc_s[:, 3, :]))
                tell.settle()
                dve.wait_ge(toks_ready, l + 1)
                gates = gates_t.rearrange("p c (g j b) -> p c g j b", g=2, j=3)
                for c in range(2):
                    r = sc_s[:, 4, :].rearrange("p (g c j) -> p g c j", g=2, c=2)[:, :, c, :]
                    ins = dve.tensor_tensor(sc_s[:, 0, :].rearrange("p (g c j) -> p g c j", g=2, c=2)[:, :, c, :], r, gates[:, c, :, :, 0], ALU.mult)
                tell(ins)
                tell.settle()
                tell(dve.tensor_tensor(s15, s15, along(sc_s[:, 0, :], CMP_N), ALU.mult), cmp_ready)

                base = 12 * l

                def maxima(u):
                    c = u // 6
                    nk = (c + 1) * P
                    b2 = shaped(bank(6 + u % 2, 0, 2 * nk), 2, nk)
                    dve.wait_ge(scores_done, base + u + 1)
                    if u >= 2:
                        dve.wait_ge(attn_exp, base + u - 1)
                    tell(dve.tensor_tensor(b2[:, :, c * P:nk], b2[:, :, c * P:nk], over(C("tri", 0, P), 2), ALU.add))
                    tell.settle()
                    tell(dve.tensor_reduce(nm[:, u % 2, 0:2], b2, AX_X, ALU.max, negate=True), scores_max)

                def weigh(u):
                    c, j, g = u // 6, (u % 6) // 2, u % 2
                    nk = (c + 1) * P
                    dve.wait_ge(attn_exp, base + u + 1)
                    tell(dve.reciprocal(nm[:, u % 2, 4:6], nm[:, u % 2, 2:4]))
                    tell.settle()
                    at = (g * 3 + j) * 3
                    tell(dve.tensor_tensor(nm[:, u % 2, 6:8], nm[:, u % 2, 4:6], gates_t[:, c, at + 1:at + 3], ALU.mult))
                    tell.settle()
                    for b in range(2):
                        e = e_at[:, u % 2, b, 0:nk]
                        ins = dve.tensor_scalar(e, e, nm[:, u % 2, 6 + b:7 + b], None, ALU.mult)
                    tell(ins, attn_p)

                for u in range(13):
                    if u < 12:
                        maxima(u)
                    if u:
                        weigh(u - 1)

                dve.wait_ge(a_done, l + 1)
                for b in range(4):
                    n = 4 if b < 2 else 2
                    ins = dve.tensor_tensor(at_gla[:, b, 0:n, :], shaped(bank(b, 0, n * P), n, P), over(C("gla_causal", 0, P), n), ALU.mult)
                tell(ins, a_masked)
                dve.wait_ge(ds_done, l + 1)
                epc = shaped(ep, 2, 4, GLA_C)
                for n in range(3):
                    for i in range(2):
                        rows = slice(0, P) if i == 0 else slice(0, HD)
                        ds = bank(5 + n % 2, (n // 2) * P + i * HD, (n // 2) * P + i * HD + HD, rows)
                        if n == 0:
                            ins = dve.tensor_copy(s_gla[rows, n, i, :], ds)
                        else:
                            ins = dve.scalar_tensor_tensor(s_gla[rows, n, i, :], s_gla[rows, n - 1, i, :], epc[rows, i, n, GLA_C - 1:GLA_C], ds,
                                                           ALU.mult, ALU.add)
                    tell(ins, s_ready if n == 2 else None)
                    tell.settle()
                dve.wait_ge(o_rstd, l + 1)
                for q in range(4):
                    dst, src = gla_out(o_rs, q)
                    ins = dve.tensor_tensor(dst, src, dst, ALU.mult)
                tell(ins)
                tell.settle()
                for i in range(3):
                    tell(dve.scalar_tensor_tensor(gmix[:, 3 + i, :], o_rs[:, i, :], pcol(f"norm_g{l}", i), og_silu[:, i, :], ALU.mult, ALU.mult), gla_mixed)

                residual(f"out1_{l}")
                layer_norm(2 * l, 1, l)
                up = products[f"up1_{l}"]["first"]
                for i in range(FT1):
                    dve.wait_ge(*evac_value(up + i))
                    tell(dve.tensor_tensor(ff1[:, i, :], ff1[:, i, :], ff1[:, i, :], ALU.mult), f_ready)
                residual(f"down1_{l}")
                layer_norm(2 * l + 1, 2, l)

            def pre_norm(n, name):
                dve.wait_ge(rstd_ready, 4 + n + 1)
                for k in range(KT):
                    tell(dve.scalar_tensor_tensor(u_all[:, k, :], h_all[:, k, :], pcol(name, k), rstd, ALU.mult, ALU.mult), u_ready)

            def post_norm(n, name):
                dve.wait_ge(rstd_ready, 4 + n + 1)
                for k in range(KT):
                    tell(dve.scalar_tensor_tensor(m_all[:, k, :], m_all[:, k, :], pcol(name, k), rstd, ALU.mult, ALU.mult))
                tell.settle()
                tell(dve.tensor_tensor(h_all, h_all, m_all, ALU.add), h2_ready)

            def taps(dst, g, count, acc_value, weight):
                dve.wait_ge(conv_acc, acc_value)
                for back in range(1, count):
                    ins = dve.scalar_tensor_tensor(dst[:, back:T], bank(g % GB, 0, T - back), weight(count - 1 - back), dst[:, back:T], ALU.mult, ALU.add)
                    if back < count - 1:
                        tell(ins)
                        tell.settle()
                tell(ins, evacuated[g % GB], g // GB + 1)

            def second_ffn(l):
                up = products[f"up2_{l}"]["first"]
                acc0 = (8, 8 + 2 * FT2 + 32)[l]
                act0 = (0, FT2 + 32)[l]
                for i in range(FT2 + 1):
                    if i < FT2:
                        for half, buf in ((0, cg), (1, cu)):
                            taps(buf[:, i % 2, :], up + 2 * i + half, 3, acc0 + 2 * i + half + 1, lambda tap: pcol(f"ffn_w{l}", tap * 2 * FT2 + 2 * i + half))
                    if i == FT2:
                        tell.settle()
                    if i:
                        dve.wait_ge(conv_act, act0 + i)
                        tell(dve.tensor_tensor(ff2[:, i - 1, :], cg[:, (i - 1) % 2, :], cu[:, (i - 1) % 2, :], ALU.mult), f_ready)

            def griffin():
                first = products["in_g"]["first"]
                for i in range(8):
                    taps(xr[:, i, :], first + i, 4, i + 1, lambda tap: pcol("lru_w", tap * 8 + i))
                tell.settle()
                tell(dve.tensor_scalar(lnv[:, 8:16], par[:, PAR["lru_lam"]:PAR["lru_lam"] + 8], -1.0, None, ALU.mult), conv_done)
                dve.wait_ge(lru_softplus, 1)
                tell.settle()
                tell(dve.scalar_tensor_tensor(lnv[:, 24:32], lnv[:, 8:16], 0.0, lnv[:, 16:24], ALU.max, ALU.add))
                tell.settle()
                tell(dve.tensor_scalar(lnv[:, 24:32], lnv[:, 24:32], -8.0, None, ALU.mult))
                tell.settle()
                dve.wait_ge(lru_gated, 8)
                tell(dve.tensor_tensor(la, rg, along(lnv[:, 24:32], T), ALU.mult), lru_log)
                dve.wait_ge(lru_gated, 16)
                tell(dve.tensor_tensor(ig, ig, xr, ALU.mult))
                dve.wait_ge(lru_exp, 1)
                tell(dve.scalar_tensor_tensor(th, sq_all, 1.0, th, ALU.add, ALU.mult), lru_a2)
                dve.wait_ge(lru_root, 1)
                tell.settle()
                dve.memset(a_sc[:, :, 0:1], 0.0)
                tell(dve.tensor_tensor(th, th, ig, ALU.mult))
                tell.settle()
                flat = lambda a: a.rearrange("p k t -> p (k t)")
                tell(dve.tensor_tensor_scan(flat(gmix_a), flat(a_sc), flat(th), 0.0, ALU.mult, ALU.add))
                tell.settle()
                tell(dve.tensor_tensor(gmix_a, gmix_a, gg, ALU.mult), lru_out)
                for b in range(len(SWA_BATCHES) + 1):
                    if b < len(SWA_BATCHES):
                        swa_scores(b)
                    if b:
                        swa_weigh(b - 1)

            def swa_scores(b):
                c, g, half = SWA_BATCHES[b]
                nk = SWA_KEYS[c]
                heads = 4 if c < 2 else 1
                st = sm[:, b % 2]
                s0 = 4 + 2 * (b % 2)
                dve.wait_ge(sw_scored, b + 1)
                if b >= 2:
                    dve.wait_ge(sw_turned, b - 1)
                per = 512 // nk
                flat = s_at[b % 2].rearrange("p a b -> p (a b)")
                for j in range(heads):
                    src = bank(s0 + j // per, (j % per) * nk, (j % per) * nk + nk)
                    slope = C("slope_last", g, g + 1) if c == 2 else -SLOPES[g * SWA_J + 4 * half + j]
                    dst = s_at[b % 2][:, j, 0:nk] if c < 2 else flat[:, 0:nk]
                    ins = dve.scalar_tensor_tensor(dst, C(f"dist{c}", 0, nk), slope, src, ALU.mult, ALU.add)
                tell(ins)
                tell.settle()
                if c < 2:
                    tell(dve.tensor_reduce(st[:, 0, 0:heads], s_at[b % 2][:, :, 0:nk], AX_X, ALU.max))
                    sink = par[:, PAR["sinks"] + g * SWA_J + 4 * half:PAR["sinks"] + g * SWA_J + 4 * half + 4]
                else:
                    tell(dve.tensor_reduce(st[:, 0, 0:1], flat[:, 0:nk], AX_X, ALU.max))
                    sink = pcol("sinks_last", g)
                tell.settle()
                tell(dve.tensor_tensor(st[:, 4, 0:heads], st[:, 0, 0:heads], sink, ALU.max))
                tell.settle()
                dve.tensor_scalar(st[:, 1, 0:heads], st[:, 4, 0:heads], -1.0, None, ALU.mult)
                tell(dve.tensor_tensor(st[:, 3, 0:heads], sink, st[:, 4, 0:heads], ALU.subtract), sw_max)

            def swa_weigh(b):
                c, g, half = SWA_BATCHES[b]
                nk = SWA_KEYS[c]
                heads = 4 if c < 2 else 1
                st = sm[:, b % 2]
                dve.wait_ge(sw_exp, b + 1)
                tell(dve.tensor_tensor(st[:, 5, 0:heads], st[:, 2, 0:heads], st[:, 3, 0:heads], ALU.add))
                tell.settle()
                tell(dve.reciprocal(st[:, 0, 0:heads], st[:, 5, 0:heads]))
                tell.settle()
                if c < 2:
                    s = s_at[b % 2][:, :, 0:nk]
                    tell(dve.tensor_tensor(s, s, along(st[:, 0, 0:heads], nk), ALU.mult), sw_p)
                else:
                    s = s_at[b % 2].rearrange("p a b -> p (a b)")[:, 0:nk]
                    tell(dve.tensor_scalar(s, s, st[:, 0, 0:1], None, ALU.mult), sw_p)

            def mamba():
                first = products["in_m"]["first"]
                r32 = slice(0, 32)
                dt, cs, w, ab, dl = (dts[r32, i, :] for i in range(5))
                dve.wait_ge(tile_done, first + 1)
                tell(dve.tensor_scalar(dt, bank(first % GB, 0, T, r32), pcol("dt_bias", 0, r32), None, ALU.add), evacuated[first % GB], first // GB + 1)
                dve.wait_ge(dt_logged, 1)
                tell(dve.scalar_tensor_tensor(dt, dt, 0.0, ab, ALU.max, ALU.add))
                tell.settle()
                tell(dve.tensor_scalar(dl, dt, aneg[r32, 0:1], -1.0, ALU.mult, ALU.mult))
                tell.settle()
                tell(dve.tensor_tensor_scan(cs, C("ssd_reset", 0, T, r32), dl, 0.0, ALU.mult, ALU.add))
                tell.settle()
                for t0, n in CHUNKS:
                    ins = dve.tensor_scalar(dts[r32, 4, t0:t0 + n], dts[r32, 1, t0:t0 + n], dts[r32, 1, t0 + n - 1:t0 + n], None, ALU.subtract)
                tell(ins, cs_ready)
                for i in range(32):
                    if i == 16:
                        dve.wait_ge(ssd_end, 1)
                        tell(dve.tensor_tensor(w, dt, dl, ALU.mult), dt_w)
                    taps(xbc[:, i, :], first + 1 + i, 4, 8 + 2 * FT2 + i + 1, lambda tap: pcol("ssm_w", tap * 32 + i))
                dve.wait_ge(dtt_ready, 1)
                for ci, (t0, n) in enumerate(CHUNKS):
                    rows = slice(0, n)
                    for i in range(4):
                        dve.wait_ge(x_turned, 4 * ci + i + 1)
                        src = shaped(bank(4 + i, rows=rows), 8, HD)
                        ins = dve.tensor_tensor(shaped(xdt[rows, 512 * i:512 * i + 512], 8, HD), src, along(dtt[rows, ci, 0, 8 * i:8 * i + 8], HD), ALU.mult)
                        if ci < 2:
                            ins = dve.tensor_tensor(shaped(xw[rows, 512 * i:512 * i + 512], 8, HD), src, along(dtt[rows, ci, 2, 8 * i:8 * i + 8], HD), ALU.mult)
                    tell(ins, xdt_ready)

                    def segments(g):
                        q = 8 * ci + g
                        dve.wait_ge(cs_spread, q + 1)
                        if g >= 2:
                            dve.wait_ge(y_done, q - 1)
                        for h in range(4):
                            ins = dve.scalar_tensor_tensor(seg[rows, q % 2, h, 0:n], bank(2 + q % 2, h * n, h * n + n, rows),
                                                           dtt[rows, ci, 1, 4 * g + h:4 * g + h + 1], C("ssd_causal", 0, n, rows), ALU.subtract, ALU.min)
                        tell(ins, seg_ready)

                    def scores(g):
                        q = 8 * ci + g
                        dve.wait_ge(ssd_exp, q + 1)
                        s = seg[rows, q % 2, :, 0:n]
                        tell(dve.tensor_tensor(s, s, over(bank(q % 2, 0, n, rows), 4), ALU.mult), mt_ready)

                    def outputs(g):
                        q = 8 * ci + g
                        dve.wait_ge(y_done, q + 1)
                        st = prev[:, 256 * g:256 * g + 256]
                        if ci == 0:
                            tell(dve.tensor_copy(st, bank(6 + q % 2, 0, 256)), prev_ready)
                        elif ci == 1:
                            tell(dve.tensor_tensor(shaped(st, 4, HD), shaped(st, 4, HD), e2[:, q % 2, :, P - 1:P].to_broadcast([P, 4, HD]), ALU.mult))
                            tell.settle()
                            tell(dve.tensor_tensor(st, st, bank(6 + q % 2, 0, 256), ALU.add), prev_ready)
                        for i in range(2):
                            t = xbc[:, 2 * g + i, t0:t0 + n]
                            ins = dve.scalar_tensor_tensor(t, t, pcol("d_skip", 2 * g + i), bank(4 + q % 2, i * n, i * n + n), ALU.mult, ALU.add)
                        tell(ins, y_out)

                    for g in range(10):
                        if g < 8:
                            segments(g)
                        if 1 <= g < 9:
                            scores(g - 1)
                        if g >= 2:
                            outputs(g - 2)
                tell.settle()
                for g in range(SSM_G):
                    t = xbc[:, 2 * g:2 * g + 2, :]
                    tell(dve.tensor_tensor(t, t, z_t[:, 2 * g:2 * g + 2, :], ALU.mult), zy_ready)
                tell.settle()
                for g in range(SSM_G):
                    dve.wait_ge(zy_rstd, g + 1)
                    dve.wait_ge(zy_sq, g + 1)
                    for i in range(2):
                        t = xbc[:, 2 * g + i, :]
                        tell(dve.scalar_tensor_tensor(t, t, pcol("gate_norm", 2 * g + i), y_rs[:, g % 2, :], ALU.mult, ALU.mult), y_ready)

            for l in range(DEPTH):
                first_layer(l)
            pre_norm(0, "mix_pre0")
            griffin()
            post_norm(1, "mix_post0")
            pre_norm(2, "ffn_pre0")
            second_ffn(0)
            post_norm(3, "ffn_post0")
            pre_norm(4, "mix_pre1")
            mamba()
            post_norm(5, "mix_post1")
            pre_norm(6, "ffn_pre1")
            second_ffn(1)
            post_norm(7, "ffn_post1")

        @block.gpsimd
        def _(pool):
            tell = Tell(pool, pool_chain)
            pool.wait_ge(tables_in, 32)
            for l in range(DEPTH):
                first = products[f"in1_{l}"]["first"]
                if l:
                    pool.wait_ge(h_ready, 16 * l)
                for buf in (pool_u, pool_a, pool_b):
                    ins = pool.memset(buf[:, :, 0:16], 0.0)
                tell(ins, pool_in)
                for t in range(3, 6):
                    pool.wait_ge(*evac_value(first + t))
                pool.wait_ge(*evac_value(first + 2))
                tell(pool.tensor_tensor(rope_cos, p1[:, 0:6, :], over(C("cos", 0, S), 6), ALU.mult), cos_ready)
                pool.wait_ge(*evac_value(first + T_PU + 1))
                pool.wait_ge(*evac_value(first + T_PU))
                live, shift = pool_u, 1
                inv = shaped(C("pool_inv", 0, 2 * S), 2, S)
                for step, dst in enumerate((pool_a, pool_b, pool_a, pool_b)):
                    tell(pool.tensor_tensor(dst[:, :, 16:272], live[:, :, 16:272], live[:, :, 16 - shift:272 - shift], ALU.add))
                    tell.settle()
                    r = slice(64 * (step % 2), 64 * (step % 2) + 64)
                    i = step // 2
                    tell(pool.tensor_tensor(pool_d[r, i, :], dst[r, i, 16:272], inv[r, i, :], ALU.mult))
                    tell.settle()
                    live, shift = dst, 2 * shift
                tell(pool.tensor_tensor(pool_d, pool_d, pool_u[:, :, 16:272], ALU.subtract), pooled)
            for ci, (t0, n) in enumerate(CHUNKS):
                if ci == 0:
                    continue
                for g in range(SSM_G):
                    q = 8 * ci + g
                    pool.wait_ge(ssd_exp, q + 1)
                    if g >= 2 or ci > 1:
                        pool.wait_ge(y_done, q - 1)
                    tell(pool.tensor_tensor(cd[:, q % 2], e2[:, q % 2], over(xbc[:, 24 + g, t0:t0 + n], 4), ALU.mult), cd_ready)


SWA_KEYS = [P, 2 * P, T]
SWA_BATCHES = [(c, g, half) for c in range(2) for g in range(2) for half in range(2)] + [(2, 0, 0), (2, 1, 0)]


def _columns_of(a, cols):
    out = np.zeros((a.shape[0], len(cols)), np.float32)
    at = [i for i, c in enumerate(cols) if c is not None]
    out[:, at] = a[:, [cols[i] for i in at]]
    return out


def _feature_major(v):
    v = v.reshape(-1, P)
    return v.transpose(1, 0)


def _twice(a):
    return np.concatenate([a, a], 0)


def lay_out_stream(x):
    slots, products, matrices, width = plan_stream()
    stream = np.zeros((P, width), np.float32)

    def put_product(name, w, tiles, rows=None):
        if rows is not None:
            w = w[rows]
        prod = products[name]
        for i, pair, k0, ks in prod["steps"]:
            cols = [c for j in pair for c in tiles[j]]
            part = _columns_of(w[k0 * P:(k0 + ks) * P], cols).reshape(ks, P, len(cols)).transpose(1, 0, 2)
            stream[:, slots[i]["at"]:slots[i]["at"] + slots[i]["width"]] = part.reshape(P, -1)

    def put_matrix(name, parts):
        at = slots[matrices[name]]["at"]
        for a in parts:
            a = a.reshape(a.shape[0], -1)
            stream[:a.shape[0], at:at + a.shape[1]] = a
            at += a.shape[1]

    for l in range(DEPTH):
        put_product(f"in1_{l}", x["w_in"][l], nsa_gla_pool_tiles())
        for which in range(2):
            w1 = x["cmp_w1"][l, which].reshape(CMP_BLOCK, HD, HD).transpose(1, 0, 2)
            put_matrix(f"cmp_{l}_{which}", [_twice(w1)])
        wg = np.zeros((P, 2 * P), np.float32)
        wg[:16, :GLA_H * GLA_DK] = x["gla_w_gate2"][l]
        pw = x["pool_w"][l].reshape(2, 2, HD, HD).transpose(1, 2, 0, 3).reshape(P, 2 * HD)
        put_matrix(f"misc_{l}", [_twice(x["cmp_w2"][l, 0]), _twice(x["cmp_w2"][l, 1]), wg, pw])
        put_product(f"out1_{l}", x["w_out"][l], straight_tiles(KT), nsa_mix_rows())
        put_product(f"up1_{l}", x["w_up"][l], straight_tiles(FT1))
        put_product(f"down1_{l}", x["w_down"][l], straight_tiles(KT))
    put_product("in_g", x["l0_w_in_2"], griffin_tiles())
    put_matrix("lru", [x["l0_lru_w_a_2"].transpose(1, 0, 2), x["l0_lru_w_x_2"].transpose(1, 0, 2)])
    put_product("out_g", x["l0_w_out_2"], straight_tiles(KT), griffin_mix_rows())
    put_product("in_m", x["l1_w_in_2"], mamba_tiles())
    put_product("out_m", x["l1_w_out_2"], straight_tiles(KT))
    for l in range(2):
        put_product(f"up2_{l}", x[f"l{l}_ffn_w_up_2"], ffn2_up_tiles())
        put_product(f"down2_{l}", x[f"l{l}_ffn_w_down_2"], straight_tiles(KT))
    return stream


def lay_out_parameters(x):
    par = np.zeros((P, PAR.n), np.float32)

    def put(name, a):
        a = a.reshape(a.shape[0], -1)
        par[:a.shape[0], PAR[name]:PAR[name] + a.shape[1]] = a

    for l in range(DEPTH):
        put(f"pos{l}", _twice(x["cmp_pos"][l].transpose(2, 0, 1)))
        bg = np.zeros(2 * P, np.float32)
        bg[:GLA_H * GLA_DK] = x["gla_b_gate"][l]
        put(f"b_gate{l}", _feature_major(bg))
        put(f"norm_g{l}", _feature_major(x["gla_norm_g"][l]))
        put(f"pool_scale{l}", _feature_major(x["pool_scale"][l]))
        for name in ("ln1_g", "ln1_b", "ln2_g", "ln2_b"):
            put(f"{name}{l}", _feature_major(x[name][l]))
    order = [c for t in ffn2_up_tiles() for c in t]
    for l in range(2):
        for name in ("mix_pre", "mix_post", "ffn_pre", "ffn_post"):
            put(f"{name}{l}", _feature_major(x[f"l{l}_{name}_norm_2"]))
        put(f"ffn_w{l}", _feature_major(x[f"l{l}_ffn_conv_w_2"][:, order]))
        put(f"ffn_b{l}", _feature_major(x[f"l{l}_ffn_conv_b_2"][order]))
    put("lru_w", _feature_major(x["l0_lru_conv_w_2"]))
    put("lru_b", _feature_major(x["l0_lru_conv_b_2"]))
    put("lru_ba", _feature_major(x["l0_lru_b_a_2"]))
    put("lru_bx", _feature_major(x["l0_lru_b_x_2"]))
    put("lru_lam", _feature_major(x["l0_lru_lambda_2"]))
    sinks = x["l0_attn_sinks_2"]
    put("sinks", np.broadcast_to(sinks[None, :], (P, 16)))
    put("sinks_last", np.repeat(sinks.reshape(2, SWA_J), META, axis=1).transpose(1, 0))
    put("ssm_w", _feature_major(x["l1_ssm_conv_w_2"]))
    put("ssm_b", _feature_major(x["l1_ssm_conv_b_2"]))
    put("dt_bias", x["l1_dt_bias_2"].reshape(-1, 1))
    put("a_log", x["l1_a_log_2"].reshape(-1, 1))
    put("d_skip", _feature_major(np.repeat(x["l1_d_skip_2"], HD)))
    put("gate_norm", _feature_major(x["l1_gate_norm_2"]))
    return par


def kernel(**inputs):
    import concourse.bacc as bacc
    from concourse.bass_utils import run_bass_kernel_spmd

    x = {name: np.asarray(a) for name, a in inputs.items()}
    feature_tiles = lambda a: np.ascontiguousarray(a.reshape(a.shape[0], KT, P).transpose(2, 1, 0))
    arrays = {
        "stream": lay_out_stream(x),
        "params": lay_out_parameters(x),
        "consts": constants(),
        "x_t": feature_tiles(x["x"][0]),
        "meta_t": feature_tiles(x["meta_tokens_2"]),
    }
    nc = bacc.Bacc("TRN2", target_bir_lowering=False, num_devices=1)
    args = [nc.dram_tensor(n, a.shape, F32, kind="ExternalInput").ap() for n, a in arrays.items()]
    args.append(nc.dram_tensor("out_t", (P, KT, S), F32, kind="ExternalOutput").ap())
    two_stacks(nc, *args)
    r = run_bass_kernel_spmd(nc, [arrays], core_ids=[0])
    out = np.asarray(r.results[0]["out_t"])
    return np.ascontiguousarray(out.transpose(2, 1, 0).reshape(1, S, D))
```

```python
from contextlib import ExitStack

import numpy as np
import concourse.bass as bass
from concourse import mybir

P = 128
F32 = mybir.dt.float32
F16 = mybir.dt.float16
ALU = mybir.AluOpType
ACT = mybir.ActivationFunctionType
AX_X = mybir.AxisListType.X

D = 1024
KT = D // P
S = 256
DEPTH = 2
META = 16
T = S + META
HD = 64
NSA_J = 3
CMP_N, CMP_BLOCK, CMP_STRIDE = 15, 32, 16
GLA_H, GLA_DK, GLA_DV, GLA_C = 6, 32, 64, 64
D_FF = 4096
FT1 = D_FF // P
D_FF2 = 2816
FT2 = D_FF2 // P
SWA_J = 8
SWA_WINDOW = 128
SSM_TILES = 16
SSM_G = 8
SSM_HEADS = 32
CHUNKS = [(0, META), (META, P), (META + P, P)]
ALPHA = float((2 * DEPTH) ** 0.25)
LN_EPS, RMS_EPS = 1e-5, 1e-6
MASKED = -1.0e30
MAX_FLOOR = -1.0e29
SLOT = 2048
MISC = 512
RAW = 4
SPLIT = 4
W_SCALE = 256.0
GLA_BANKS = [4, 7, 2, 3]
GB = 4


def nsa_gla_pool_tiles():
    q0, kv0, gate0 = 0, 384, 384 + 768
    gq0 = gate0 + 18
    gk0, gv0 = gq0 + 192, gq0 + 384
    glr0 = gv0 + 384
    og0 = glr0 + 16
    pu0 = og0 + 384
    kv = lambda branch, which: [kv0 + (branch * 2 + which) * 128 + i for i in range(128)]
    q = lambda j: [q0 + (g * NSA_J + j) * HD + i for g in range(2) for i in range(HD)]
    run = lambda a, n: list(range(a, a + n))
    tiles = [kv(0, 0), kv(1, 0), kv(2, 0), q(0), q(1), q(2), kv(0, 1), kv(1, 1), kv(2, 1)]
    tiles.append(run(glr0, 16) + [None] * 16 + run(gate0, 18))
    tiles += [run(gq0, 128), run(gq0 + 128, 64) + [None] * 64, run(gk0, 128), run(gk0 + 128, 64) + [None] * 64]
    tiles += [run(gv0 + 128 * i, 128) for i in range(3)]
    tiles += [run(og0 + 128 * i, 128) for i in range(3)]
    tiles += [run(pu0 + 128 * i, 128) for i in range(2)]
    return tiles


T_KC, T_KS, T_KW, T_Q, T_VC, T_VS, T_VW, T_LR, T_GQ, T_GK, T_GV, T_OG, T_PU = 0, 1, 2, 3, 6, 7, 8, 9, 10, 12, 14, 17, 20
N_IN1 = 22


def griffin_tiles():
    run = lambda a, n: list(range(a, a + n))
    gate0, xr0, q0, k0, v0 = 0, D, 2 * D, 3 * D, 3 * D + 128
    tiles = [run(xr0 + 128 * i, 128) for i in range(8)]
    tiles += [run(gate0 + 128 * i, 128) for i in range(8)]
    tiles += [[q0 + (g * SWA_J + j) * HD + i for g in range(2) for i in range(HD)] for j in range(SWA_J)]
    return tiles + [run(k0, 128), run(v0, 128)]


def mamba_tiles():
    run = lambda a, n: list(range(a, a + n))
    z0, x0, b0, c0, dt0 = 0, 2048, 4096, 5120, 6144
    tiles = [run(dt0, 32)]
    tiles += [run(x0 + 128 * i, 128) for i in range(16)]
    tiles += [run(b0 + 128 * i, 128) for i in range(8)]
    tiles += [run(c0 + 128 * i, 128) for i in range(8)]
    return tiles + [run(z0 + 128 * i, 128) for i in range(16)]


def straight_tiles(n):
    return [list(range(P * i, P * i + P)) for i in range(n)]


def ffn2_up_tiles():
    out = []
    for i in range(FT2):
        out += [list(range(P * i, P * i + P)), list(range(D_FF2 + P * i, D_FF2 + P * i + P))]
    return out


def nsa_mix_rows():
    rows = [(g * NSA_J + j) * HD + i for j in range(NSA_J) for g in range(2) for i in range(HD)]
    return rows + list(range(384, 1024))


def griffin_mix_rows():
    rows = list(range(D))
    return rows + [D + (g * SWA_J + j) * HD + i for j in range(SWA_J) for g in range(2) for i in range(HD)]


def stream_items():
    items = []
    for l in range(DEPTH):
        items.append(("product", f"in1_{l}", KT, [len(t) for t in nsa_gla_pool_tiles()]))
        items.append(("matrix", f"cmp_{l}_0", 2048))
        items.append(("matrix", f"cmp_{l}_1", 2048))
        items.append(("product", f"out1_{l}", KT, [P] * KT))
        items.append(("product", f"up1_{l}", KT, [P] * FT1))
        items.append(("product", f"down1_{l}", FT1, [P] * KT))
    items.append(("product", "in_g", KT, [P] * 26))
    items.append(("matrix", "lru", 2048))
    items.append(("product", "out_g", 16, [P] * KT))
    items.append(("product", "up2_0", KT, [P] * (2 * FT2)))
    items.append(("product", "down2_0", FT2, [P] * KT))
    items.append(("product", "in_m", KT, [len(t) for t in mamba_tiles()]))
    items.append(("product", "out_m", SSM_TILES, [P] * KT))
    items.append(("product", "up2_1", KT, [P] * (2 * FT2)))
    items.append(("product", "down2_1", FT2, [P] * KT))
    return items


def plan_stream():
    slots, products, matrices = [], {}, {}
    at, tile = 0, 0

    def slot(name, width, first_k=0, ks=0, tiles=()):
        nonlocal at
        slots.append(dict(name=name, at=at, width=width, first_k=first_k, ks=ks, tiles=tiles, release=None))
        at += width
        return len(slots) - 1

    for kind, name, *rest in stream_items():
        if kind == "matrix":
            matrices[name] = slot(name, rest[0])
            continue
        kt, widths = rest
        steps = []
        i = 0
        while i < len(widths):
            pair = [i]
            if i + 1 < len(widths):
                pair.append(i + 1)
            cols = sum(widths[j] for j in pair)
            for k0 in range(0, kt, 8):
                ks = min(8, kt - k0)
                steps.append((slot(name, ks * cols, k0, ks, tuple(pair)), pair, k0, ks))
            i += len(pair)
        products[name] = dict(first=tile, kt=kt, widths=widths, steps=steps)
        tile += len(widths)
    return slots, products, matrices, at


class Columns:

    def __init__(self):
        self.n, self.at = 0, {}

    def add(self, name, width):
        self.at[name] = self.n
        self.n += width

    def __getitem__(self, name):
        return self.at[name]


def parameter_columns():
    c = Columns()
    for l in range(DEPTH):
        for name, w in (("pos", 64), ("b_gate", 2), ("norm_g", 3), ("pool_scale", 2),
                        ("ln1_g", 8), ("ln1_b", 8), ("ln2_g", 8), ("ln2_b", 8)):
            c.add(f"{name}{l}", w)
    for l in range(2):
        for name in ("mix_pre", "mix_post", "ffn_pre", "ffn_post"):
            c.add(f"{name}{l}", 8)
        c.add(f"ffn_w{l}", 3 * 2 * FT2)
        c.add(f"ffn_b{l}", 2 * FT2)
    c.add("lru_w", 32)
    for name in ("lru_b", "lru_ba", "lru_bx", "lru_lam"):
        c.add(name, 8)
    c.add("sinks", 16)
    c.add("sinks_last", 2)
    c.add("ssm_w", 4 * 32)
    c.add("ssm_b", 32)
    c.add("dt_bias", 1)
    c.add("a_log", 1)
    c.add("d_skip", 16)
    c.add("gate_norm", 16)
    return c


def constant_columns():
    c = Columns()
    for name, w in (("ident", P), ("mean", P), ("head_mean", P), ("rope_swap", P), ("cos", S), ("sin", S),
                    ("tri", P), ("cmp_mask", 12 * 16), ("pool_inv", 2 * S), ("gla_causal", P),
                    ("gla_reset", 2 * S), ("dist0", P), ("dist1", 2 * P), ("dist2", T), ("slope_last", 2),
                    ("ssd_reset", T), ("ssd_causal", P), ("eps", 2)):
        c.add(name, w)
    return c


PAR = parameter_columns()
CON = constant_columns()
SLOPES = [2.0 ** (-8.0 * (h + 1) / (2 * SWA_J)) for h in range(2 * SWA_J)]


def constants():
    c = np.zeros((P, CON.n), np.float32)

    def put(name, a):
        a = np.asarray(a, np.float32).reshape(a.shape[0], -1)
        c[:a.shape[0], CON[name]:CON[name] + a.shape[1]] = a

    put("ident", np.eye(P))
    put("mean", np.full((P, P), 1.0 / D))
    put("head_mean", np.kron(np.eye(2), np.full((HD, HD), 1.0 / GLA_DV)))
    half = HD // 8
    swap = np.zeros((P, P))
    for g in range(2):
        for i in range(half):
            swap[g * HD + half + i, g * HD + i] = 1.0
            swap[g * HD + i, g * HD + half + i] = 1.0
    put("rope_swap", swap)
    inv = np.float32(500000.0) ** (-np.arange(half, dtype=np.float32) * np.float32(2.0) / np.float32(2 * half))
    ang = np.arange(S, dtype=np.float32)[None, :] * inv.astype(np.float32)[:, None]
    cos, sin = np.ones((P, S), np.float32), np.zeros((P, S), np.float32)
    for g in range(2):
        b = g * HD
        cos[b:b + half] = cos[b + half:b + 2 * half] = np.cos(ang)
        sin[b:b + half] = -np.sin(ang)
        sin[b + half:b + 2 * half] = np.sin(ang)
    put("cos", cos)
    put("sin", sin)
    r = np.arange(P)
    put("tri", np.where(r[None, :] <= r[:, None], 0.0, MASKED))
    cm = np.full((P, 2, 2, 3, 16), MASKED)
    last = CMP_STRIDE * np.arange(CMP_N) + CMP_BLOCK - 1
    for ch in range(2):
        cm[:, :, ch, :, :CMP_N] = np.where(last[None, :] <= (ch * P + r)[:, None], 0.0, MASKED)[:, None, None, :]
    put("cmp_mask", cm)
    win = np.array([[2, 4], [8, 16]])
    t = np.arange(S)
    pi = np.zeros((P, 2, S))
    for i in range(2):
        for h in range(2):
            pi[h * HD:(h + 1) * HD, i] = 1.0 / np.minimum(t + 1, win[i, h]).astype(np.float32)
    put("pool_inv", pi)
    same = (r[:, None] // GLA_C) == (r[None, :] // GLA_C)
    put("gla_causal", np.where(same & (r[None, :] >= r[:, None]), 1.0, 0.0))
    put("gla_reset", np.tile(np.where(np.arange(2 * S) % GLA_C == 0, 0.0, 1.0), (P, 1)))
    far = 1.0e32

    def dist(tq, key):
        d = tq[:, None] - key[None, :]
        meta = key[None, :] < META
        ok = (d >= 0) & (meta | (d < SWA_WINDOW))
        return np.where(ok, np.where(meta, np.minimum(d, SWA_WINDOW), d), far)

    put("dist0", dist(r, r))
    put("dist1", dist(P + r, np.arange(2 * P)))
    put("dist2", dist(2 * P + np.tile(np.arange(META), SWA_J), np.arange(T)))
    put("slope_last", np.stack([-np.repeat([SLOPES[g * SWA_J + j] for j in range(SWA_J)], META) for g in range(2)], 1))
    reset = np.ones(T)
    reset[[t0 for t0, _ in CHUNKS]] = 0.0
    put("ssd_reset", np.tile(reset, (P, 1)))
    put("ssd_causal", np.where(r[None, :] >= r[:, None], 0.0, MASKED))
    put("eps", np.tile([LN_EPS, RMS_EPS], (P, 1)))
    return c


def two_stacks(nc, stream, small, params, consts, x_t, meta_t, out_t):
    slots, products, matrices, stream_width = plan_stream()

    freed = 0
    for s in slots:
        prod = products.get(s["name"])
        if prod and s["first_k"] + s["ks"] == prod["kt"]:
            s["release"] = ("tile", prod["first"] + s["tiles"][-1] + 1)
        else:
            freed += 1
            s["release"] = ("free", freed)

    with ExitStack() as ctx:
        def sb(name, cols):
            return ctx.enter_context(nc.sbuf_tensor(name, [P, cols], F32))[:, :]

        def sem(name):
            return ctx.enter_context(nc.semaphore(name))

        raw = sb("raw", RAW * SLOT)
        high = ctx.enter_context(nc.sbuf_tensor("high", [P, SPLIT * SLOT], F16))[:, :]
        low = ctx.enter_context(nc.sbuf_tensor("low", [P, SPLIT * SLOT], F16))[:, :]
        misc = sb("misc", DEPTH * MISC)
        par = sb("par", PAR.n)
        con = sb("con", CON.n)
        h_all = sb("h", KT * T).rearrange("p (k t) -> p k t", t=T)
        u_all = sb("u", KT * T).rearrange("p (k t) -> p k t", t=T)
        m_all = sb("m", KT * T).rearrange("p (k t) -> p k t", t=T)
        sq_all = sb("sq", KT * T).rearrange("p (k t) -> p k t", t=T)
        rstd = sb("rstd", T)
        lnv = sb("lnv", T)
        ARENA = 21900
        arena = sb("arena", ARENA)
        psum = ctx.enter_context(nc.psum_tensor("psum", [P, 8, 512], F32))

        def bank(b, lo=0, hi=512, rows=slice(0, P)):
            return psum[rows, b, lo:hi]

        def shaped(ap, *dims):
            if len(dims) == 1:
                return ap
            names = "abc"[:len(dims)]
            return ap.rearrange(f"p ({' '.join(names)}) -> p {' '.join(names)}", **dict(zip(names, dims)))

        def carve(sizes):
            at, out = 0, []
            for dims in sizes:
                n = int(np.prod(dims))
                out.append(shaped(arena[:, at:at + n], *dims))
                at += n
            assert at <= ARENA, at
            return out

        def C(name, lo, hi, rows=slice(0, P)):
            return con[rows, CON[name] + lo:CON[name] + hi]

        def pcol(name, i, rows=slice(0, P)):
            return par[rows, PAR[name] + i:PAR[name] + i + 1]

        ident = C("ident", 0, P)
        h1 = h_all[:, :, META:T]
        eps_ln, eps_rms = C("eps", 0, 1), C("eps", 1, 2)

        def over(ap, n):
            return ap.unsqueeze(1).to_broadcast([ap.shape[0], n] + list(ap.shape[1:]))

        def along(ap, n):
            return ap.unsqueeze(len(ap.shape)).to_broadcast(list(ap.shape) + [n])

        (p1, rope_cos, roped, tb, hid, kc, vc, v_tok, gv_tok, gates_t, sc, sc_s, e_at, pt_at, ptc, nm, gk_x, gk_l, bc,
         ep, en, qd, kinv, kend, kend_tok, gmix) = carve([
             (N_IN1, S), (6, S), (6, S), (2, 32, 15), (2, 16), (16,), (2, HD), (4, P), (6, P), (2, 18), (12, 16), (5, 12),
             (2, 2, S), (2, 512), (12, P), (2, 8), (2 * S,), (2 * S,), (2 * S,),
             (2 * S,), (2 * S,), (2 * S,), (2 * S,), (2 * S,), (4, P), (KT, S)])
        def halves(region, *dims):
            n = int(np.prod(dims))
            flat16 = region.bitcast(F16)
            return shaped(flat16[:, 0:n], *dims), shaped(flat16[:, n:2 * n], *dims)

        at_gla = shaped(sq_all.rearrange("p k t -> p (k t)")[:, 0:2048], 4, 4, P)
        flat3 = lambda a: a.rearrange("p a b -> p (a b)")
        x_hi, x_lo = halves(flat3(u_all), KT, T)
        s_gla = shaped(flat3(rope_cos)[:, 0:384], 3, 2, HD)
        o_sq = shaped(flat3(rope_cos)[:, 384:384 + 768], 3, S)
        o_rs = p1[:, 0:3, :]
        tb_hi, tb_lo = halves(e_at.rearrange("p a b c -> p (a b c)")[:, 0:960], 2, 32, 15)
        m_flat = m_all.rearrange("p k t -> p (k t)")
        pool_u = shaped(m_flat[:, 0:544], 2, 272)
        pool_a = shaped(m_flat[:, 544:1088], 2, 272)
        pool_b = shaped(m_flat[:, 1088:1632], 2, 272)
        pool_d = shaped(m_flat[:, 1632:2144], 2, S)
        og_silu = roped[:, 0:3, :]
        ff1, f_relu, f_sq = carve([(FT1, S), (4, S), (2, S)])
        f1_hi, f1_lo = halves(flat3(ff1), FT1, S)
        (xr, gg, qt, kv_t, rg, ig, la, a_sc, th, gmix_a, v_swa) = carve(
            [(8, T), (8, T), (8, T), (3, T), (8, T), (8, T), (8, T), (8, T), (8, T), (8, T), (3, P)])
        xr_hi, xr_lo = halves(flat3(th), 8, T)
        ya_hi, ya_lo = halves(flat3(xr), 8, T)
        yb_hi, yb_lo = halves(flat3(gg), 8, T)
        gmix_b = rg
        s_at = [shaped(ig.rearrange("p k t -> p (k t)")[:, 0:1024], 4, S), shaped(ig.rearrange("p k t -> p (k t)")[:, 1024:2048], 4, S)]
        pt_sw = shaped(la.rearrange("p k t -> p (k t)")[:, 0:2048], 4, 512)
        sm = shaped(th.rearrange("p k t -> p (k t)")[:, 0:96], 2, 6, 8)
        ff2, cg, cu, f_prod = carve([(FT2, T), (2, T), (2, T), (2, T)])
        f2_hi, f2_lo = halves(flat3(ff2), FT2, T)
        (xbc, z_t, b_tok, prev, seg, e2, cd, dtt, dts, y_rs, aneg) = carve(
            [(32, T), (SSM_TILES, T), (SSM_G, P), (2048,), (2, 4, P), (2, 4, P), (2, 4, P), (3, 3, 32), (6, T), (2, T), (2,)])
        ym_hi, ym_lo = halves(flat3(z_t), SSM_TILES, T)
        xdt = m_flat[:, 0:2048]
        xw = sq_all.rearrange("p k t -> p (k t)")[:, 0:2048]

        def gla_out(buf, q):
            rows = slice(64 * (q % 2), 64 * (q % 2) + 64)
            if q < 2:
                return buf[rows, 0:3:2, :], shaped(bank(GLA_BANKS[q], rows=rows), 2, S)
            return buf[rows, 1, :], bank(GLA_BANKS[q], 0, S, rows)

        slot_full = [sem(f"slot_full{i}") for i in range(RAW)]
        high_ready, split_ready = sem("high_ready"), sem("split_ready")
        xh_ready, x_ready = sem("xh_ready"), sem("x_ready")
        fh_ready, params_scaled = sem("fh_ready"), sem("params_scaled")
        ya_high, y_split, xr_high, xr_split, tb_high, tb_split = sem("ya_high"), sem("y_split"), sem("xr_high"), sem("xr_split"), sem("tb_high"), sem("tb_split")
        ym_high, m_scaled, zy_normed = sem("ym_high"), sem("m_scaled"), sem("zy_normed")
        slot_free = sem("slot_free")
        tile_done = sem("tile_done")
        evacuated = [sem(f"evacuated{i}") for i in range(GB)]
        tables_in, x_in = sem("tables_in"), sem("x_in")
        out_stored = sem("out_stored")
        act_chain, dve_chain, pool_chain = sem("act_chain"), sem("dve_chain"), sem("pool_chain")
        sq_ready, sums_done, rstd_ready = sem("sq_ready"), sem("sums_done"), sem("rstd_ready")
        mean_done, centred, ln_scaled, h_ready = sem("mean_done"), sem("centred"), sem("ln_scaled"), sem("h_ready")
        u_ready, h2_ready = sem("u_ready"), sem("h2_ready")
        rope_done, cos_ready, roped_ready = sem("rope_done"), sem("cos_ready"), sem("roped_ready")
        tb_ready, hid_done, hid_ready, kcvc_done, kcvc_ready = sem("tb_ready"), sem("hid_done"), sem("hid_ready"), sem("kcvc_done"), sem("kcvc_ready")
        gate_sig, v_turned, gv_turned, gates_turned, toks_ready = sem("gate_sig"), sem("v_turned"), sem("gv_turned"), sem("gates_turned"), sem("toks_ready")
        cmp_scored, cmp_shifted, cmp_exped, cmp_ready, cmp_turned, ptc_ready = (
            sem("cmp_scored"), sem("cmp_shifted"), sem("cmp_exped"), sem("cmp_ready"), sem("cmp_turned"), sem("ptc_ready"))
        scores_done, scores_max, attn_exp, attn_p, p_turned, pt_ready, pv_done, mix_out = (
            sem("scores_done"), sem("scores_max"), sem("attn_exp"), sem("attn_p"), sem("p_turned"), sem("pt_ready"), sem("pv_done"), sem("mix_out"))
        gk_done, gk_biased, gk_logged, bcum_ready, decays_ready, gla_in, kend_ready = (
            sem("gk_done"), sem("gk_biased"), sem("gk_logged"), sem("bcum_ready"), sem("decays_ready"), sem("gla_in"), sem("kend_ready"))
        kend_turned, kend_tok_ready, a_done, a_masked, ds_done, s_ready, o_done, o_squared, o_sums, o_rstd, gla_mixed = (
            sem("kend_turned"), sem("kend_tok_ready"), sem("a_done"), sem("a_masked"), sem("ds_done"), sem("s_ready"),
            sem("o_done"), sem("o_squared"), sem("o_sums"), sem("o_rstd"), sem("gla_mixed"))
        pool_in, pooled, pool_done, pool_mixed = sem("pool_in"), sem("pooled"), sem("pool_done"), sem("pool_mixed")
        relu_ready, f_ready = sem("relu_ready"), sem("f_ready")
        conv_acc, conv_done, conv_act = sem("conv_acc"), sem("conv_done"), sem("conv_act")
        lru_softplus, ssd_end = sem("lru_softplus"), sem("ssd_end")
        lru_done, lru_gated, lru_log, lru_exp, lru_root, lru_a2, lru_out = (
            sem("lru_done"), sem("lru_gated"), sem("lru_log"), sem("lru_exp"), sem("lru_root"), sem("lru_a2"), sem("lru_out"))
        v2_turned, v2_ready = sem("v2_turned"), sem("v2_ready")
        sw_scored, sw_max, sw_exp, sw_p, sw_turned, sw_pt, sw_pv, sw_out = (
            sem("sw_scored"), sem("sw_max"), sem("sw_exp"), sem("sw_p"), sem("sw_turned"), sem("sw_pt"), sem("sw_pv"), sem("sw_out"))
        dt_logged, cs_ready, dt_w, dtt_done, dtt_ready = (
            sem("dt_logged"), sem("cs_ready"), sem("dt_w"), sem("dtt_done"), sem("dtt_ready"))
        x_turned, xdt_ready, b_turned, b_ready = sem("x_turned"), sem("xdt_ready"), sem("b_turned"), sem("b_ready")
        cs_spread, seg_ready, ssd_exp, mt_ready, cd_ready, y_done, y_out, prev_ready, zy_ready, zy_sq, zy_sums, zy_rstd, y_ready = (
            sem("cs_spread"), sem("seg_ready"), sem("ssd_exp"), sem("mt_ready"), sem("cd_ready"), sem("y_done"), sem("y_out"),
            sem("prev_ready"), sem("zy_ready"), sem("zy_sq"), sem("zy_sums"), sem("zy_rstd"), sem("y_ready"))
        block = ctx.enter_context(nc.Block())

        class Tell:

            def __init__(self, eng, chain):
                self.eng, self.chain, self.counts, self.last = eng, chain, {}, None

            def __call__(self, ins, sem=None, value=None):
                sem = self.chain if sem is None else sem
                ins.then_inc(sem, 1)
                self.counts[sem.name] = self.counts.get(sem.name, 0) + 1
                self.last = (sem, self.counts[sem.name] if value is None else value)

            def settle(self):
                self.eng.wait_ge(*self.last)

        def evac_value(g):
            return evacuated[g % GB], g // GB + 1

        def freed_by_pe(eng, i):
            if i >= 0:
                kind, n = slots[i]["release"]
                eng.wait_ge(tile_done if kind == "tile" else slot_free, n)

        def ready_steps(name):
            prod = products[name]
            for i, pair, k0, ks in prod["steps"]:
                yield i, pair if k0 + ks == prod["kt"] else []

        @block.sync
        def _(sp):
            def load(i):
                s = slots[i]
                sp.dma_start(raw[:, (i % RAW) * SLOT:(i % RAW) * SLOT + s["width"]],
                             stream[:, s["at"]:s["at"] + s["width"]]).then_inc(slot_full[i % RAW], 16)

            sp.dma_start(h1, x_t).then_inc(x_in, 16)
            load(0)
            sp.dma_start(con, consts).then_inc(tables_in, 16)
            sp.dma_start(par, params).then_inc(tables_in, 16)
            sp.dma_start(misc, small).then_inc(tables_in, 16)
            sp.dma_start(h_all[:, :, 0:META], meta_t).then_inc(x_in, 16)
            for i in range(1, len(slots)):
                if i >= RAW:
                    sp.wait_ge(split_ready, i - RAW + 1)
                load(i)
            sp.wait_ge(h2_ready, 4)
            sp.dma_start(out_t, h1).then_inc(out_stored, 16)
            sp.wait_ge(out_stored, 16)

        @block.tensor
        def _(pe):
            def await_slot(i):
                pe.wait_ge(split_ready, i + 1)

            def split_matmul(out, i, lo, hi, x, start, stop, rows=slice(0, P)):
                at = (i % SPLIT) * SLOT
                w_hi, w_lo = high[rows, at + lo:at + hi], low[rows, at + lo:at + hi]
                pe.matmul(out, w_hi, x[0], start=start, stop=False)
                pe.matmul(out, w_hi, x[1], start=False, stop=False)
                return pe.matmul(out, w_lo, x[0], start=False, stop=stop)

            def product(name, rhs, ready, n, after=None):
                prod = products[name]
                first, kt, widths = prod["first"], prod["kt"], prod["widths"]
                for i, pair, k0, ks in prod["steps"]:
                    await_slot(i)
                    cols = sum(widths[j] for j in pair)
                    off = 0
                    for j in pair:
                        g, w = first + j, widths[j]
                        if k0 == 0 and g >= GB:
                            pe.wait_ge(*evac_value(g - GB))
                        for k in range(k0, k0 + ks):
                            if j == 0:
                                ready(k)
                            at = (k - k0) * cols + off
                            mm = split_matmul(bank(g % GB, 0, n, slice(0, w)), i, at, at + w, rhs(k),
                                              start=(k == 0), stop=(k == kt - 1))
                        if k == kt - 1:
                            mm.then_inc(tile_done, 1)
                        elif j == pair[-1]:
                            mm.then_inc(slot_free, 1)
                        off += w
                        if after and k == kt - 1:
                            after(j)

            def sums(src, n, value, ones="mean"):
                pe.wait_ge(sq_ready, value)
                for k in range(KT):
                    mm = pe.matmul(bank(4, 0, n), C(ones, 0, P), src[:, k, 0:n], start=(k == 0), stop=(k == KT - 1))
                mm.then_inc(sums_done, 1)

            def layer_norm(name, m):
                first = products[name]["first"]
                for k in range(KT):
                    pe.wait_ge(*evac_value(first + k))
                    mm = pe.matmul(bank(5, 0, S), C("mean", 0, P), m_all[:, k, 0:S], start=(k == 0), stop=(k == KT - 1))
                mm.then_inc(mean_done, 1)
                sums(sq_all, S, m + 1)

            def first_layer(l):
                first = products[f"in1_{l}"]["first"]

                def small_at(lo, hi, rows):
                    return misc[rows, MISC * l + lo:MISC * l + hi]

                def evac_wait(t):
                    pe.wait_ge(*evac_value(first + t))

                def x_at(k):
                    return x_hi[:, k, 0:S], x_lo[:, k, 0:S]

                def rope():
                    evac_wait(5)
                    pe.wait_ge(tables_in, 48)
                    for i in range(3):
                        pe.matmul(bank(4 + i), C("rope_swap", 0, P), p1[:, 2 * i:2 * i + 2, :], start=True,
                                  stop=True).then_inc(rope_done, 1)

                product(f"in1_{l}", x_at, operand_ready(3 * l), S, lambda j: rope() if j == 7 else None)

                evac_wait(T_LR)
                for i in range(2):
                    mm = pe.matmul(bank(7, i * S, i * S + S), small_at(P + P * i, 2 * P + P * i, slice(0, 16)),
                                   p1[0:16, T_LR, :], start=True, stop=True)
                mm.then_inc(gk_done, 1)
                evac_wait(N_IN1 - 1)
                evac_wait(N_IN1 - 2)
                evac_wait(N_IN1 - 3)
                evac_wait(N_IN1 - 4)
                for b in range(2):
                    for c in range(2):
                        n = 2 * b + c
                        mm = pe.transpose(bank(0, n * P, n * P + P), p1[:, T_VS + b, c * P:c * P + P], ident)
                mm.then_inc(v_turned, 1)
                for i in range(3):
                    for c in range(2):
                        n = 2 * i + c
                        mm = pe.transpose(bank(1 + n // 4, (n % 4) * P, (n % 4) * P + P), p1[:, T_GV + i, c * P:c * P + P], ident)
                mm.then_inc(gv_turned, 1)
                pe.wait_ge(gate_sig, l + 1)
                for c in range(2):
                    mm = pe.transpose(bank(3, c * 18, c * 18 + 18), p1[32:50, T_LR, c * P:c * P + P], C("ident", 32, 50, slice(32, 50)))
                mm.then_inc(gates_turned, 1)

                pe.wait_ge(roped_ready, 3 * l + 3)
                for which in range(2):
                    w1 = matrices[f"cmp_{l}_{which}"]
                    await_slot(w1)
                    pe.wait_ge(tb_split, l + 1)
                    for j in range(CMP_BLOCK):
                        for g in range(2):
                            r = slice(g * HD, g * HD + HD)
                            mm = split_matmul(bank(4 + g, 16 * which, 16 * which + CMP_N, r), w1, j * HD, j * HD + HD,
                                              (tb_hi[r, which, j, :], tb_lo[r, which, j, :]), j == 0, j == CMP_BLOCK - 1, r)
                    mm.then_inc(slot_free, 1)
                pe.matmul(bank(6, 0, 1), ident, C("eps", 0, 1), start=True, stop=True).then_inc(hid_done, 1)
                pe.wait_ge(hid_ready, l + 1)
                pe.wait_ge(gk_biased, l + 1)
                for g in range(2):
                    r = slice(g * HD, g * HD + HD)
                    pe.matmul(bank(6 + g, 0, CMP_N, r), small_at(0, HD, r), hid[r, 0, 0:CMP_N], start=True, stop=True)
                    mm = pe.matmul(bank(6 + g, 64, 64 + HD, slice(0, CMP_N)), hid[r, 1, 0:CMP_N], small_at(HD, 2 * HD, r),
                                   start=True, stop=True)
                mm.then_inc(kcvc_done, 1)

                pe.wait_ge(kcvc_ready, l + 1)
                for g in range(2):
                    r = slice(g * HD, g * HD + HD)
                    for c in range(2):
                        for j in range(NSA_J):
                            at = (c * NSA_J + j) * 16
                            mm = pe.matmul(bank(4 + g, at, at + CMP_N), roped[r, T_Q + j, c * P:c * P + P], kc[r, 0:CMP_N],
                                           start=True, stop=True)
                mm.then_inc(cmp_scored, 1)
                pe.wait_ge(cmp_ready, l + 1)
                pe.wait_ge(toks_ready, l + 1)
                for n in range(12):
                    mm = pe.transpose(bank(n // 4, (n % 4) * P, (n % 4) * P + P, slice(0, CMP_N)), sc[:, n, 0:CMP_N], ident)
                mm.then_inc(cmp_turned, 1)

                units = [(c, j, g) for c in range(2) for j in range(NSA_J) for g in range(2)]
                base = 12 * l

                def scores(u):
                    c, j, g = units[u]
                    r, nk = slice(g * HD, g * HD + HD), (c + 1) * P
                    if u >= 2:
                        pe.wait_ge(attn_exp, base + u - 1)
                    for b in range(2):
                        mm = pe.matmul(bank(6 + u % 2, b * nk, b * nk + nk), roped[r, T_Q + j, c * P:c * P + P],
                                       roped[r, T_KS + b, 0:nk], start=True, stop=True)
                    mm.then_inc(scores_done, 1)

                def turn(u):
                    c, j, g = units[u]
                    pe.wait_ge(attn_p, base + u + 1)
                    if u >= 2:
                        pe.wait_ge(pt_ready, base + u - 1)
                    else:
                        pe.wait_ge(ptc_ready, l + 1)
                    for b in range(2):
                        for k in range(c + 1):
                            n = b * (c + 1) + k
                            mm = pe.transpose(bank(u % 2, n * P, n * P + P), e_at[:, u % 2, b, k * P:k * P + P], ident)
                    mm.then_inc(p_turned, 1)

                def values(u):
                    c, j, g = units[u]
                    r = slice(g * HD, g * HD + HD)
                    pe.wait_ge(pt_ready, base + u + 1)
                    if u >= 2:
                        pe.wait_ge(mix_out, base + u - 1)
                    out = bank(2 + u % 2, 0, P, r)
                    pe.matmul(out, vc[0:CMP_N, g, :], ptc[0:CMP_N, (g * 2 + c) * NSA_J + j, :], start=True, stop=False)
                    for b in range(2):
                        for k in range(c + 1):
                            n = b * (c + 1) + k
                            last = b == 1 and k == c
                            mm = pe.matmul(out, v_tok[:, 2 * b + k, g * HD:g * HD + HD], pt_at[:, u % 2, n * P:n * P + P],
                                           start=False, stop=last)
                    mm.then_inc(pv_done, 1)

                for u in range(14):
                    if u < 12:
                        scores(u)
                    if 1 <= u < 13:
                        turn(u - 1)
                    if u >= 2:
                        values(u - 2)

                pe.wait_ge(kend_ready, l + 1)
                pe.wait_ge(cmp_shifted, l + 1)
                for i in range(2):
                    for c in range(2):
                        n = 2 * i + c
                        mm = pe.transpose(bank(4, n * P, n * P + P), shaped(kend, 2, S)[:, i, c * P:c * P + P], ident)
                mm.then_inc(kend_turned, 1)
                pe.wait_ge(gla_in, l + 1)
                pe.wait_ge(mix_out, base + 12)
                for h in range(GLA_H):
                    r, i = slice(32 * (h % 4), 32 * (h % 4) + 32), h // 4
                    for c in range(2):
                        n = 2 * i + c
                        mm = pe.matmul(bank(h % 4, n * P, n * P + P), shaped(kinv, 2, S)[r, i, c * P:c * P + P],
                                       shaped(qd, 2, S)[r, i, c * P:c * P + P], start=True, stop=True)
                mm.then_inc(a_done, 1)
                pe.wait_ge(kend_tok_ready, l + 1)
                pe.wait_ge(attn_exp, base + 12)
                for n in range(3):
                    t = slice(64 * (n % 2), 64 * (n % 2) + 64)
                    for h in range(GLA_H):
                        i = h // 4
                        r = slice(32 * (h % 4), 32 * (h % 4) + 32)
                        at = (n // 2) * P + i * HD
                        mm = pe.matmul(bank(5 + n % 2, at, at + HD, r), kend_tok[t, 2 * i + n // 2, r],
                                       gv_tok[t, 2 * (h // 2) + n // 2, 64 * (h % 2):64 * (h % 2) + 64], start=True, stop=True)
                mm.then_inc(ds_done, 1)
                pe.wait_ge(a_masked, l + 1)
                pe.wait_ge(s_ready, l + 1)
                for h in range(GLA_H):
                    r, i, m = slice(32 * (h % 4), 32 * (h % 4) + 32), h // 4, h // 2
                    o = slice(64 * (h % 2), 64 * (h % 2) + 64)
                    b, at = GLA_BANKS[h % 4], i * S
                    for c in range(2):
                        pe.matmul(bank(b, at + c * P, at + c * P + P, o), gv_tok[:, 2 * m + c, o],
                                  at_gla[:, h % 4, 2 * i + c, :], start=True, stop=False)
                        for n in range(max(1, 2 * c), 2 * c + 2):
                            mm = pe.matmul(bank(b, at + n * 64, at + n * 64 + 64, o), s_gla[r, n - 1, i, :],
                                           shaped(qd, 2, S)[r, i, n * 64:n * 64 + 64], start=False, stop=(n == 2 * c + 1))
                mm.then_inc(o_done, 1)
                pe.wait_ge(pooled, l + 1)
                for g in range(4):
                    r = slice(64 * (g % 2), 64 * (g % 2) + 64)
                    mm = pe.matmul(bank(g % 2, (g // 2) * S, (g // 2) * S + S, r),
                                   small_at(384 + (g // 2) * HD, 384 + (g // 2) * HD + HD, r), pool_d[r, g // 2, :],
                                   start=True, stop=True)
                mm.then_inc(pool_done, 1)
                pe.wait_ge(o_squared, l + 1)
                pe.matmul(bank(5), C("head_mean", 0, P), o_sq[:, 0:2, :], start=True, stop=True)
                pe.matmul(bank(6, 0, S), C("head_mean", 0, P), o_sq[:, 2, :], start=True, stop=True).then_inc(o_sums, 1)

                pe.wait_ge(pool_mixed, 4 * l + 4)
                pe.wait_ge(gla_mixed, 3 * l + 1)
                product(f"out1_{l}", x_at, operand_ready(3 * l + 1), S)
                layer_norm(f"out1_{l}", 2 * l)
                product(f"up1_{l}", x_at, operand_ready(3 * l + 2), S)
                product(f"down1_{l}", lambda k: (f1_hi[:, k, :], f1_lo[:, k, :]), lambda k: pe.wait_ge(f_ready, FT1 * l + k + 1), S)
                layer_norm(f"down1_{l}", 2 * l + 1)

            def norm2(n):
                sums(sq_all, T, 4 + n + 1)

            def x_at(k):
                return x_hi[:, k, :], x_lo[:, k, :]

            def operand_ready(p):
                return lambda k: pe.wait_ge(x_ready, 8 * p + k + 1)

            def second_ffn(l):
                product(f"up2_{l}", x_at, operand_ready(7 + 2 * l), T)
                product(f"down2_{l}", lambda k: (f2_hi[:, k, :], f2_lo[:, k, :]), lambda k: pe.wait_ge(f_ready, 2 * FT1 + FT2 * l + k + 1), T)

            def griffin():
                product("in_g", x_at, operand_ready(6), T)
                first = products["in_g"]["first"]
                w = matrices["lru"]
                await_slot(w)
                pe.wait_ge(xr_split, 1)
                for n in range(16):
                    if n >= 4:
                        pe.wait_ge(lru_gated, n - 3)
                    split_matmul(bank(4 + n % 4, 0, T), w, n * P, n * P + P, (xr_hi[:, n % 8, :], xr_lo[:, n % 8, :]), True,
                                 True).then_inc(lru_done, 1)
                for t in range(GB):
                    pe.wait_ge(*evac_value(first + 25 - t))
                for c in range(3):
                    n = min(P, T - c * P)
                    mm = pe.transpose(bank(0, c * P, c * P + P, slice(0, n)), kv_t[:, 1, c * P:c * P + n], ident)
                mm.then_inc(v2_turned, 1)
                pe.matmul(bank(1, 0, 1), ident, C("eps", 0, 1), start=True, stop=True).then_inc(slot_free, 1)
                for b, (c, g, half) in enumerate(SWA_BATCHES):
                    r = slice(g * HD, g * HD + HD)
                    nk = SWA_KEYS[c]
                    if b >= 2:
                        pe.wait_ge(sw_max, b - 1)
                    else:
                        pe.wait_ge(lru_gated, 16)
                    s0 = 4 + 2 * (b % 2)
                    for j in range(4 if c < 2 else 1):
                        if c < 2:
                            lhs = qt[r, 4 * half + j, c * P:c * P + P]
                            per = 512 // nk
                            out = bank(s0 + j // per, (j % per) * nk, (j % per) * nk + nk)
                        else:
                            lhs = kv_t[r, 2, 0:P]
                            out = bank(s0, 0, nk)
                        mm = pe.matmul(out, lhs, kv_t[r, 0, 0:nk], start=True, stop=True)
                    mm.then_inc(sw_scored, 1)
                    if b >= 1:
                        swa_values(b - 1)
                swa_values(len(SWA_BATCHES) - 1)

                pe.wait_ge(sw_out, len(SWA_BATCHES))

                def mixed_at(k):
                    return (ya_hi[:, k, :], ya_lo[:, k, :]) if k < 8 else (yb_hi[:, k - 8, :], yb_lo[:, k - 8, :])

                product("out_g", mixed_at, lambda k: pe.wait_ge(y_split, 1 + k // 8), T)

            def swa_values(b):
                c, g, half = SWA_BATCHES[b]
                nk = SWA_KEYS[c]
                chunks = [(k * P, min(P, nk - k * P)) for k in range((nk + P - 1) // P)]
                heads = 4 if c < 2 else 1
                pe.wait_ge(sw_p, b + 1)
                if b >= 1:
                    pe.wait_ge(sw_pt, b)
                else:
                    pe.wait_ge(v2_ready, 1)
                for k, (k0, kn) in enumerate(chunks):
                    for j in range(heads):
                        mm = pe.transpose(bank(1 + k, j * P, j * P + P, slice(0, kn)), s_at[b % 2][:, j, k0:k0 + kn] if c < 2
                                          else s_at[b % 2].rearrange("p a b -> p (a b)")[:, k0:k0 + kn], ident)
                mm.then_inc(sw_turned, 1)
                pe.wait_ge(sw_pt, b + 1)
                if b >= 1:
                    pe.wait_ge(sw_out, b)
                for k, (k0, kn) in enumerate(chunks):
                    mm = pe.matmul(bank(0, 0, heads * P, slice(g * HD, g * HD + HD)), v_swa[0:kn, k, g * HD:g * HD + HD],
                                   pt_sw[0:kn, k, 0:heads * P], start=(k == 0), stop=(k == len(chunks) - 1))
                mm.then_inc(sw_pv, 1)

            def mamba():
                product("in_m", x_at, operand_ready(8), T)
                first = products["in_m"]["first"]
                for t in range(GB):
                    pe.wait_ge(*evac_value(first + 48 - t))
                pe.wait_ge(dt_w, 1)
                for ci, (t0, n) in enumerate(CHUNKS):
                    for v in range(3):
                        at = (3 * ci + v) * 32
                        mm = pe.transpose(bank(7, at, at + 32, slice(0, n)), dts[0:32, v, t0:t0 + n], C("ident", 0, 32, slice(0, 32)))
                mm.then_inc(dtt_done, 1)
                pe.wait_ge(conv_act, FT2 + 32)
                for ci, (t0, n) in enumerate(CHUNKS):
                    if ci == 0:
                        pe.wait_ge(dtt_ready, 1)
                    else:
                        pe.wait_ge(y_out, 8 * ci)
                    for i in range(4):
                        for t in range(4):
                            mm = pe.transpose(bank(4 + i, t * P, t * P + P, slice(0, n)), xbc[:, 4 * i + t, t0:t0 + n], ident)
                        mm.then_inc(x_turned, 1)
                    if ci < 2:
                        for g in range(SSM_G):
                            mm = pe.transpose(bank(g // 4, (g % 4) * P, (g % 4) * P + P, slice(0, n)), xbc[:, 16 + g, t0:t0 + n], ident)
                        mm.then_inc(b_turned, 1)
                        pe.wait_ge(b_ready, ci + 1)
                    pe.wait_ge(xdt_ready, ci + 1)

                    def spread(g):
                        q = 8 * ci + g
                        if g >= 2:
                            pe.wait_ge(mt_ready, q - 1)
                        pe.matmul(bank(q % 2, 0, n, slice(0, n)), xbc[:, 16 + g, t0:t0 + n], xbc[:, 24 + g, t0:t0 + n], start=True, stop=True)
                        for h in range(4):
                            mm = pe.matmul(bank(2 + q % 2, h * n, h * n + n), C("ident", 4 * g + h, 4 * g + h + 1, slice(0, 32)).to_broadcast([32, P]),
                                           dts[0:32, 1, t0:t0 + n], start=True, stop=True)
                        mm.then_inc(cs_spread, 1)

                    def outputs(g):
                        q = 8 * ci + g
                        pe.wait_ge(mt_ready, q + 1)
                        if ci:
                            pe.wait_ge(cd_ready, q - 8 + 1)
                        if g >= 2:
                            pe.wait_ge(y_out, q - 1)
                        for h in range(4):
                            o = slice(64 * (h % 2), 64 * (h % 2) + 64)
                            head = 4 * g + h
                            out = bank(4 + q % 2, (h // 2) * n, (h // 2) * n + n, o)
                            mm = pe.matmul(out, xdt[0:n, head * HD:head * HD + HD], seg[0:n, q % 2, h, 0:n], start=True, stop=(ci == 0))
                            if ci:
                                mm = pe.matmul(out, prev[:, head * HD:head * HD + HD], cd[:, q % 2, h, 0:n], start=False, stop=True)
                        if ci < 2:
                            mm = pe.matmul(bank(6 + q % 2, 0, 256), b_tok[0:n, g, :], xw[0:n, g * 256:g * 256 + 256], start=True, stop=True)
                        mm.then_inc(y_done, 1)

                    for g in range(9):
                        if g < 8:
                            spread(g)
                        if g:
                            outputs(g - 1)
                for g in range(SSM_G):
                    pe.wait_ge(zy_sq, g + 1)
                    if g >= 4:
                        pe.wait_ge(zy_rstd, g - 3)
                    for i in range(2):
                        mm = pe.matmul(bank(g % 4, 0, T), C("mean", 0, P), (u_all if g < 4 else m_all)[:, 2 * (g % 4) + i, :], start=(i == 0), stop=(i == 1))
                    mm.then_inc(zy_sums, 1)
                pe.wait_ge(zy_rstd, 8)
                product("out_m", lambda k: (ym_hi[:, k, :], ym_lo[:, k, :]), lambda k: pe.wait_ge(y_ready, k + 1), T)

            for l in range(DEPTH):
                first_layer(l)
            norm2(0)
            griffin()
            norm2(1)
            norm2(2)
            second_ffn(0)
            norm2(3)
            norm2(4)
            mamba()
            norm2(5)
            norm2(6)
            second_ffn(1)
            norm2(7)

        @block.scalar
        def _(act):
            tell = Tell(act, act_chain)

            def done(g):
                act.wait_ge(tile_done, g + 1)

            def evacuate(dst, g, n, func=ACT.Copy, rows=slice(0, P), scale=1.0):
                done(g)
                tell(act.activation(dst, bank(g % GB, 0, n, rows), func, scale=scale / W_SCALE), evacuated[g % GB], g // GB + 1)

            def high_part(i):
                if i >= len(slots):
                    return
                w, at = slots[i]["width"], (i % SPLIT) * SLOT
                freed_by_pe(act, i - SPLIT)
                if i >= SPLIT:
                    act.wait_ge(split_ready, i - SPLIT + 1)
                act.wait_ge(slot_full[i % RAW], 16 * (i // RAW + 1))
                tell(act.activation(high[:, at:at + w], raw[:, (i % RAW) * SLOT:(i % RAW) * SLOT + w], ACT.Copy, scale=W_SCALE), high_ready)

            def product(name, evac):
                for i, tiles in ready_steps(name):
                    for t in tiles:
                        evac(t)
                    high_part(i + SPLIT)

            def high_x(src, wait=None):
                for k in range(KT):
                    if wait:
                        wait(k)
                    tell(act.activation(x_hi[:, k, 0:src.shape[2]], src[:, k, :], ACT.Copy), xh_ready)

            def inverse_root(dst, tmp, src, eps, scale=1.0):
                tell(act.activation(tmp, src, ACT.Ln, bias=eps, scale=scale))
                tell.settle()
                return act.activation(dst, tmp, ACT.Exp, scale=-0.5)

            def finish_norm(value, n, eps):
                act.wait_ge(sums_done, value)
                tell(inverse_root(rstd[:, 0:n], lnv[:, 0:n], bank(4, 0, n), eps), rstd_ready)

            def layer_norm(m, which, l):
                act.wait_ge(centred, m + 1)
                tell(act.activation(sq_all[:, :, 0:S], m_all[:, :, 0:S], ACT.Square), sq_ready)
                finish_norm(m + 1, S, eps_ln)
                if m == 2 * DEPTH - 1:
                    return
                for k in range(KT):
                    act.wait_ge(ln_scaled, 8 * m + k + 1)
                    tell(act.activation(x_hi[:, k, 0:S], m_all[:, k, 0:S], ACT.Identity, bias=pcol(f"ln{which}_b{l}", k)), xh_ready)

            def first_layer(l):
                first = products[f"in1_{l}"]["first"]
                widths = products[f"in1_{l}"]["widths"]

                def evac(t):
                    rows = slice(0, widths[t])
                    if T_Q <= t < T_Q + NSA_J:
                        evacuate(p1[:, t, :], first + t, S, scale=float(HD) ** -0.5)
                    elif t >= T_PU:
                        if t == T_PU:
                            act.wait_ge(pool_in, l + 1)
                        evacuate(pool_u[:, t - T_PU, 16:272], first + t, S)
                    else:
                        evacuate(p1[rows, t, :], first + t, S, rows=rows)

                product(f"in1_{l}", evac)
                tell.settle()
                tell(act.activation(p1[32:50, T_LR, :], p1[32:50, T_LR, :], ACT.Sigmoid), gate_sig)
                act.wait_ge(gk_biased, l + 1)
                tell(act.activation(gk_l, gk_x, ACT.Abs))
                tell.settle()
                tell(act.activation(gk_l, gk_l, ACT.Exp, scale=-1.0))
                tell.settle()
                tell(act.activation(gk_l, gk_l, ACT.Ln, bias=1.0), gk_logged)
                act.wait_ge(tb_ready, 2 * l + 2)
                tell(act.activation(tb_hi, tb, ACT.Copy), tb_high)
                act.wait_ge(v_turned, l + 1)
                act.activation(v_tok, shaped(bank(0), 4, P), ACT.Copy)
                act.wait_ge(gv_turned, l + 1)
                act.activation(gv_tok[:, 0:4, :], shaped(bank(1), 4, P), ACT.Copy)
                act.activation(gv_tok[:, 4:6, :], shaped(bank(2, 0, 256), 2, P), ACT.Copy)
                act.wait_ge(gates_turned, l + 1)
                tell(act.activation(gates_t, shaped(bank(3, 0, 36), 2, 18), ACT.Copy), toks_ready)
                act.wait_ge(bcum_ready, l + 1)
                act.activation(ep, bc, ACT.Exp, scale=1.0 / 16.0)
                act.activation(en, bc, ACT.Exp, scale=-1.0 / 16.0)
                tell(act.activation(gk_x, gk_l, ACT.Exp, scale=1.0 / 16.0), decays_ready)
                act.wait_ge(hid_done, l + 1)
                for g in range(2):
                    r = slice(g * HD, g * HD + HD)
                    ins = act.activation(hid[r, :, 0:CMP_N], shaped(bank(4 + g, 0, 32, r), 2, 16)[:, :, 0:CMP_N], ACT.Gelu_apprx_tanh, scale=1.0 / W_SCALE)
                tell(ins, hid_ready)
                for which in range(2):
                    high_part(matrices[f"cmp_{l}_{which}"] + SPLIT)
                act.wait_ge(kcvc_done, l + 1)
                for g in range(2):
                    r = slice(g * HD, g * HD + HD)
                    act.activation(kc[r, 0:CMP_N], bank(6 + g, 0, CMP_N, r), ACT.Copy)
                    ins = act.activation(vc[0:CMP_N, g, :], bank(6 + g, 64, 64 + HD, slice(0, CMP_N)), ACT.Copy)
                tell(ins, kcvc_ready)
                act.wait_ge(cmp_shifted, l + 1)
                tell(act.activation(sc[:, :, 0:CMP_N], sc[:, :, 0:CMP_N], ACT.Exp), cmp_exped)

                base = 12 * l

                def exps(u):
                    nk = (u // 6 + 1) * P
                    act.wait_ge(scores_max, base + u + 1)
                    if u >= 2:
                        act.wait_ge(p_turned, base + u - 1)
                    for b in range(2):
                        ins = act.activation(e_at[:, u % 2, b, 0:nk], bank(6 + u % 2, b * nk, b * nk + nk), ACT.Exp,
                                             bias=nm[:, u % 2, b:b + 1], accum_out=nm[:, u % 2, 2 + b:3 + b])
                    tell(ins, attn_exp)

                def copy_pt(u):
                    n = 2 * (u // 6 + 1) * P
                    act.wait_ge(p_turned, base + u + 1)
                    if u >= 2:
                        act.wait_ge(pv_done, base + u - 1)
                    tell(act.activation(pt_at[:, u % 2, 0:n], bank(u % 2, 0, n), ACT.Copy), pt_ready)

                def copy_out(u):
                    c, j, g = u // 6, (u % 6) // 2, u % 2
                    r = slice(g * HD, g * HD + HD)
                    act.wait_ge(pv_done, base + u + 1)
                    tell(act.activation(gmix[r, j, c * P:c * P + P], bank(2 + u % 2, 0, P, r), ACT.Copy), mix_out)

                for u in range(14):
                    if u < 12:
                        exps(u)
                    if u == 0:
                        act.wait_ge(cmp_turned, l + 1)
                        for n in range(3):
                            ins = act.activation(ptc[0:CMP_N, 4 * n:4 * n + 4, :], shaped(bank(n, rows=slice(0, CMP_N)), 4, P), ACT.Copy)
                        tell(ins, ptc_ready)
                    if 1 <= u < 13:
                        copy_pt(u - 1)
                    if u >= 2:
                        copy_out(u - 2)

                act.wait_ge(kend_turned, l + 1)
                tell(act.activation(kend_tok, shaped(bank(4), 4, P), ACT.Copy), kend_tok_ready)
                tell(act.activation(og_silu, p1[:, T_OG:T_OG + 3, :], ACT.Silu))
                act.wait_ge(o_done, l + 1)
                for q in range(4):
                    dst, src = gla_out(o_sq, q)
                    ins = act.activation(dst, src, ACT.Square)
                tell(ins, o_squared)
                act.wait_ge(pool_done, l + 1)
                for g in range(4):
                    r = slice(64 * (g % 2), 64 * (g % 2) + 64)
                    tell(act.activation(gmix[r, 6 + g // 2, :], bank(g % 2, (g // 2) * S, (g // 2) * S + S, r), ACT.Identity,
                                        scale=pcol(f"pool_scale{l}", g // 2, r)), pool_mixed)
                act.wait_ge(o_sums, l + 1)
                act.activation(o_rs[:, 0:2, :], shaped(bank(5), 2, S), ACT.Ln, bias=eps_rms)
                tell(act.activation(o_rs[:, 2, :], bank(6, 0, S), ACT.Ln, bias=eps_rms))
                tell.settle()
                tell(act.activation(o_rs, o_rs, ACT.Exp, scale=-0.5), o_rstd)

                tell.settle()
                high_x(gmix, lambda k: act.wait_ge(gla_mixed, 3 * l + k - 2) if 3 <= k < 6 else None)
                product(f"out1_{l}", lambda t: None)
                layer_norm(2 * l, 1, l)
                up = products[f"up1_{l}"]["first"]

                def relu(t):
                    if t >= 4:
                        act.wait_ge(f_ready, FT1 * l + t - 3)
                    evacuate(f_relu[:, t % 4, :], up + t, S, ACT.Relu)

                product(f"up1_{l}", relu)
                product(f"down1_{l}", lambda t: None)
                layer_norm(2 * l + 1, 2, l)

            def square_norm(n, src, wait):
                wait()
                tell(act.activation(sq_all, src, ACT.Square), sq_ready)
                finish_norm(4 + n + 1, T, eps_rms)
                if n % 2 == 0:
                    high_x(sq_all, lambda k: act.wait_ge(u_ready, 8 * (n // 2) + k + 1))

            def out_product(name):
                product(name, lambda t: evacuate(m_all[:, t, :], products[name]["first"] + t, T))

            def second_ffn(l):
                up = products[f"up2_{l}"]["first"]

                def gelu(i):
                    act.wait_ge(*evac_value(up + 2 * i))
                    tell(act.activation(cg[:, i % 2, :], cg[:, i % 2, :], ACT.Gelu_apprx_tanh), conv_act)

                def last_tap(t):
                    i, half = divmod(t, 2)
                    g, buf = up + t, (cg, cu)[half]
                    done(g)
                    if i >= 2:
                        act.wait_ge(f_ready, 2 * FT1 + FT2 * l + i - 1)
                    tell(act.activation(buf[:, i % 2, :], bank(g % GB, 0, T), ACT.Identity, scale=pcol(f"ffn_w{l}", 2 * 2 * FT2 + t),
                                        bias=pcol(f"ffn_b{l}", t)), conv_acc)
                    if half and i:
                        gelu(i - 1)

                product(f"up2_{l}", last_tap)
                gelu(FT2 - 1)
                out_product(f"down2_{l}")

            def griffin():
                first = products["in_g"]["first"]

                def evac(t):
                    i, g = t % 8, first + t
                    if t < 8:
                        done(g)
                        tell(act.activation(xr[:, i, :], bank(g % GB, 0, T), ACT.Identity, scale=pcol("lru_w", 24 + i), bias=pcol("lru_b", i)), conv_acc)
                    elif t < 16:
                        evacuate(gg[:, i, :], g, T, ACT.Gelu_apprx_tanh)
                    elif t < 24:
                        done(g)
                        act.activation(kv_t[:, 2, META * i:META * i + META], bank(g % GB, 2 * P, T), ACT.Copy, scale=float(HD) ** -0.5 / W_SCALE)
                        evacuate(qt[:, i, :], g, T, scale=float(HD) ** -0.5)
                    else:
                        evacuate(kv_t[:, i, :], g, T)

                product("in_g", evac)
                act.wait_ge(conv_done, 1)
                tell(act.activation(xr_hi, xr, ACT.Copy), xr_high)
                act.wait_ge(conv_done, 1)
                tell(act.activation(lnv[:, 16:24], lnv[:, 8:16], ACT.Abs))
                tell.settle()
                tell(act.activation(lnv[:, 16:24], lnv[:, 16:24], ACT.Exp, scale=-1.0))
                tell.settle()
                tell(act.activation(lnv[:, 16:24], lnv[:, 16:24], ACT.Ln, bias=1.0), lru_softplus)
                for n in range(16):
                    act.wait_ge(lru_done, n + 1)
                    dst = (rg if n < 8 else ig)[:, n % 8, :]
                    tell(act.activation(dst, bank(4 + n % 4, 0, T), ACT.Sigmoid, bias=pcol("lru_ba" if n < 8 else "lru_bx", n % 8), scale=1.0 / W_SCALE), lru_gated)
                high_part(matrices["lru"] + SPLIT)
                act.wait_ge(lru_log, 1)
                act.activation(a_sc, la, ACT.Exp)
                act.activation(th, la, ACT.Tanh, scale=-1.0)
                tell(act.activation(sq_all, la, ACT.Exp, scale=2.0), lru_exp)
                act.wait_ge(v2_turned, 1)
                act.activation(v_swa[:, 0:2, :], shaped(bank(0, 0, 256), 2, P), ACT.Copy)
                tell(act.activation(v_swa[0:16, 2, :], bank(0, 256, 384, slice(0, 16)), ACT.Copy), v2_ready)
                act.wait_ge(lru_a2, 1)
                tell(act.activation(th, th, ACT.Sqrt), lru_root)
                act.wait_ge(lru_out, 1)
                tell(act.activation(ya_hi, gmix_a, ACT.Copy), ya_high)
                for b, (c, g, half) in enumerate(SWA_BATCHES):
                    nk = SWA_KEYS[c]
                    heads = 4 if c < 2 else 1
                    act.wait_ge(sw_max, b + 1)
                    st = sm[:, b % 2]
                    for j in range(heads):
                        s = s_at[b % 2][:, j, 0:nk] if c < 2 else s_at[b % 2].rearrange("p a b -> p (a b)")[:, 0:nk]
                        act.activation(s, s, ACT.Exp, bias=st[:, 1, j:j + 1], accum_out=st[:, 2, j:j + 1])
                    tell(act.activation(st[:, 3, 0:heads], st[:, 3, 0:heads], ACT.Exp), sw_exp)
                    if b:
                        swa_copies(b - 1)
                swa_copies(len(SWA_BATCHES) - 1)
                tell.settle()
                tell(act.activation(yb_hi, gmix_b, ACT.Copy), ya_high)
                out_product("out_g")

            def swa_copies(b):
                c, g, half = SWA_BATCHES[b]
                nk = SWA_KEYS[c]
                heads = 4 if c < 2 else 1
                act.wait_ge(sw_turned, b + 1)
                if b:
                    act.wait_ge(sw_pv, b)
                for k in range((nk + P - 1) // P):
                    rows = slice(0, min(P, nk - k * P))
                    ins = act.activation(pt_sw[rows, k, 0:heads * P], bank(1 + k, 0, heads * P, rows), ACT.Copy)
                tell(ins, sw_pt)
                act.wait_ge(sw_pv, b + 1)
                r = slice(g * HD, g * HD + HD)
                if c < 2:
                    ins = act.activation(gmix_b[r, 4 * half:4 * half + 4, c * P:c * P + P], shaped(bank(0, rows=r), 4, P), ACT.Copy)
                else:
                    ins = act.activation(gmix_b[r, :, 2 * P:T], shaped(bank(0, 0, P, r), 8, META), ACT.Copy)
                tell(ins, sw_out)

            def mamba():
                first = products["in_m"]["first"]

                def softplus():
                    act.wait_ge(*evac_value(first))
                    ab = dts[0:32, 3, :]
                    tell(act.activation(ab, dts[0:32, 0, :], ACT.Abs))
                    tell.settle()
                    tell(act.activation(ab, ab, ACT.Exp, scale=-1.0))
                    tell(act.activation(aneg[0:32, 0:1], pcol("a_log", 0, slice(0, 32)), ACT.Exp))
                    tell.settle()
                    tell(act.activation(ab, ab, ACT.Ln, bias=1.0), dt_logged)

                def silu(i):
                    act.wait_ge(*evac_value(first + 1 + i))
                    tell(act.activation(xbc[:, i, :], xbc[:, i, :], ACT.Silu), conv_act)

                def evac(t):
                    if t == 0:
                        return softplus()
                    i, g = t - 1, first + t
                    if i == 8:
                        act.wait_ge(cs_ready, 1)
                        tell(act.activation(dts[0:32, 4, :], dts[0:32, 4, :], ACT.Exp, scale=-1.0), ssd_end)
                    if i < 32:
                        done(g)
                        tell(act.activation(xbc[:, i, :], bank(g % GB, 0, T), ACT.Identity, scale=pcol("ssm_w", 96 + i), bias=pcol("ssm_b", i)), conv_acc)
                    else:
                        evacuate(z_t[:, i - 32, :], g, T, ACT.Silu)
                    if 1 <= i <= 32:
                        silu(i - 1)

                product("in_m", evac)
                act.wait_ge(dtt_done, 1)
                act.activation(dtt[0:META, 0], shaped(bank(7, 0, 96, slice(0, META)), 3, 32), ACT.Copy)
                tell(act.activation(dtt[:, 1:3], shaped(bank(7, 96, 288), 2, 3, 32), ACT.Copy), dtt_ready)
                for ci, (t0, n) in enumerate(CHUNKS):
                    if ci < 2:
                        act.wait_ge(b_turned, ci + 1)
                        for i in range(2):
                            ins = act.activation(b_tok[0:n, 4 * i:4 * i + 4, :], shaped(bank(i, rows=slice(0, n)), 4, P), ACT.Copy)
                        tell(ins, b_ready)
                    for g in range(SSM_G):
                        q = 8 * ci + g
                        if ci:
                            act.wait_ge(seg_ready, q + 1)
                            if q - 8 >= 2:
                                act.wait_ge(cd_ready, q - 8 - 1)
                                act.wait_ge(prev_ready, min(q - 1, 16))
                            act.activation(e2[:, q % 2], shaped(bank(2 + q % 2), 4, P), ACT.Exp)
                        act.wait_ge(seg_ready, q + 1)
                        s = seg[0:n, q % 2, :, 0:n]
                        tell(act.activation(s, s, ACT.Exp), ssd_exp)
                for g in range(SSM_G):
                    act.wait_ge(zy_ready, g + 1)
                    dst = (u_all if g < 4 else m_all)[:, 2 * (g % 4):2 * (g % 4) + 2, :]
                    tell(act.activation(dst, xbc[:, 2 * g:2 * g + 2, :], ACT.Square), zy_sq)

                def high_y(g):
                    act.wait_ge(zy_normed, 2 * g + 2)
                    tell(act.activation(ym_hi[:, 2 * g:2 * g + 2, :], xbc[:, 2 * g:2 * g + 2, :], ACT.Copy), ym_high)

                for g in range(SSM_G):
                    act.wait_ge(zy_sums, g + 1)
                    if g >= 2:
                        act.wait_ge(zy_normed, 2 * (g - 1))
                    tell(inverse_root(y_rs[:, g % 2, :], y_rs[:, g % 2, :], bank(g % 4, 0, T), eps_rms, scale=float(D) / 256.0), zy_rstd)
                    if g:
                        high_y(g - 1)
                high_y(SSM_G - 1)
                out_product("out_m")

            act.wait_ge(tables_in, 48)
            act.wait_ge(x_in, 32)
            for i in range(SPLIT):
                if i == 1:
                    high_x(h1)
                high_part(i)
            act.wait_ge(params_scaled, 1)
            for l in range(DEPTH):
                first_layer(l)

            square_norm(0, h_all, lambda: act.wait_ge(h_ready, 16 * DEPTH))
            griffin()
            square_norm(1, m_all, lambda: tell.settle())
            square_norm(2, h_all, lambda: act.wait_ge(h2_ready, 1))
            second_ffn(0)
            square_norm(3, m_all, lambda: tell.settle())
            square_norm(4, h_all, lambda: act.wait_ge(h2_ready, 2))
            mamba()
            square_norm(5, m_all, lambda: tell.settle())
            square_norm(6, h_all, lambda: act.wait_ge(h2_ready, 3))
            second_ffn(1)
            square_norm(7, m_all, lambda: tell.settle())

        @block.vector
        def _(dve):
            tell = Tell(dve, dve_chain)

            def low_part(i):
                if i >= len(slots):
                    return
                w, at = slots[i]["width"], (i % SPLIT) * SLOT
                dve.wait_ge(high_ready, i + 1)
                tell(dve.scalar_tensor_tensor(low[:, at:at + w], raw[:, (i % RAW) * SLOT:(i % RAW) * SLOT + w], W_SCALE,
                                              high[:, at:at + w], ALU.mult, ALU.subtract), split_ready)

            def product(name, evac=lambda t: None):
                for i, tiles in ready_steps(name):
                    for t in tiles:
                        evac(t)
                    low_part(i + SPLIT)

            def low_x(src, p):
                for k in range(KT):
                    dve.wait_ge(xh_ready, 8 * p + k + 1)
                    n = src.shape[2]
                    tell(dve.tensor_tensor(x_lo[:, k, 0:n], src[:, k, :], x_hi[:, k, 0:n], ALU.subtract), x_ready)

            def residual(name, n):
                first = products[name]["first"]

                def add(t):
                    g = first + t
                    dve.wait_ge(tile_done, g + 1)
                    dve.wait_ge(m_scaled, n + 1)
                    tell(dve.scalar_tensor_tensor(m_all[:, t, 0:S], bank(g % GB, 0, S), 1.0 / W_SCALE, m_all[:, t, 0:S], ALU.mult, ALU.add),
                         evacuated[g % GB], g // GB + 1)

                product(name, add)

            def layer_norm(m, which, l):
                dve.wait_ge(mean_done, m + 1)
                tell.settle()
                tell(dve.tensor_tensor(m_all[:, :, 0:S], m_all[:, :, 0:S], over(bank(5, 0, S), KT), ALU.subtract), centred)
                dve.wait_ge(rstd_ready, m + 1)
                tell.settle()
                for k in range(KT):
                    tell(dve.scalar_tensor_tensor(m_all[:, k, 0:S], m_all[:, k, 0:S], pcol(f"ln{which}_g{l}", k), rstd[:, 0:S],
                                                  ALU.mult, ALU.mult), ln_scaled)
                if m == 2 * DEPTH - 1:
                    return
                for k in range(KT):
                    dve.wait_ge(xh_ready, 8 * (2, 3, 5)[m] + k + 1)
                    tell(dve.scalar_tensor_tensor(x_lo[:, k, 0:S], m_all[:, k, 0:S], pcol(f"ln{which}_b{l}", k), x_hi[:, k, 0:S],
                                                  ALU.add, ALU.subtract), x_ready)

            def first_layer(l):
                first = products[f"in1_{l}"]["first"]

                def evac_wait(t):
                    dve.wait_ge(*evac_value(first + t))

                def rotate():
                    for i in range(3):
                        pair = roped[:, 2 * i:2 * i + 2, :]
                        dve.wait_ge(rope_done, 3 * l + i + 1)
                        tell(dve.tensor_tensor(pair, shaped(bank(4 + i), 2, S), over(C("sin", 0, S), 2), ALU.mult))
                        tell.settle()
                        dve.wait_ge(cos_ready, l + 1)
                        tell(dve.tensor_tensor(pair, pair, rope_cos[:, 2 * i:2 * i + 2, :], ALU.add), roped_ready)

                product(f"in1_{l}", lambda t: rotate() if t == 9 else None)
                tell.settle()
                evac_wait(T_VC)
                for which, src in ((0, roped[:, T_KC, :]), (1, p1[:, T_VC, :])):
                    windows = bass.AP(src.tensor, src.offset, [list(src.ap[0]), [1, CMP_BLOCK], [CMP_STRIDE, CMP_N]])
                    pos = par[:, PAR[f"pos{l}"] + 32 * which:PAR[f"pos{l}"] + 32 * which + 32]
                    tell(dve.tensor_tensor(tb[:, which], windows, along(pos, CMP_N), ALU.add), tb_ready)
                dve.wait_ge(gk_done, l + 1)
                for i in range(2):
                    ins = dve.tensor_scalar(shaped(gk_x, 2, S)[:, i, :], bank(7, i * S, i * S + S), pcol(f"b_gate{l}", i), None, ALU.add)
                tell(ins, gk_biased)
                dve.wait_ge(tb_high, l + 1)
                tell(dve.tensor_tensor(tb_lo, tb, tb_hi, ALU.subtract), tb_split)
                tell.settle()
                dve.wait_ge(gk_logged, l + 1)
                tell(dve.scalar_tensor_tensor(gk_l, gk_x, 0.0, gk_l, ALU.min, ALU.subtract))
                tell.settle()
                tell(dve.tensor_tensor_scan(bc, C("gla_reset", 0, 2 * S), gk_l, 0.0, ALU.mult, ALU.add))
                tell.settle()
                chunked = shaped(bc, 8, GLA_C)
                tell(dve.tensor_tensor(shaped(gk_l, 8, GLA_C), chunked[:, :, GLA_C - 1:GLA_C].to_broadcast([P, 8, GLA_C]), chunked, ALU.subtract), bcum_ready)
                dve.wait_ge(decays_ready, l + 1)
                p1q = p1[:, T_GQ:T_GQ + 2, :].rearrange("p a b -> p (a b)")
                p1k = p1[:, T_GK:T_GK + 2, :].rearrange("p a b -> p (a b)")
                dve.scalar_tensor_tensor(qd, p1q, float(np.float32(GLA_DK ** -0.5)), ep, ALU.mult, ALU.mult)
                tell(dve.tensor_tensor(kinv, p1k, en, ALU.mult), gla_in)
                tell(dve.tensor_tensor(kend, p1k, gk_x, ALU.mult), kend_ready)
                for which in range(2):
                    low_part(matrices[f"cmp_{l}_{which}"] + SPLIT)
                dve.wait_ge(cmp_scored, l + 1)
                s15 = sc[:, :, 0:CMP_N]
                mask = shaped(C("cmp_mask", 0, 192), 12, 16)
                for g in range(2):
                    ins = dve.tensor_tensor(sc[:, 6 * g:6 * g + 6, 0:CMP_N], shaped(bank(4 + g, 0, 96), 6, 16)[:, :, 0:CMP_N],
                                            mask[:, 6 * g:6 * g + 6, 0:CMP_N], ALU.add)
                tell(ins)
                tell.settle()
                tell(dve.tensor_reduce(sc_s[:, 0, :], s15, AX_X, ALU.max))
                tell.settle()
                tell(dve.tensor_scalar(sc_s[:, 1, :], sc_s[:, 0, :], MAX_FLOOR, None, ALU.max))
                tell.settle()
                tell(dve.tensor_tensor(s15, s15, along(sc_s[:, 1, :], CMP_N), ALU.subtract), cmp_shifted)
                dve.wait_ge(cmp_exped, l + 1)
                tell(dve.tensor_reduce(sc_s[:, 2, :], s15, AX_X, ALU.add))
                tell.settle()
                tell(dve.tensor_scalar(sc_s[:, 3, :], sc_s[:, 2, :], 1.0e-30, None, ALU.max))
                tell.settle()
                tell(dve.reciprocal(sc_s[:, 4, :], sc_s[:, 3, :]))
                tell.settle()
                dve.wait_ge(toks_ready, l + 1)
                gates = gates_t.rearrange("p c (g j b) -> p c g j b", g=2, j=3)
                for c in range(2):
                    r = sc_s[:, 4, :].rearrange("p (g c j) -> p g c j", g=2, c=2)[:, :, c, :]
                    ins = dve.tensor_tensor(sc_s[:, 0, :].rearrange("p (g c j) -> p g c j", g=2, c=2)[:, :, c, :], r, gates[:, c, :, :, 0], ALU.mult)
                tell(ins)
                tell.settle()
                tell(dve.tensor_tensor(s15, s15, along(sc_s[:, 0, :], CMP_N), ALU.mult), cmp_ready)

                base = 12 * l

                def maxima(u):
                    c = u // 6
                    nk = (c + 1) * P
                    b2 = shaped(bank(6 + u % 2, 0, 2 * nk), 2, nk)
                    dve.wait_ge(scores_done, base + u + 1)
                    if u >= 2:
                        dve.wait_ge(attn_exp, base + u - 1)
                    tell(dve.tensor_tensor(b2[:, :, c * P:nk], b2[:, :, c * P:nk], over(C("tri", 0, P), 2), ALU.add))
                    tell.settle()
                    tell(dve.tensor_reduce(nm[:, u % 2, 0:2], b2, AX_X, ALU.max, negate=True), scores_max)

                def weigh(u):
                    c, j, g = u // 6, (u % 6) // 2, u % 2
                    nk = (c + 1) * P
                    dve.wait_ge(attn_exp, base + u + 1)
                    tell(dve.reciprocal(nm[:, u % 2, 4:6], nm[:, u % 2, 2:4]))
                    tell.settle()
                    at = (g * 3 + j) * 3
                    tell(dve.tensor_tensor(nm[:, u % 2, 6:8], nm[:, u % 2, 4:6], gates_t[:, c, at + 1:at + 3], ALU.mult))
                    tell.settle()
                    for b in range(2):
                        e = e_at[:, u % 2, b, 0:nk]
                        ins = dve.tensor_scalar(e, e, nm[:, u % 2, 6 + b:7 + b], None, ALU.mult)
                    tell(ins, attn_p)

                for u in range(13):
                    if u < 12:
                        maxima(u)
                    if u:
                        weigh(u - 1)

                dve.wait_ge(a_done, l + 1)
                for b in range(4):
                    n = 4 if b < 2 else 2
                    ins = dve.tensor_tensor(at_gla[:, b, 0:n, :], shaped(bank(b, 0, n * P), n, P), over(C("gla_causal", 0, P), n), ALU.mult)
                tell(ins, a_masked)
                dve.wait_ge(ds_done, l + 1)
                epc = shaped(ep, 2, 4, GLA_C)
                for n in range(3):
                    for i in range(2):
                        rows = slice(0, P) if i == 0 else slice(0, HD)
                        ds = bank(5 + n % 2, (n // 2) * P + i * HD, (n // 2) * P + i * HD + HD, rows)
                        if n == 0:
                            ins = dve.tensor_copy(s_gla[rows, n, i, :], ds)
                        else:
                            ins = dve.scalar_tensor_tensor(s_gla[rows, n, i, :], s_gla[rows, n - 1, i, :], epc[rows, i, n, GLA_C - 1:GLA_C], ds,
                                                           ALU.mult, ALU.add)
                    tell(ins, s_ready if n == 2 else None)
                    tell.settle()
                dve.wait_ge(o_rstd, l + 1)
                for q in range(4):
                    dst, src = gla_out(o_rs, q)
                    ins = dve.tensor_tensor(dst, src, dst, ALU.mult)
                tell(ins)
                tell.settle()
                for i in range(3):
                    tell(dve.scalar_tensor_tensor(gmix[:, 3 + i, :], o_rs[:, i, :], pcol(f"norm_g{l}", i), og_silu[:, i, :], ALU.mult, ALU.mult), gla_mixed)

                low_x(gmix, 3 * l + 1)
                residual(f"out1_{l}", 2 * l)
                layer_norm(2 * l, 1, l)
                up = products[f"up1_{l}"]["first"]

                def square(t):
                    dve.wait_ge(*evac_value(up + t))
                    tell(dve.tensor_tensor(f1_hi[:, t, :], f_relu[:, t % 4, :], f_relu[:, t % 4, :], ALU.mult), fh_ready)

                product(f"up1_{l}", square)
                residual(f"down1_{l}", 2 * l + 1)
                layer_norm(2 * l + 1, 2, l)

            def pre_norm(n, name):
                dve.wait_ge(rstd_ready, 4 + n + 1)
                for k in range(KT):
                    tell(dve.scalar_tensor_tensor(sq_all[:, k, :], h_all[:, k, :], pcol(name, k), rstd, ALU.mult, ALU.mult), u_ready)
                low_x(sq_all, 6 + n // 2)

            def post_norm(n, name):
                dve.wait_ge(rstd_ready, 4 + n + 1)
                for k in range(KT):
                    tell(dve.scalar_tensor_tensor(m_all[:, k, :], m_all[:, k, :], pcol(name, k), rstd, ALU.mult, ALU.mult))
                tell.settle()
                tell(dve.tensor_tensor(h_all, h_all, m_all, ALU.add), h2_ready)

            def taps(dst, g, count, acc_value, weight):
                dve.wait_ge(conv_acc, acc_value)
                for back in range(1, count):
                    ins = dve.scalar_tensor_tensor(dst[:, back:T], bank(g % GB, 0, T - back), weight(count - 1 - back), dst[:, back:T], ALU.mult, ALU.add)
                    if back < count - 1:
                        tell(ins)
                        tell.settle()
                tell(ins, evacuated[g % GB], g // GB + 1)

            def second_ffn(l):
                up = products[f"up2_{l}"]["first"]
                acc0 = (8, 8 + 2 * FT2 + 32)[l]
                act0 = (0, FT2 + 32)[l]

                def gated(i):
                    dve.wait_ge(conv_act, act0 + i + 1)
                    tell(dve.tensor_tensor(f2_hi[:, i, :], cg[:, i % 2, :], cu[:, i % 2, :], ALU.mult), fh_ready)

                def other_taps(t):
                    i, half = divmod(t, 2)
                    taps((cg, cu)[half][:, i % 2, :], up + t, 3, acc0 + t + 1, lambda tap: pcol(f"ffn_w{l}", tap * 2 * FT2 + t))
                    if half and i:
                        gated(i - 1)

                product(f"up2_{l}", other_taps)
                tell.settle()
                gated(FT2 - 1)
                product(f"down2_{l}")

            def griffin():
                first = products["in_g"]["first"]
                product("in_g", lambda t: taps(xr[:, t, :], first + t, 4, t + 1, lambda tap: pcol("lru_w", tap * 8 + t)) if t < 8 else None)
                tell.settle()
                tell(dve.tensor_scalar(lnv[:, 8:16], par[:, PAR["lru_lam"]:PAR["lru_lam"] + 8], -1.0, None, ALU.mult), conv_done)
                dve.wait_ge(xr_high, 1)
                tell(dve.tensor_tensor(xr_lo, xr, xr_hi, ALU.subtract), xr_split)
                dve.wait_ge(lru_softplus, 1)
                tell.settle()
                tell(dve.scalar_tensor_tensor(lnv[:, 24:32], lnv[:, 8:16], 0.0, lnv[:, 16:24], ALU.max, ALU.add))
                tell.settle()
                tell(dve.tensor_scalar(lnv[:, 24:32], lnv[:, 24:32], -8.0, None, ALU.mult))
                tell.settle()
                dve.wait_ge(lru_gated, 8)
                tell(dve.tensor_tensor(la, rg, along(lnv[:, 24:32], T), ALU.mult), lru_log)
                dve.wait_ge(lru_gated, 16)
                tell(dve.tensor_tensor(ig, ig, xr, ALU.mult))
                low_part(matrices["lru"] + SPLIT)
                dve.wait_ge(lru_exp, 1)
                tell(dve.scalar_tensor_tensor(th, sq_all, 1.0, th, ALU.add, ALU.mult), lru_a2)
                dve.wait_ge(lru_root, 1)
                tell.settle()
                dve.memset(a_sc[:, :, 0:1], 0.0)
                tell(dve.tensor_tensor(th, th, ig, ALU.mult))
                tell.settle()
                flat = lambda a: a.rearrange("p k t -> p (k t)")
                tell(dve.tensor_tensor_scan(flat(gmix_a), flat(a_sc), flat(th), 0.0, ALU.mult, ALU.add))
                tell.settle()
                tell(dve.tensor_tensor(gmix_a, gmix_a, gg, ALU.mult), lru_out)
                dve.wait_ge(ya_high, 1)
                tell(dve.tensor_tensor(ya_lo, gmix_a, ya_hi, ALU.subtract), y_split)
                for b in range(len(SWA_BATCHES) + 1):
                    if b < len(SWA_BATCHES):
                        swa_scores(b)
                    if b:
                        swa_weigh(b - 1)
                dve.wait_ge(ya_high, 2)
                tell(dve.tensor_tensor(yb_lo, gmix_b, yb_hi, ALU.subtract), y_split)
                product("out_g")

            def swa_scores(b):
                c, g, half = SWA_BATCHES[b]
                nk = SWA_KEYS[c]
                heads = 4 if c < 2 else 1
                st = sm[:, b % 2]
                s0 = 4 + 2 * (b % 2)
                dve.wait_ge(sw_scored, b + 1)
                if b >= 2:
                    dve.wait_ge(sw_turned, b - 1)
                per = 512 // nk
                flat = s_at[b % 2].rearrange("p a b -> p (a b)")
                for j in range(heads):
                    src = bank(s0 + j // per, (j % per) * nk, (j % per) * nk + nk)
                    slope = C("slope_last", g, g + 1) if c == 2 else -SLOPES[g * SWA_J + 4 * half + j]
                    dst = s_at[b % 2][:, j, 0:nk] if c < 2 else flat[:, 0:nk]
                    ins = dve.scalar_tensor_tensor(dst, C(f"dist{c}", 0, nk), slope, src, ALU.mult, ALU.add)
                tell(ins)
                tell.settle()
                if c < 2:
                    tell(dve.tensor_reduce(st[:, 0, 0:heads], s_at[b % 2][:, :, 0:nk], AX_X, ALU.max))
                    sink = par[:, PAR["sinks"] + g * SWA_J + 4 * half:PAR["sinks"] + g * SWA_J + 4 * half + 4]
                else:
                    tell(dve.tensor_reduce(st[:, 0, 0:1], flat[:, 0:nk], AX_X, ALU.max))
                    sink = pcol("sinks_last", g)
                tell.settle()
                tell(dve.tensor_tensor(st[:, 4, 0:heads], st[:, 0, 0:heads], sink, ALU.max))
                tell.settle()
                dve.tensor_scalar(st[:, 1, 0:heads], st[:, 4, 0:heads], -1.0, None, ALU.mult)
                tell(dve.tensor_tensor(st[:, 3, 0:heads], sink, st[:, 4, 0:heads], ALU.subtract), sw_max)

            def swa_weigh(b):
                c, g, half = SWA_BATCHES[b]
                nk = SWA_KEYS[c]
                heads = 4 if c < 2 else 1
                st = sm[:, b % 2]
                dve.wait_ge(sw_exp, b + 1)
                tell(dve.tensor_tensor(st[:, 5, 0:heads], st[:, 2, 0:heads], st[:, 3, 0:heads], ALU.add))
                tell.settle()
                tell(dve.reciprocal(st[:, 0, 0:heads], st[:, 5, 0:heads]))
                tell.settle()
                if c < 2:
                    s = s_at[b % 2][:, :, 0:nk]
                    tell(dve.tensor_tensor(s, s, along(st[:, 0, 0:heads], nk), ALU.mult), sw_p)
                else:
                    s = s_at[b % 2].rearrange("p a b -> p (a b)")[:, 0:nk]
                    tell(dve.tensor_scalar(s, s, st[:, 0, 0:1], None, ALU.mult), sw_p)

            def mamba():
                first = products["in_m"]["first"]
                r32 = slice(0, 32)
                dt, cs, w, ab, dl = (dts[r32, i, :] for i in range(5))

                def step_sizes():
                    dve.wait_ge(tile_done, first + 1)
                    tell(dve.tensor_scalar(dt, bank(first % GB, 0, T, r32), 1.0 / W_SCALE, pcol("dt_bias", 0, r32), ALU.mult, ALU.add),
                         evacuated[first % GB], first // GB + 1)
                    dve.wait_ge(dt_logged, 1)
                    tell(dve.scalar_tensor_tensor(dt, dt, 0.0, ab, ALU.max, ALU.add))
                    tell.settle()
                    tell(dve.tensor_scalar(dl, dt, aneg[r32, 0:1], -1.0, ALU.mult, ALU.mult))
                    tell.settle()
                    tell(dve.tensor_tensor_scan(cs, C("ssd_reset", 0, T, r32), dl, 0.0, ALU.mult, ALU.add))
                    tell.settle()
                    for t0, n in CHUNKS:
                        ins = dve.tensor_scalar(dts[r32, 4, t0:t0 + n], dts[r32, 1, t0:t0 + n], dts[r32, 1, t0 + n - 1:t0 + n], None, ALU.subtract)
                    tell(ins, cs_ready)

                def evac(t):
                    if t == 0:
                        return step_sizes()
                    i = t - 1
                    if i == 16:
                        dve.wait_ge(ssd_end, 1)
                        tell(dve.tensor_tensor(w, dt, dl, ALU.mult), dt_w)
                    if i < 32:
                        taps(xbc[:, i, :], first + t, 4, 8 + 2 * FT2 + t, lambda tap: pcol("ssm_w", tap * 32 + i))

                product("in_m", evac)
                dve.wait_ge(dtt_ready, 1)
                for ci, (t0, n) in enumerate(CHUNKS):
                    rows = slice(0, n)
                    for i in range(4):
                        dve.wait_ge(x_turned, 4 * ci + i + 1)
                        src = shaped(bank(4 + i, rows=rows), 8, HD)
                        ins = dve.tensor_tensor(shaped(xdt[rows, 512 * i:512 * i + 512], 8, HD), src, along(dtt[rows, ci, 0, 8 * i:8 * i + 8], HD), ALU.mult)
                        if ci < 2:
                            ins = dve.tensor_tensor(shaped(xw[rows, 512 * i:512 * i + 512], 8, HD), src, along(dtt[rows, ci, 2, 8 * i:8 * i + 8], HD), ALU.mult)
                    tell(ins, xdt_ready)

                    def segments(g):
                        q = 8 * ci + g
                        dve.wait_ge(cs_spread, q + 1)
                        if g >= 2:
                            dve.wait_ge(y_done, q - 1)
                        for h in range(4):
                            ins = dve.scalar_tensor_tensor(seg[rows, q % 2, h, 0:n], bank(2 + q % 2, h * n, h * n + n, rows),
                                                           dtt[rows, ci, 1, 4 * g + h:4 * g + h + 1], C("ssd_causal", 0, n, rows), ALU.subtract, ALU.min)
                        tell(ins, seg_ready)

                    def scores(g):
                        q = 8 * ci + g
                        dve.wait_ge(ssd_exp, q + 1)
                        s = seg[rows, q % 2, :, 0:n]
                        tell(dve.tensor_tensor(s, s, over(bank(q % 2, 0, n, rows), 4), ALU.mult), mt_ready)

                    def outputs(g):
                        q = 8 * ci + g
                        dve.wait_ge(y_done, q + 1)
                        st = prev[:, 256 * g:256 * g + 256]
                        if ci == 0:
                            tell(dve.tensor_copy(st, bank(6 + q % 2, 0, 256)), prev_ready)
                        elif ci == 1:
                            tell(dve.tensor_tensor(shaped(st, 4, HD), shaped(st, 4, HD), e2[:, q % 2, :, P - 1:P].to_broadcast([P, 4, HD]), ALU.mult))
                            tell.settle()
                            tell(dve.tensor_tensor(st, st, bank(6 + q % 2, 0, 256), ALU.add), prev_ready)
                        for i in range(2):
                            t = xbc[:, 2 * g + i, t0:t0 + n]
                            ins = dve.scalar_tensor_tensor(t, t, pcol("d_skip", 2 * g + i), bank(4 + q % 2, i * n, i * n + n), ALU.mult, ALU.add)
                        tell(ins, y_out)

                    for g in range(10):
                        if g < 8:
                            segments(g)
                        if 1 <= g < 9:
                            scores(g - 1)
                        if g >= 2:
                            outputs(g - 2)
                tell.settle()
                for g in range(SSM_G):
                    t = xbc[:, 2 * g:2 * g + 2, :]
                    tell(dve.tensor_tensor(t, t, z_t[:, 2 * g:2 * g + 2, :], ALU.mult), zy_ready)
                tell.settle()

                def low_y(g):
                    dve.wait_ge(ym_high, g + 1)
                    for i in (2 * g, 2 * g + 1):
                        tell(dve.tensor_tensor(ym_lo[:, i, :], xbc[:, i, :], ym_hi[:, i, :], ALU.subtract), y_ready)

                for g in range(SSM_G):
                    dve.wait_ge(zy_rstd, g + 1)
                    dve.wait_ge(zy_sq, g + 1)
                    for i in range(2):
                        t = xbc[:, 2 * g + i, :]
                        tell(dve.scalar_tensor_tensor(t, t, pcol("gate_norm", 2 * g + i), y_rs[:, g % 2, :], ALU.mult, ALU.mult), zy_normed)
                    if g:
                        low_y(g - 1)
                low_y(SSM_G - 1)
                product("out_m")

            dve.wait_ge(tables_in, 48)
            for name, n in (("ffn_w0", 3 * 2 * FT2), ("ffn_w1", 3 * 2 * FT2), ("lru_w", 32), ("ssm_w", 4 * 32)):
                at = par[:, PAR[name]:PAR[name] + n]
                ins = dve.tensor_scalar(at, at, 1.0 / W_SCALE, None, ALU.mult)
            tell(ins, params_scaled)
            for i in range(SPLIT):
                low_part(i)
                if i == 0:
                    low_x(h1, 0)
            for l in range(DEPTH):
                first_layer(l)
            pre_norm(0, "mix_pre0")
            griffin()
            post_norm(1, "mix_post0")
            pre_norm(2, "ffn_pre0")
            second_ffn(0)
            post_norm(3, "ffn_post0")
            pre_norm(4, "mix_pre1")
            mamba()
            post_norm(5, "mix_post1")
            pre_norm(6, "ffn_pre1")
            second_ffn(1)
            post_norm(7, "ffn_post1")

        @block.gpsimd
        def _(pool):
            tell = Tell(pool, pool_chain)
            pool.wait_ge(tables_in, 48)
            pool.wait_ge(x_in, 32)

            def layer_norm(m, which, l):
                for k in range(KT):
                    pool.wait_ge(ln_scaled, 8 * m + k + 1)
                    tell(pool.tensor_scalar(h1[:, k, :], m_all[:, k, 0:S], pcol(f"ln{which}_b{l}", k), None, ALU.add), h_ready)
                if which == 1:
                    pool.wait_ge(x_ready, 8 * (3 * l + 3))
                    tell.settle()
                    tell(pool.tensor_scalar(m_all[:, :, 0:S], h1, ALPHA, None, ALU.mult), m_scaled)

            def hidden_low(n0, tiles, a, b, depth, hi, lo, tmp):
                for t in range(tiles):
                    pool.wait_ge(fh_ready, n0 + t + 1)
                    tell(pool.tensor_tensor(tmp[:, t % 2, :], a[:, t % depth, :], b[:, t % depth, :], ALU.mult))
                    tell.settle()
                    tell(pool.tensor_tensor(lo[:, t, :], tmp[:, t % 2, :], hi[:, t, :], ALU.subtract), f_ready)

            for l in range(DEPTH):
                first = products[f"in1_{l}"]["first"]
                if l:
                    pool.wait_ge(x_ready, 8 * 3 * l + 8)
                    tell.settle()
                for buf in (pool_u, pool_a, pool_b):
                    ins = pool.memset(buf[:, :, 0:16], 0.0)
                tell(ins, pool_in)
                for t in range(3, 6):
                    pool.wait_ge(*evac_value(first + t))
                pool.wait_ge(*evac_value(first + 2))
                tell(pool.tensor_tensor(rope_cos, p1[:, 0:6, :], over(C("cos", 0, S), 6), ALU.mult), cos_ready)
                pool.wait_ge(*evac_value(first + T_PU + 1))
                pool.wait_ge(*evac_value(first + T_PU))
                live, shift = pool_u, 1
                inv = shaped(C("pool_inv", 0, 2 * S), 2, S)
                for step, dst in enumerate((pool_a, pool_b, pool_a, pool_b)):
                    tell(pool.tensor_tensor(dst[:, :, 16:272], live[:, :, 16:272], live[:, :, 16 - shift:272 - shift], ALU.add))
                    tell.settle()
                    r = slice(64 * (step % 2), 64 * (step % 2) + 64)
                    i = step // 2
                    tell(pool.tensor_tensor(pool_d[r, i, :], dst[r, i, 16:272], inv[r, i, :], ALU.mult))
                    tell.settle()
                    live, shift = dst, 2 * shift
                tell(pool.tensor_tensor(pool_d, pool_d, pool_u[:, :, 16:272], ALU.subtract), pooled)
                pool.wait_ge(pool_done, l + 1)
                tell.settle()
                tell(pool.tensor_scalar(m_all[:, :, 0:S], h1, ALPHA, None, ALU.mult), m_scaled)
                layer_norm(2 * l, 1, l)
                hidden_low(FT1 * l, FT1, f_relu, f_relu, 4, f1_hi, f1_lo, f_sq)
                layer_norm(2 * l + 1, 2, l)
            hidden_low(2 * FT1, FT2, cg, cu, 2, f2_hi, f2_lo, f_prod)
            for ci, (t0, n) in enumerate(CHUNKS):
                if ci == 0:
                    continue
                for g in range(SSM_G):
                    q = 8 * ci + g
                    pool.wait_ge(ssd_exp, q + 1)
                    if g >= 2 or ci > 1:
                        pool.wait_ge(y_done, q - 1)
                    tell(pool.tensor_tensor(cd[:, q % 2], e2[:, q % 2], over(xbc[:, 24 + g, t0:t0 + n], 4), ALU.mult), cd_ready)
            hidden_low(2 * FT1 + FT2, FT2, cg, cu, 2, f2_hi, f2_lo, f_prod)


SWA_KEYS = [P, 2 * P, T]
SWA_BATCHES = [(c, g, half) for c in range(2) for g in range(2) for half in range(2)] + [(2, 0, 0), (2, 1, 0)]


def _columns_of(a, cols):
    out = np.zeros((a.shape[0], len(cols)), np.float32)
    at = [i for i, c in enumerate(cols) if c is not None]
    out[:, at] = a[:, [cols[i] for i in at]]
    return out


def _feature_major(v):
    v = v.reshape(-1, P)
    return v.transpose(1, 0)


def _twice(a):
    return np.concatenate([a, a], 0)


def lay_out_stream(x):
    slots, products, matrices, width = plan_stream()
    stream = np.zeros((P, width), np.float32)

    def put_product(name, w, tiles, rows=None):
        if rows is not None:
            w = w[rows]
        prod = products[name]
        for i, pair, k0, ks in prod["steps"]:
            cols = [c for j in pair for c in tiles[j]]
            part = _columns_of(w[k0 * P:(k0 + ks) * P], cols).reshape(ks, P, len(cols)).transpose(1, 0, 2)
            stream[:, slots[i]["at"]:slots[i]["at"] + slots[i]["width"]] = part.reshape(P, -1)

    def put_matrix(name, parts):
        at = slots[matrices[name]]["at"]
        for a in parts:
            a = a.reshape(a.shape[0], -1)
            stream[:a.shape[0], at:at + a.shape[1]] = a
            at += a.shape[1]

    small = []
    for l in range(DEPTH):
        put_product(f"in1_{l}", x["w_in"][l], nsa_gla_pool_tiles())
        for which in range(2):
            w1 = x["cmp_w1"][l, which].reshape(CMP_BLOCK, HD, HD).transpose(1, 0, 2)
            put_matrix(f"cmp_{l}_{which}", [_twice(w1)])
        wg = np.zeros((P, 2 * P), np.float32)
        wg[:16, :GLA_H * GLA_DK] = x["gla_w_gate2"][l]
        pw = x["pool_w"][l].reshape(2, 2, HD, HD).transpose(1, 2, 0, 3).reshape(P, 2 * HD)
        small += [_twice(x["cmp_w2"][l, 0]), _twice(x["cmp_w2"][l, 1]), wg, pw]
        put_product(f"out1_{l}", x["w_out"][l], straight_tiles(KT), nsa_mix_rows())
        put_product(f"up1_{l}", x["w_up"][l], straight_tiles(FT1))
        put_product(f"down1_{l}", x["w_down"][l], straight_tiles(KT))
    put_product("in_g", x["l0_w_in_2"], griffin_tiles())
    put_matrix("lru", [x["l0_lru_w_a_2"].transpose(1, 0, 2), x["l0_lru_w_x_2"].transpose(1, 0, 2)])
    put_product("out_g", x["l0_w_out_2"], straight_tiles(KT), griffin_mix_rows())
    put_product("in_m", x["l1_w_in_2"], mamba_tiles())
    put_product("out_m", x["l1_w_out_2"], straight_tiles(KT))
    for l in range(2):
        put_product(f"up2_{l}", x[f"l{l}_ffn_w_up_2"], ffn2_up_tiles())
        put_product(f"down2_{l}", x[f"l{l}_ffn_w_down_2"], straight_tiles(KT))
    return stream, np.concatenate(small, 1)


def lay_out_parameters(x):
    par = np.zeros((P, PAR.n), np.float32)

    def put(name, a):
        a = a.reshape(a.shape[0], -1)
        par[:a.shape[0], PAR[name]:PAR[name] + a.shape[1]] = a

    for l in range(DEPTH):
        put(f"pos{l}", _twice(x["cmp_pos"][l].transpose(2, 0, 1)))
        bg = np.zeros(2 * P, np.float32)
        bg[:GLA_H * GLA_DK] = x["gla_b_gate"][l]
        put(f"b_gate{l}", _feature_major(bg))
        put(f"norm_g{l}", _feature_major(x["gla_norm_g"][l]))
        put(f"pool_scale{l}", _feature_major(x["pool_scale"][l]))
        for name in ("ln1_g", "ln1_b", "ln2_g", "ln2_b"):
            put(f"{name}{l}", _feature_major(x[name][l]))
    order = [c for t in ffn2_up_tiles() for c in t]
    for l in range(2):
        for name in ("mix_pre", "mix_post", "ffn_pre", "ffn_post"):
            put(f"{name}{l}", _feature_major(x[f"l{l}_{name}_norm_2"]))
        put(f"ffn_w{l}", _feature_major(x[f"l{l}_ffn_conv_w_2"][:, order]))
        put(f"ffn_b{l}", _feature_major(x[f"l{l}_ffn_conv_b_2"][order]))
    put("lru_w", _feature_major(x["l0_lru_conv_w_2"]))
    put("lru_b", _feature_major(x["l0_lru_conv_b_2"]))
    put("lru_ba", _feature_major(x["l0_lru_b_a_2"]))
    put("lru_bx", _feature_major(x["l0_lru_b_x_2"]))
    put("lru_lam", _feature_major(x["l0_lru_lambda_2"]))
    sinks = x["l0_attn_sinks_2"]
    put("sinks", np.broadcast_to(sinks[None, :], (P, 16)))
    put("sinks_last", np.repeat(sinks.reshape(2, SWA_J), META, axis=1).transpose(1, 0))
    put("ssm_w", _feature_major(x["l1_ssm_conv_w_2"]))
    put("ssm_b", _feature_major(x["l1_ssm_conv_b_2"]))
    put("dt_bias", x["l1_dt_bias_2"].reshape(-1, 1))
    put("a_log", x["l1_a_log_2"].reshape(-1, 1))
    put("d_skip", _feature_major(np.repeat(x["l1_d_skip_2"], HD)))
    put("gate_norm", _feature_major(x["l1_gate_norm_2"]))
    return par


def kernel(**inputs):
    import concourse.bacc as bacc
    from concourse.bass_utils import run_bass_kernel_spmd

    x = {name: np.asarray(a) for name, a in inputs.items()}
    feature_tiles = lambda a: np.ascontiguousarray(a.reshape(a.shape[0], KT, P).transpose(2, 1, 0))
    stream, small = lay_out_stream(x)
    arrays = {
        "stream": stream,
        "small": small,
        "params": lay_out_parameters(x),
        "consts": constants(),
        "x_t": feature_tiles(x["x"][0]),
        "meta_t": feature_tiles(x["meta_tokens_2"]),
    }
    nc = bacc.Bacc("TRN2", target_bir_lowering=False, num_devices=1)
    args = [nc.dram_tensor(n, a.shape, F32, kind="ExternalInput").ap() for n, a in arrays.items()]
    args.append(nc.dram_tensor("out_t", (P, KT, S), F32, kind="ExternalOutput").ap())
    two_stacks(nc, *args)
    r = run_bass_kernel_spmd(nc, [arrays], core_ids=[0])
    out = np.asarray(r.results[0]["out_t"])
    return np.ascontiguousarray(out.transpose(2, 1, 0).reshape(1, S, D))
```

```python
from contextlib import ExitStack

import numpy as np
import concourse.bass as bass
from concourse import mybir

P = 128
F32 = mybir.dt.float32
F16 = mybir.dt.float16
ALU = mybir.AluOpType
ACT = mybir.ActivationFunctionType
AX_X = mybir.AxisListType.X

D = 1024
KT = D // P
S = 256
DEPTH = 2
META = 16
T = S + META
HD = 64
NSA_J = 3
CMP_N, CMP_BLOCK, CMP_STRIDE = 15, 32, 16
GLA_H, GLA_DK, GLA_DV, GLA_C = 6, 32, 64, 64
D_FF = 4096
FT1 = D_FF // P
D_FF2 = 2816
FT2 = D_FF2 // P
SWA_J = 8
SWA_WINDOW = 128
SSM_TILES = 16
SSM_G = 8
SSM_HEADS = 32
CHUNKS = [(0, META), (META, P), (META + P, P)]
ALPHA = float((2 * DEPTH) ** 0.25)
LN_EPS, RMS_EPS = 1e-5, 1e-6
MASKED = -1.0e30
MAX_FLOOR = -1.0e29
SLOT = 2048
MISC = 512
RAW = 4
SPLIT = 4
W_SCALE = 256.0
GLA_BANKS = [4, 7, 2, 3]
GB = 4
BESIDE = {"in_z": (0, 1)}


def nsa_gla_pool_tiles():
    q0, kv0, gate0 = 0, 384, 384 + 768
    gq0 = gate0 + 18
    gk0, gv0 = gq0 + 192, gq0 + 384
    glr0 = gv0 + 384
    og0 = glr0 + 16
    pu0 = og0 + 384
    kv = lambda branch, which: [kv0 + (branch * 2 + which) * 128 + i for i in range(128)]
    q = lambda j: [q0 + (g * NSA_J + j) * HD + i for g in range(2) for i in range(HD)]
    run = lambda a, n: list(range(a, a + n))
    tiles = [kv(0, 0), kv(1, 0), kv(2, 0), q(0), q(1), q(2), kv(0, 1), kv(1, 1), kv(2, 1)]
    tiles.append(run(glr0, 16) + [None] * 16 + run(gate0, 18))
    tiles += [run(gq0, 128), run(gq0 + 128, 64) + [None] * 64, run(gk0, 128), run(gk0 + 128, 64) + [None] * 64]
    tiles += [run(gv0 + 128 * i, 128) for i in range(3)]
    tiles += [run(og0 + 128 * i, 128) for i in range(3)]
    tiles += [run(pu0 + 128 * i, 128) for i in range(2)]
    return tiles


T_KC, T_KS, T_KW, T_Q, T_VC, T_VS, T_VW, T_LR, T_GQ, T_GK, T_GV, T_OG, T_PU = 0, 1, 2, 3, 6, 7, 8, 9, 10, 12, 14, 17, 20
N_IN1 = 22


def griffin_tiles():
    run = lambda a, n: list(range(a, a + n))
    gate0, xr0, q0, k0, v0 = 0, D, 2 * D, 3 * D, 3 * D + 128
    tiles = [run(xr0 + 128 * i, 128) for i in range(8)]
    tiles += [run(gate0 + 128 * i, 128) for i in range(8)]
    tiles += [[q0 + (g * SWA_J + j) * HD + i for g in range(2) for i in range(HD)] for j in range(SWA_J)]
    return tiles + [run(k0, 128), run(v0, 128)]


def mamba_tiles():
    run = lambda a, n: list(range(a, a + n))
    z0, x0, b0, c0, dt0 = 0, 2048, 4096, 5120, 6144
    tiles = [run(dt0, 32)]
    tiles += [run(x0 + 128 * i, 128) for i in range(16)]
    tiles += [run(b0 + 128 * i, 128) for i in range(8)]
    tiles += [run(c0 + 128 * i, 128) for i in range(8)]
    return tiles


def gate_tiles():
    return straight_tiles(SSM_TILES)


def straight_tiles(n):
    return [list(range(P * i, P * i + P)) for i in range(n)]


def ffn2_up_tiles():
    out = []
    for i in range(FT2):
        out += [list(range(P * i, P * i + P)), list(range(D_FF2 + P * i, D_FF2 + P * i + P))]
    return out


def nsa_mix_rows():
    rows = [(g * NSA_J + j) * HD + i for j in range(NSA_J) for g in range(2) for i in range(HD)]
    return rows + list(range(384, 1024))


def griffin_mix_rows():
    rows = list(range(D))
    return rows + [D + (g * SWA_J + j) * HD + i for j in range(SWA_J) for g in range(2) for i in range(HD)]


def stream_items():
    items = []
    for l in range(DEPTH):
        items.append(("product", f"in1_{l}", KT, [len(t) for t in nsa_gla_pool_tiles()]))
        items.append(("matrix", f"cmp_{l}_0", 2048))
        items.append(("matrix", f"cmp_{l}_1", 2048))
        items.append(("product", f"out1_{l}", KT, [P] * KT))
        items.append(("product", f"up1_{l}", KT, [P] * FT1))
        items.append(("product", f"down1_{l}", FT1, [P] * KT))
    items.append(("product", "in_g", KT, [P] * 26))
    items.append(("matrix", "lru", 2048))
    items.append(("product", "out_g", 16, [P] * KT))
    items.append(("product", "up2_0", KT, [P] * (2 * FT2)))
    items.append(("product", "down2_0", FT2, [P] * KT))
    items.append(("product", "in_m", KT, [len(t) for t in mamba_tiles()]))
    items.append(("product", "in_z", KT, [P] * SSM_TILES))
    items.append(("product", "out_m", SSM_TILES, [P] * KT))
    items.append(("product", "up2_1", KT, [P] * (2 * FT2)))
    items.append(("product", "down2_1", FT2, [P] * KT))
    return items


def plan_stream():
    slots, products, matrices = [], {}, {}
    banks, nth, previous = [], [], []
    at, tile = 0, 0

    def slot(name, width, first_k=0, ks=0, tiles=()):
        nonlocal at
        slots.append(dict(name=name, at=at, width=width, first_k=first_k, ks=ks, tiles=tiles, release=None))
        at += width
        return len(slots) - 1

    for kind, name, *rest in stream_items():
        if kind == "matrix":
            matrices[name] = slot(name, rest[0])
            continue
        kt, widths = rest
        steps = []
        i = 0
        while i < len(widths):
            pair = [i]
            if i + 1 < len(widths):
                pair.append(i + 1)
            cols = sum(widths[j] for j in pair)
            for k0 in range(0, kt, 8):
                ks = min(8, kt - k0)
                steps.append((slot(name, ks * cols, k0, ks, tuple(pair)), pair, k0, ks))
            i += len(pair)
        products[name] = dict(first=tile, kt=kt, widths=widths, steps=steps)
        for j in range(len(widths)):
            beside = BESIDE.get(name, range(GB))
            bank = beside[j % len(beside)]
            before = [t for t, b in enumerate(banks) if b == bank]
            banks.append(bank)
            nth.append(len(before) + 1)
            previous.append(before[-1] if before else None)
        tile += len(widths)
    return slots, products, matrices, at, (banks, nth, previous)


class Columns:

    def __init__(self):
        self.n, self.at = 0, {}

    def add(self, name, width):
        self.at[name] = self.n
        self.n += width

    def __getitem__(self, name):
        return self.at[name]


def parameter_columns():
    c = Columns()
    for l in range(DEPTH):
        for name, w in (("pos", 64), ("b_gate", 2), ("norm_g", 3), ("pool_scale", 2),
                        ("ln1_g", 8), ("ln1_b", 8), ("ln2_g", 8), ("ln2_b", 8)):
            c.add(f"{name}{l}", w)
    for l in range(2):
        for name in ("mix_pre", "mix_post", "ffn_pre", "ffn_post"):
            c.add(f"{name}{l}", 8)
        c.add(f"ffn_w{l}", 3 * 2 * FT2)
        c.add(f"ffn_b{l}", 2 * FT2)
    c.add("lru_w", 32)
    for name in ("lru_b", "lru_ba", "lru_bx", "lru_lam"):
        c.add(name, 8)
    c.add("sinks", 16)
    c.add("sinks_last", 2)
    c.add("ssm_w", 4 * 32)
    c.add("ssm_b", 32)
    c.add("dt_bias", 1)
    c.add("a_log", 1)
    c.add("d_skip", 16)
    c.add("gate_norm", 16)
    return c


def constant_columns():
    c = Columns()
    for name, w in (("ident", P), ("mean", P), ("head_mean", P), ("rope_swap", P), ("cos", S), ("sin", S),
                    ("tri", P), ("cmp_mask", 12 * 16), ("pool_inv", 2 * S), ("gla_causal", P),
                    ("gla_reset", 2 * S), ("dist0", P), ("dist1", 2 * P), ("dist2", T), ("slope_last", 2),
                    ("ssd_reset", T), ("ssd_causal", P), ("eps", 2)):
        c.add(name, w)
    return c


PAR = parameter_columns()
CON = constant_columns()
SLOPES = [2.0 ** (-8.0 * (h + 1) / (2 * SWA_J)) for h in range(2 * SWA_J)]


def constants():
    c = np.zeros((P, CON.n), np.float32)

    def put(name, a):
        a = np.asarray(a, np.float32).reshape(a.shape[0], -1)
        c[:a.shape[0], CON[name]:CON[name] + a.shape[1]] = a

    put("ident", np.eye(P))
    put("mean", np.full((P, P), 1.0 / D))
    put("head_mean", np.kron(np.eye(2), np.full((HD, HD), 1.0 / GLA_DV)))
    half = HD // 8
    swap = np.zeros((P, P))
    for g in range(2):
        for i in range(half):
            swap[g * HD + half + i, g * HD + i] = 1.0
            swap[g * HD + i, g * HD + half + i] = 1.0
    put("rope_swap", swap)
    inv = np.float32(500000.0) ** (-np.arange(half, dtype=np.float32) * np.float32(2.0) / np.float32(2 * half))
    ang = np.arange(S, dtype=np.float32)[None, :] * inv.astype(np.float32)[:, None]
    cos, sin = np.ones((P, S), np.float32), np.zeros((P, S), np.float32)
    for g in range(2):
        b = g * HD
        cos[b:b + half] = cos[b + half:b + 2 * half] = np.cos(ang)
        sin[b:b + half] = -np.sin(ang)
        sin[b + half:b + 2 * half] = np.sin(ang)
    put("cos", cos)
    put("sin", sin)
    r = np.arange(P)
    put("tri", np.where(r[None, :] <= r[:, None], 0.0, MASKED))
    cm = np.full((P, 2, 2, 3, 16), MASKED)
    last = CMP_STRIDE * np.arange(CMP_N) + CMP_BLOCK - 1
    for ch in range(2):
        cm[:, :, ch, :, :CMP_N] = np.where(last[None, :] <= (ch * P + r)[:, None], 0.0, MASKED)[:, None, None, :]
    put("cmp_mask", cm)
    win = np.array([[2, 4], [8, 16]])
    t = np.arange(S)
    pi = np.zeros((P, 2, S))
    for i in range(2):
        for h in range(2):
            pi[h * HD:(h + 1) * HD, i] = 1.0 / np.minimum(t + 1, win[i, h]).astype(np.float32)
    put("pool_inv", pi)
    same = (r[:, None] // GLA_C) == (r[None, :] // GLA_C)
    put("gla_causal", np.where(same & (r[None, :] >= r[:, None]), 1.0, 0.0))
    put("gla_reset", np.tile(np.where(np.arange(2 * S) % GLA_C == 0, 0.0, 1.0), (P, 1)))
    far = 1.0e32

    def dist(tq, key):
        d = tq[:, None] - key[None, :]
        meta = key[None, :] < META
        ok = (d >= 0) & (meta | (d < SWA_WINDOW))
        return np.where(ok, np.where(meta, np.minimum(d, SWA_WINDOW), d), far)

    put("dist0", dist(r, r))
    put("dist1", dist(P + r, np.arange(2 * P)))
    put("dist2", dist(2 * P + np.tile(np.arange(META), SWA_J), np.arange(T)))
    put("slope_last", np.stack([-np.repeat([SLOPES[g * SWA_J + j] for j in range(SWA_J)], META) for g in range(2)], 1))
    reset = np.ones(T)
    reset[[t0 for t0, _ in CHUNKS]] = 0.0
    put("ssd_reset", np.tile(reset, (P, 1)))
    put("ssd_causal", np.where(r[None, :] >= r[:, None], 0.0, MASKED))
    put("eps", np.tile([LN_EPS, RMS_EPS], (P, 1)))
    return c


def two_stacks(nc, stream, small, params, consts, x_t, meta_t, out_t):
    slots, products, matrices, stream_width, (BANK, NTH, PREVIOUS) = plan_stream()

    freed = 0
    for s in slots:
        prod = products.get(s["name"])
        if prod and s["first_k"] + s["ks"] == prod["kt"]:
            s["release"] = ("tile", prod["first"] + s["tiles"][-1] + 1)
        else:
            freed += 1
            s["release"] = ("free", freed)

    with ExitStack() as ctx:
        def sb(name, cols):
            return ctx.enter_context(nc.sbuf_tensor(name, [P, cols], F32))[:, :]

        def sem(name):
            return ctx.enter_context(nc.semaphore(name))

        raw = sb("raw", RAW * SLOT)
        high = ctx.enter_context(nc.sbuf_tensor("high", [P, SPLIT * SLOT], F16))[:, :]
        low = ctx.enter_context(nc.sbuf_tensor("low", [P, SPLIT * SLOT], F16))[:, :]
        misc = sb("misc", DEPTH * MISC)
        par = sb("par", PAR.n)
        con = sb("con", CON.n)
        h_all = sb("h", KT * T).rearrange("p (k t) -> p k t", t=T)
        u_all = sb("u", KT * T).rearrange("p (k t) -> p k t", t=T)
        m_all = sb("m", KT * T).rearrange("p (k t) -> p k t", t=T)
        sq_all = sb("sq", KT * T).rearrange("p (k t) -> p k t", t=T)
        rstd = sb("rstd", T)
        lnv = sb("lnv", 48)
        root = sb("root", T)
        ARENA = 21900
        arena = sb("arena", ARENA)
        psum = ctx.enter_context(nc.psum_tensor("psum", [P, 8, 512], F32))

        def bank(b, lo=0, hi=512, rows=slice(0, P)):
            return psum[rows, b, lo:hi]

        def shaped(ap, *dims):
            if len(dims) == 1:
                return ap
            names = "abcd"[:len(dims)]
            return ap.rearrange(f"p ({' '.join(names)}) -> p {' '.join(names)}", **dict(zip(names, dims)))

        def carve(sizes):
            at, out = 0, []
            for dims in sizes:
                n = int(np.prod(dims))
                out.append(shaped(arena[:, at:at + n], *dims))
                at += n
            assert at <= ARENA, at
            return out

        def C(name, lo, hi, rows=slice(0, P)):
            return con[rows, CON[name] + lo:CON[name] + hi]

        def pcol(name, i, rows=slice(0, P)):
            return par[rows, PAR[name] + i:PAR[name] + i + 1]

        ident = C("ident", 0, P)
        h1 = h_all[:, :, META:T]
        eps_ln, eps_rms = C("eps", 0, 1), C("eps", 1, 2)

        def over(ap, n):
            return ap.unsqueeze(1).to_broadcast([ap.shape[0], n] + list(ap.shape[1:]))

        def along(ap, n):
            return ap.unsqueeze(len(ap.shape)).to_broadcast(list(ap.shape) + [n])

        (p1, rope_cos, roped, tb, hid, kc, vc, v_tok, gv_tok, gates_t, sc, sc_s, e_at, pt_at, ptc, nm, gk_x, gk_l, bc,
         ep, en, qd, kinv, kend, kend_tok, gmix) = carve([
             (N_IN1, S), (6, S), (6, S), (2, 32, 15), (2, 16), (16,), (2, HD), (4, P), (6, P), (2, 18), (12, 16), (5, 12),
             (2, 2, S), (2, 512), (12, P), (2, 8), (2 * S,), (2 * S,), (2 * S,),
             (2 * S,), (2 * S,), (2 * S,), (2 * S,), (2 * S,), (4, P), (KT, S)])
        def halves(region, *dims):
            n = int(np.prod(dims))
            flat16 = region.bitcast(F16)
            return shaped(flat16[:, 0:n], *dims), shaped(flat16[:, n:2 * n], *dims)

        at_gla = shaped(sq_all.rearrange("p k t -> p (k t)")[:, 0:2048], 4, 4, P)
        flat3 = lambda a: a.rearrange("p a b -> p (a b)")
        x_hi, x_lo = halves(flat3(u_all), KT, T)
        s_gla = shaped(flat3(rope_cos)[:, 0:384], 3, 2, HD)
        o_sq = shaped(flat3(rope_cos)[:, 384:384 + 768], 3, S)
        o_rs = p1[:, 0:3, :]
        tb_parts = shaped(e_at.rearrange("p a b c -> p (a b c)")[:, 0:960].bitcast(F16), 2, 2, 32, 15)
        tb_hi, tb_lo = halves(e_at.rearrange("p a b c -> p (a b c)")[:, 0:960], 2, 32, 15)
        m_flat = m_all.rearrange("p k t -> p (k t)")
        pool_u = shaped(m_flat[:, 0:544], 2, 272)
        pool_a = shaped(m_flat[:, 544:1088], 2, 272)
        pool_b = shaped(m_flat[:, 1088:1632], 2, 272)
        pool_d = shaped(m_flat[:, 1632:2144], 2, S)
        og_silu = roped[:, 0:3, :]
        ff1, f_relu, f_sq = carve([(FT1, S), (4, S), (2, S)])
        f1_hi, f1_lo = halves(flat3(ff1), FT1, S)
        (xr, gg, qt, kv_t, rg, ig, la, a_sc, th, gmix_a, v_swa) = carve(
            [(8, T), (8, T), (8, T), (3, T), (8, T), (8, T), (8, T), (8, T), (8, T), (8, T), (3, P)])
        xr_hi, xr_lo = halves(flat3(th), 8, T)
        ya_hi, ya_lo = halves(flat3(xr), 8, T)
        yb_hi, yb_lo = halves(flat3(gg), 8, T)
        gmix_b = rg
        s_at = [shaped(ig.rearrange("p k t -> p (k t)")[:, 0:1024], 4, S), shaped(ig.rearrange("p k t -> p (k t)")[:, 1024:2048], 4, S)]
        pt_sw = shaped(la.rearrange("p k t -> p (k t)")[:, 0:2048], 4, 512)
        sm = shaped(th.rearrange("p k t -> p (k t)")[:, 0:96], 2, 6, 8)
        ff2, cg, cu, f_prod = carve([(FT2, T), (2, T), (2, T), (2, T)])
        f2_hi, f2_lo = halves(flat3(ff2), FT2, T)
        (xbc, z_t, b_tok, prev, seg, e2, cd, dtt, dts, y_rs, aneg) = carve(
            [(32, T), (SSM_TILES, T), (SSM_G, P), (2048,), (2, 4, P), (2, 4, P), (2, 4, P), (3, 3, 32), (6, T), (2, T), (2,)])
        ym_hi, ym_lo = halves(flat3(z_t), SSM_TILES, T)
        xdt = m_flat[:, 0:2048]
        groups = lambda buf: shaped(buf.rearrange("p a b c -> p (a b c)")[:, 0:SSM_G * 4 * META], SSM_G, 4, META)
        seg_all = groups(seg)
        at_seg = 32 * T + SSM_TILES * T + SSM_G * P + 2048
        g_rs = shaped(arena[:, at_seg:at_seg + SSM_G * T], SSM_G, T)
        cs_diag = flat3(y_rs)[0:32, 0:SSM_G * 4 * META]
        xw = sq_all.rearrange("p k t -> p (k t)")[:, 0:2048]

        def gla_out(buf, q):
            rows = slice(64 * (q % 2), 64 * (q % 2) + 64)
            if q < 2:
                return buf[rows, 0:3:2, :], shaped(bank(GLA_BANKS[q], rows=rows), 2, S)
            return buf[rows, 1, :], bank(GLA_BANKS[q], 0, S, rows)

        slot_full = [sem(f"slot_full{i}") for i in range(RAW)]
        high_ready, split_ready = sem("high_ready"), sem("split_ready")
        xh_ready, x_ready = sem("xh_ready"), sem("x_ready")
        fh_ready, params_scaled = sem("fh_ready"), sem("params_scaled")
        ya_high, y_split, xr_high, xr_split, tb_high, tb_split = sem("ya_high"), sem("y_split"), sem("xr_high"), sem("xr_split"), sem("tb_high"), sem("tb_split")
        ym_high, m_scaled, zy_normed = sem("ym_high"), sem("m_scaled"), sem("zy_normed")
        slot_free = sem("slot_free")
        tile_done = sem("tile_done")
        evacuated = [sem(f"evacuated{i}") for i in range(GB)]
        tables_in, x_in = sem("tables_in"), sem("x_in")
        out_stored = sem("out_stored")
        act_chain, dve_chain, pool_chain = sem("act_chain"), sem("dve_chain"), sem("pool_chain")
        sq_ready, sums_done, root_ready = sem("sq_ready"), sem("sums_done"), sem("root_ready")
        mean_done, centred, ln_scaled, h_ready = sem("mean_done"), sem("centred"), sem("ln_scaled"), sem("h_ready")
        u_ready, h2_ready, first_out = sem("u_ready"), sem("h2_ready"), sem("first_out")
        rope_done, cos_ready, roped_ready = sem("rope_done"), sem("cos_ready"), sem("roped_ready")
        tb_ready, hid_done, hid_ready, kcvc_done, kcvc_ready = sem("tb_ready"), sem("hid_done"), sem("hid_ready"), sem("kcvc_done"), sem("kcvc_ready")
        gate_sig, v_turned, gv_turned, gates_turned, toks_ready = sem("gate_sig"), sem("v_turned"), sem("gv_turned"), sem("gates_turned"), sem("toks_ready")
        cmp_scored, cmp_shifted, cmp_exped, cmp_ready, cmp_turned, ptc_ready = (
            sem("cmp_scored"), sem("cmp_shifted"), sem("cmp_exped"), sem("cmp_ready"), sem("cmp_turned"), sem("ptc_ready"))
        scores_done, scores_max, attn_exp, attn_p, p_turned, pt_ready, pv_done, mix_out = (
            sem("scores_done"), sem("scores_max"), sem("attn_exp"), sem("attn_p"), sem("p_turned"), sem("pt_ready"), sem("pv_done"), sem("mix_out"))
        gk_done, gk_biased, gk_logged, bcum_ready, decays_ready, gla_in, kend_ready = (
            sem("gk_done"), sem("gk_biased"), sem("gk_logged"), sem("bcum_ready"), sem("decays_ready"), sem("gla_in"), sem("kend_ready"))
        kend_turned, kend_tok_ready, a_done, a_masked, ds_done, s_ready, o_done, o_squared, o_sums, o_rstd, gla_mixed = (
            sem("kend_turned"), sem("kend_tok_ready"), sem("a_done"), sem("a_masked"), sem("ds_done"), sem("s_ready"),
            sem("o_done"), sem("o_squared"), sem("o_sums"), sem("o_rstd"), sem("gla_mixed"))
        pool_in, pooled, pool_done, pool_mixed = sem("pool_in"), sem("pooled"), sem("pool_done"), sem("pool_mixed")
        relu_ready, f_ready = sem("relu_ready"), sem("f_ready")
        conv_acc, conv_done, conv_act = sem("conv_acc"), sem("conv_done"), sem("conv_act")
        lru_softplus, ssd_end, gates_act = sem("lru_softplus"), sem("ssd_end"), sem("gates_act")
        diag_ready, hid_summed, og_read = sem("diag_ready"), sem("hid_summed"), sem("og_read")
        lru_done, lru_gated, lru_log, lru_exp, lru_root, lru_a2, lru_out = (
            sem("lru_done"), sem("lru_gated"), sem("lru_log"), sem("lru_exp"), sem("lru_root"), sem("lru_a2"), sem("lru_out"))
        v2_turned, v2_ready = sem("v2_turned"), sem("v2_ready")
        sw_scored, sw_max, sw_exp, sw_p, sw_turned, sw_pt, sw_pv, sw_out = (
            sem("sw_scored"), sem("sw_max"), sem("sw_exp"), sem("sw_p"), sem("sw_turned"), sem("sw_pt"), sem("sw_pv"), sem("sw_out"))
        dt_logged, cs_ready, dt_w, dtt_done, dtt_ready = (
            sem("dt_logged"), sem("cs_ready"), sem("dt_w"), sem("dtt_done"), sem("dtt_ready"))
        x_turned, xdt_ready, b_turned, b_ready = sem("x_turned"), sem("xdt_ready"), sem("b_turned"), sem("b_ready")
        cs_spread, seg_ready, ssd_exp, mt_ready, cd_ready, y_done, y_out, prev_ready, zy_ready, zy_sq, zy_sums, zy_rstd, y_ready = (
            sem("cs_spread"), sem("seg_ready"), sem("ssd_exp"), sem("mt_ready"), sem("cd_ready"), sem("y_done"), sem("y_out"),
            sem("prev_ready"), sem("zy_ready"), sem("zy_sq"), sem("zy_sums"), sem("zy_rstd"), sem("y_ready"))
        block = ctx.enter_context(nc.Block())

        class Tell:

            def __init__(self, eng, chain):
                self.eng, self.chain, self.counts, self.last = eng, chain, {}, None

            def __call__(self, ins, sem=None, value=None, n=1):
                sem = self.chain if sem is None else sem
                ins.then_inc(sem, n)
                self.counts[sem.name] = self.counts.get(sem.name, 0) + n
                self.last = (sem, self.counts[sem.name] if value is None else value)

            def settle(self):
                self.eng.wait_ge(*self.last)

        def evac_value(g):
            return evacuated[BANK[g]], NTH[g]

        def freed_by_pe(eng, i):
            if i >= 0:
                kind, n = slots[i]["release"]
                eng.wait_ge(tile_done if kind == "tile" else slot_free, n)

        def ready_steps(name):
            prod = products[name]
            for i, pair, k0, ks in prod["steps"]:
                yield i, pair if k0 + ks == prod["kt"] else []

        @block.sync
        def _(sp):
            def load(i):
                s = slots[i]
                sp.dma_start(raw[:, (i % RAW) * SLOT:(i % RAW) * SLOT + s["width"]],
                             stream[:, s["at"]:s["at"] + s["width"]]).then_inc(slot_full[i % RAW], 16)

            sp.dma_start(h1, x_t).then_inc(x_in, 16)
            load(0)
            load(1)
            sp.dma_start(h_all[:, :, 0:META], meta_t).then_inc(tables_in, 16)
            sp.dma_start(con, consts).then_inc(tables_in, 16)
            sp.dma_start(par, params).then_inc(tables_in, 16)
            sp.dma_start(misc, small).then_inc(tables_in, 16)
            for i in range(2, len(slots)):
                if i >= RAW:
                    sp.wait_ge(split_ready, i - RAW + 1)
                load(i)
            for k in range(0, KT, 2):
                sp.wait_ge(h2_ready, 8 * 3 + k + 2)
                sp.dma_start(out_t[:, k:k + 2, :], h1[:, k:k + 2, :]).then_inc(out_stored, 16)
            sp.wait_ge(out_stored, 16 * (KT // 2))

        @block.tensor
        def _(pe):
            def await_slot(i):
                pe.wait_ge(split_ready, i + 1)

            def split_matmul(out, i, lo, hi, x, start, stop, rows=slice(0, P)):
                at = (i % SPLIT) * SLOT
                w_hi, w_lo = high[rows, at + lo:at + hi], low[rows, at + lo:at + hi]
                pe.matmul(out, w_hi, x[0], start=start, stop=False)
                pe.matmul(out, w_hi, x[1], start=False, stop=False)
                return pe.matmul(out, w_lo, x[0], start=False, stop=stop)

            def bank_free(g):
                if PREVIOUS[g] is not None:
                    pe.wait_ge(*evac_value(PREVIOUS[g]))

            def tile(name, step, k, j, rhs, n):
                prod = products[name]
                slot, pair, k0, _ = step
                widths, g, w = prod["widths"], prod["first"] + j, prod["widths"][j]
                at = (k - k0) * sum(widths[t] for t in pair) + sum(widths[t] for t in pair if t < j)
                return split_matmul(bank(BANK[g], 0, n, slice(0, w)), slot, at, at + w, rhs(k), start=(k == 0), stop=(k == prod["kt"] - 1))

            def single_tile(name, j, rhs, n):
                step = products[name]["steps"][j // 2]
                await_slot(step[0])
                bank_free(products[name]["first"] + j)
                for k in range(KT):
                    mm = tile(name, step, k, j, rhs, n)
                mm.then_inc(tile_done, 1)

            def product(name, rhs, ready, n, after=None):
                prod = products[name]
                first, kt, steps = prod["first"], prod["kt"], prod["steps"]
                ahead = 2 if steps[0][3] == steps[1][3] == kt else 0
                for step in steps[:ahead]:
                    await_slot(step[0])
                    for j in step[1]:
                        bank_free(first + j)
                for k in range(kt if ahead else 0):
                    ready(k)
                    for step in steps[:ahead]:
                        for j in step[1]:
                            mm = tile(name, step, k, j, rhs, n)
                            if k == kt - 1:
                                mm.then_inc(tile_done, 1)
                if ahead and after:
                    for step in steps[:ahead]:
                        for j in step[1]:
                            after(j)

                for step in steps[ahead:]:
                    i, pair, k0, ks = step
                    await_slot(i)
                    for j in pair:
                        if k0 == 0:
                            bank_free(first + j)
                        for k in range(k0, k0 + ks):
                            if j == 0:
                                ready(k)
                            mm = tile(name, step, k, j, rhs, n)
                        if k == kt - 1:
                            mm.then_inc(tile_done, 1)
                        elif j == pair[-1]:
                            mm.then_inc(slot_free, 1)
                        if after and k == kt - 1:
                            after(j)

            def sum_squares(norm, k, n):
                pe.wait_ge(sq_ready, 8 * norm + k + 1)
                mm = pe.matmul(bank(4, 0, n), C("mean", 0, P), sq_all[:, k, 0:n], start=(k == 0), stop=(k == KT - 1))
                if k == KT - 1:
                    mm.then_inc(sums_done, 1)

            def layer_norm(name, m):
                first = products[name]["first"]

                def mean(k):
                    pe.wait_ge(*evac_value(first + k))
                    mm = pe.matmul(bank(5, 0, S), C("mean", 0, P), m_all[:, k, 0:S], start=(k == 0), stop=(k == KT - 1))
                    if k == KT - 1:
                        mm.then_inc(mean_done, 1)

                def finish():
                    mean(KT - 1)
                    for k in range(KT):
                        sum_squares(m, k, S)

                return (lambda j: mean(j - 1) if j else None), finish

            def first_layer(l):
                first = products[f"in1_{l}"]["first"]

                def small_at(lo, hi, rows):
                    return misc[rows, MISC * l + lo:MISC * l + hi]

                def evac_wait(t):
                    pe.wait_ge(*evac_value(first + t))

                def x_at(k):
                    return x_hi[:, k, 0:S], x_lo[:, k, 0:S]

                def rope():
                    evac_wait(5)
                    pe.wait_ge(tables_in, 64)
                    for i in range(3):
                        pe.matmul(bank(4 + i), C("rope_swap", 0, P), p1[:, 2 * i:2 * i + 2, :], start=True,
                                  stop=True).then_inc(rope_done, 1)

                product(f"in1_{l}", x_at, operand_ready(3 * l), S, lambda j: rope() if j == 7 else None)

                evac_wait(T_LR)
                for i in range(2):
                    mm = pe.matmul(bank(7, i * S, i * S + S), small_at(P + P * i, 2 * P + P * i, slice(0, 16)),
                                   p1[0:16, T_LR, :], start=True, stop=True)
                mm.then_inc(gk_done, 1)
                evac_wait(N_IN1 - 1)
                evac_wait(N_IN1 - 2)
                evac_wait(N_IN1 - 3)
                evac_wait(N_IN1 - 4)
                for b in range(2):
                    for c in range(2):
                        n = 2 * b + c
                        mm = pe.transpose(bank(0, n * P, n * P + P), p1[:, T_VS + b, c * P:c * P + P], ident)
                mm.then_inc(v_turned, 1)
                for i in range(3):
                    for c in range(2):
                        n = 2 * i + c
                        mm = pe.transpose(bank(1 + n // 4, (n % 4) * P, (n % 4) * P + P), p1[:, T_GV + i, c * P:c * P + P], ident)
                mm.then_inc(gv_turned, 1)
                pe.wait_ge(roped_ready, 3 * l + 3)
                for which in range(2):
                    w1 = matrices[f"cmp_{l}_{which}"]
                    await_slot(w1)
                    pe.wait_ge(tb_split, l + 1)
                    for j in range(CMP_BLOCK):
                        for g in range(2):
                            r = slice(g * HD, g * HD + HD)
                            at = (w1 % SPLIT) * SLOT + j * HD
                            pe.matmul(shaped(bank(4 + g, 32 * which, 32 * which + 2 * CMP_N, r), 2, CMP_N), high[r, at:at + HD],
                                      tb_parts[r, :, which, j, :], start=(j == 0), stop=False)
                            mm = pe.matmul(bank(4 + g, 32 * which, 32 * which + CMP_N, r), low[r, at:at + HD], tb_hi[r, which, j, :],
                                           start=False, stop=(j == CMP_BLOCK - 1))
                    mm.then_inc(slot_free, 1)
                pe.matmul(bank(6, 0, 1), ident, C("eps", 0, 1), start=True, stop=True).then_inc(hid_done, 1)
                pe.wait_ge(gate_sig, l + 1)
                for c in range(2):
                    mm = pe.transpose(bank(3, c * 18, c * 18 + 18), p1[32:50, T_LR, c * P:c * P + P], C("ident", 32, 50, slice(32, 50)))
                mm.then_inc(gates_turned, 1)
                pe.wait_ge(hid_ready, l + 1)
                pe.wait_ge(gk_biased, l + 1)
                for g in range(2):
                    r = slice(g * HD, g * HD + HD)
                    pe.matmul(bank(6 + g, 0, CMP_N, r), small_at(0, HD, r), hid[r, 0, 0:CMP_N], start=True, stop=True)
                    mm = pe.matmul(bank(6 + g, 64, 64 + HD, slice(0, CMP_N)), hid[r, 1, 0:CMP_N], small_at(HD, 2 * HD, r),
                                   start=True, stop=True)
                mm.then_inc(kcvc_done, 1)

                pe.wait_ge(kcvc_ready, l + 1)
                for g in range(2):
                    r = slice(g * HD, g * HD + HD)
                    for c in range(2):
                        for j in range(NSA_J):
                            at = (c * NSA_J + j) * 16
                            mm = pe.matmul(bank(4 + g, at, at + CMP_N), roped[r, T_Q + j, c * P:c * P + P], kc[r, 0:CMP_N],
                                           start=True, stop=True)
                mm.then_inc(cmp_scored, 1)
                pe.wait_ge(cmp_ready, l + 1)
                pe.wait_ge(toks_ready, l + 1)
                for n in range(12):
                    mm = pe.transpose(bank(n // 4, (n % 4) * P, (n % 4) * P + P, slice(0, CMP_N)), sc[:, n, 0:CMP_N], ident)
                mm.then_inc(cmp_turned, 1)

                units = [(c, j, g) for c in range(2) for j in range(NSA_J) for g in range(2)]
                base = 12 * l

                def scores(u):
                    c, j, g = units[u]
                    r, nk = slice(g * HD, g * HD + HD), (c + 1) * P
                    if u >= 2:
                        pe.wait_ge(attn_exp, base + u - 1)
                    for b in range(2):
                        mm = pe.matmul(bank(6 + u % 2, b * nk, b * nk + nk), roped[r, T_Q + j, c * P:c * P + P],
                                       roped[r, T_KS + b, 0:nk], start=True, stop=True)
                    mm.then_inc(scores_done, 1)

                def turn(u):
                    c, j, g = units[u]
                    pe.wait_ge(attn_p, base + u + 1)
                    if u >= 2:
                        pe.wait_ge(pt_ready, base + u - 1)
                    else:
                        pe.wait_ge(ptc_ready, l + 1)
                    for b in range(2):
                        for k in range(c + 1):
                            n = b * (c + 1) + k
                            mm = pe.transpose(bank(u % 2, n * P, n * P + P), e_at[:, u % 2, b, k * P:k * P + P], ident)
                    mm.then_inc(p_turned, 1)

                def values(u):
                    c, j, g = units[u]
                    r = slice(g * HD, g * HD + HD)
                    pe.wait_ge(pt_ready, base + u + 1)
                    if u >= 2:
                        pe.wait_ge(mix_out, base + u - 1)
                    out = bank(2 + u % 2, 0, P, r)
                    pe.matmul(out, vc[0:CMP_N, g, :], ptc[0:CMP_N, (g * 2 + c) * NSA_J + j, :], start=True, stop=False)
                    for b in range(2):
                        for k in range(c + 1):
                            n = b * (c + 1) + k
                            last = b == 1 and k == c
                            mm = pe.matmul(out, v_tok[:, 2 * b + k, g * HD:g * HD + HD], pt_at[:, u % 2, n * P:n * P + P],
                                           start=False, stop=last)
                    mm.then_inc(pv_done, 1)

                for u in range(14):
                    if u < 12:
                        scores(u)
                    if 1 <= u < 13:
                        turn(u - 1)
                    if u >= 2:
                        values(u - 2)

                pe.wait_ge(kend_ready, l + 1)
                pe.wait_ge(cmp_shifted, l + 1)
                for i in range(2):
                    for c in range(2):
                        n = 2 * i + c
                        mm = pe.transpose(bank(4, n * P, n * P + P), shaped(kend, 2, S)[:, i, c * P:c * P + P], ident)
                mm.then_inc(kend_turned, 1)
                pe.wait_ge(gla_in, l + 1)
                pe.wait_ge(mix_out, base + 12)
                for h in range(GLA_H):
                    r, i = slice(32 * (h % 4), 32 * (h % 4) + 32), h // 4
                    for c in range(2):
                        n = 2 * i + c
                        mm = pe.matmul(bank(h % 4, n * P, n * P + P), shaped(kinv, 2, S)[r, i, c * P:c * P + P],
                                       shaped(qd, 2, S)[r, i, c * P:c * P + P], start=True, stop=True)
                mm.then_inc(a_done, 1)
                pe.wait_ge(kend_tok_ready, l + 1)
                pe.wait_ge(attn_exp, base + 12)
                for n in range(3):
                    t = slice(64 * (n % 2), 64 * (n % 2) + 64)
                    for h in range(GLA_H):
                        i = h // 4
                        r = slice(32 * (h % 4), 32 * (h % 4) + 32)
                        at = (n // 2) * P + i * HD
                        mm = pe.matmul(bank(5 + n % 2, at, at + HD, r), kend_tok[t, 2 * i + n // 2, r],
                                       gv_tok[t, 2 * (h // 2) + n // 2, 64 * (h % 2):64 * (h % 2) + 64], start=True, stop=True)
                mm.then_inc(ds_done, 1)
                pe.wait_ge(a_masked, l + 1)
                pe.wait_ge(s_ready, l + 1)
                for h in range(GLA_H):
                    r, i, m = slice(32 * (h % 4), 32 * (h % 4) + 32), h // 4, h // 2
                    o = slice(64 * (h % 2), 64 * (h % 2) + 64)
                    b, at = GLA_BANKS[h % 4], i * S
                    for c in range(2):
                        pe.matmul(bank(b, at + c * P, at + c * P + P, o), gv_tok[:, 2 * m + c, o],
                                  at_gla[:, h % 4, 2 * i + c, :], start=True, stop=False)
                        for n in range(max(1, 2 * c), 2 * c + 2):
                            mm = pe.matmul(bank(b, at + n * 64, at + n * 64 + 64, o), s_gla[r, n - 1, i, :],
                                           shaped(qd, 2, S)[r, i, n * 64:n * 64 + 64], start=False, stop=(n == 2 * c + 1))
                mm.then_inc(o_done, 1)
                pe.wait_ge(pooled, l + 1)
                for g in range(4):
                    r = slice(64 * (g % 2), 64 * (g % 2) + 64)
                    mm = pe.matmul(bank(g % 2, (g // 2) * S, (g // 2) * S + S, r),
                                   small_at(384 + (g // 2) * HD, 384 + (g // 2) * HD + HD, r), pool_d[r, g // 2, :],
                                   start=True, stop=True)
                mm.then_inc(pool_done, 1)
                pe.wait_ge(o_squared, l + 1)
                pe.matmul(bank(5), C("head_mean", 0, P), o_sq[:, 0:2, :], start=True, stop=True)
                pe.matmul(bank(6, 0, S), C("head_mean", 0, P), o_sq[:, 2, :], start=True, stop=True).then_inc(o_sums, 1)

                pe.wait_ge(pool_mixed, 4 * l + 4)
                pe.wait_ge(og_read, l + 1)
                mean, finish = layer_norm(f"out1_{l}", 2 * l)
                product(f"out1_{l}", x_at, operand_ready(3 * l + 1), S, mean)
                finish()
                product(f"up1_{l}", x_at, operand_ready(3 * l + 2), S)
                mean, finish = layer_norm(f"down1_{l}", 2 * l + 1)
                product(f"down1_{l}", lambda k: (f1_hi[:, k, :], f1_lo[:, k, :]), lambda k: pe.wait_ge(f_ready, FT1 * l + k + 1), S, mean)
                finish()

            def behind(n):
                return lambda j: sum_squares(4 + n, j - 1, T) if j else None

            def pre_norm(n):
                for k in range(KT):
                    sum_squares(4 + n, k, T)

            def post_norm(n):
                sum_squares(4 + n, KT - 1, T)

            def x_at(k):
                return x_hi[:, k, :], x_lo[:, k, :]

            def operand_ready(p):
                return lambda k: pe.wait_ge(x_ready, 8 * p + k + 1)

            def second_ffn(l):
                product(f"up2_{l}", x_at, operand_ready(7 + 2 * l), T)
                product(f"down2_{l}", lambda k: (f2_hi[:, k, :], f2_lo[:, k, :]), lambda k: pe.wait_ge(f_ready, 2 * FT1 + FT2 * l + k + 1), T, behind(3 + 4 * l))

            def griffin():
                product("in_g", x_at, operand_ready(6), T)
                first = products["in_g"]["first"]
                w = matrices["lru"]
                await_slot(w)
                pe.wait_ge(xr_split, 1)
                for n in range(16):
                    if n >= 4:
                        pe.wait_ge(lru_gated, n - 3)
                    split_matmul(bank(4 + n % 4, 0, T), w, n * P, n * P + P, (xr_hi[:, n % 8, :], xr_lo[:, n % 8, :]), True,
                                 True).then_inc(lru_done, 1)
                for t in range(GB):
                    pe.wait_ge(*evac_value(first + 25 - t))
                for c in range(3):
                    n = min(P, T - c * P)
                    mm = pe.transpose(bank(0, c * P, c * P + P, slice(0, n)), kv_t[:, 1, c * P:c * P + n], ident)
                mm.then_inc(v2_turned, 1)
                pe.matmul(bank(1, 0, 1), ident, C("eps", 0, 1), start=True, stop=True).then_inc(slot_free, 1)
                for b, (c, g, half) in enumerate(SWA_BATCHES):
                    r = slice(g * HD, g * HD + HD)
                    nk = SWA_KEYS[c]
                    if b >= 2:
                        pe.wait_ge(sw_max, b - 1)
                    else:
                        pe.wait_ge(lru_gated, 16)
                    s0 = 4 + 2 * (b % 2)
                    for j in range(4 if c < 2 else 1):
                        if c < 2:
                            lhs = qt[r, 4 * half + j, c * P:c * P + P]
                            per = 512 // nk
                            out = bank(s0 + j // per, (j % per) * nk, (j % per) * nk + nk)
                        else:
                            lhs = kv_t[r, 2, 0:P]
                            out = bank(s0, 0, nk)
                        mm = pe.matmul(out, lhs, kv_t[r, 0, 0:nk], start=True, stop=True)
                    mm.then_inc(sw_scored, 1)
                    if b >= 1:
                        swa_values(b - 1)
                swa_values(len(SWA_BATCHES) - 1)

                pe.wait_ge(sw_out, len(SWA_BATCHES))

                def mixed_at(k):
                    return (ya_hi[:, k, :], ya_lo[:, k, :]) if k < 8 else (yb_hi[:, k - 8, :], yb_lo[:, k - 8, :])

                product("out_g", mixed_at, lambda k: pe.wait_ge(y_split, 1 + k // 8), T, behind(1))

            def swa_values(b):
                c, g, half = SWA_BATCHES[b]
                nk = SWA_KEYS[c]
                chunks = [(k * P, min(P, nk - k * P)) for k in range((nk + P - 1) // P)]
                heads = 4 if c < 2 else 1
                pe.wait_ge(sw_p, b + 1)
                if b >= 1:
                    pe.wait_ge(sw_pt, b)
                else:
                    pe.wait_ge(v2_ready, 1)
                for k, (k0, kn) in enumerate(chunks):
                    for j in range(heads):
                        mm = pe.transpose(bank(1 + k, j * P, j * P + P, slice(0, kn)), s_at[b % 2][:, j, k0:k0 + kn] if c < 2
                                          else s_at[b % 2].rearrange("p a b -> p (a b)")[:, k0:k0 + kn], ident)
                mm.then_inc(sw_turned, 1)
                pe.wait_ge(sw_pt, b + 1)
                if b >= 1:
                    pe.wait_ge(sw_out, b)
                for k, (k0, kn) in enumerate(chunks):
                    mm = pe.matmul(bank(0, 0, heads * P, slice(g * HD, g * HD + HD)), v_swa[0:kn, k, g * HD:g * HD + HD],
                                   pt_sw[0:kn, k, 0:heads * P], start=(k == 0), stop=(k == len(chunks) - 1))
                mm.then_inc(sw_pv, 1)

            def first_chunk():
                n = META
                for g in range(SSM_G):
                    pe.matmul(bank(3, g * n, g * n + n, slice(0, n)), xbc[:, 16 + g, 0:n], xbc[:, 24 + g, 0:n], start=True, stop=True)
                pe.wait_ge(diag_ready, 1)
                pe.matmul(bank(2), C("mean", 0, P, slice(0, 32)), cs_diag, start=True, stop=True).then_inc(cs_spread, SSM_G)
                pe.wait_ge(mt_ready, SSM_G)
                for head in range(4 * SSM_G):
                    g, h = divmod(head, 4)
                    pe.matmul(bank(4, head // 2 * n, head // 2 * n + n, slice(64 * (h % 2), 64 * (h % 2) + 64)),
                              xdt[0:n, head * HD:head * HD + HD], seg_all[0:n, g, h, :], start=True, stop=True)
                for g in range(SSM_G):
                    mm = pe.matmul(bank((5, 6, 7, 2)[g // 2], 256 * (g % 2), 256 * (g % 2) + 256), b_tok[0:n, g, :],
                                   xw[0:n, g * 256:g * 256 + 256], start=True, stop=True)
                mm.then_inc(y_done, SSM_G)

            def mamba():
                product("in_m", x_at, operand_ready(8), T)
                first = products["in_m"]["first"]
                for j in range(2):
                    single_tile("in_z", j, x_at, T)
                for t in range(GB):
                    pe.wait_ge(*evac_value(first + 32 - t))
                pe.wait_ge(dt_w, 1)
                for ci, (t0, n) in enumerate(CHUNKS):
                    for v in range(3):
                        at = (3 * ci + v) * 32
                        mm = pe.transpose(bank(7, at, at + 32, slice(0, n)), dts[0:32, v, t0:t0 + n], C("ident", 0, 32, slice(0, 32)))
                mm.then_inc(dtt_done, 1)
                pe.wait_ge(conv_act, FT2 + 32)
                for ci, (t0, n) in enumerate(CHUNKS):
                    if ci == 0:
                        pe.wait_ge(dtt_ready, 1)
                    else:
                        pe.wait_ge(y_out, 8 * ci)
                    for i in range(4):
                        for t in range(4):
                            mm = pe.transpose(bank(4 + i, t * P, t * P + P, slice(0, n)), xbc[:, 4 * i + t, t0:t0 + n], ident)
                        mm.then_inc(x_turned, 1)
                    if ci < 2:
                        for g in range(SSM_G):
                            mm = pe.transpose(bank(2 + g // 4, (g % 4) * P, (g % 4) * P + P, slice(0, n)), xbc[:, 16 + g, t0:t0 + n], ident)
                        mm.then_inc(b_turned, 1)
                        pe.wait_ge(b_ready, ci + 1)
                    else:
                        for j in (8, 9):
                            single_tile("in_z", j, x_at, T)
                    pe.wait_ge(xdt_ready, ci + 1)
                    if ci == 0:
                        first_chunk()
                        continue

                    def spread(g):
                        q = 8 * ci + g
                        if g >= 2:
                            pe.wait_ge(y_out, q - 1)
                        pe.matmul(bank(4 + q % 2, 256, 256 + n, slice(0, n)), xbc[:, 16 + g, t0:t0 + n], xbc[:, 24 + g, t0:t0 + n], start=True, stop=True)
                        for h in range(4):
                            mm = pe.matmul(bank(2 + q % 2, h * n, h * n + n), C("ident", 4 * g + h, 4 * g + h + 1, slice(0, 32)).to_broadcast([32, P]),
                                           dts[0:32, 1, t0:t0 + n], start=True, stop=True)
                        mm.then_inc(cs_spread, 1)

                    def outputs(g):
                        q = 8 * ci + g
                        pe.wait_ge(mt_ready, q + 1)
                        if ci:
                            pe.wait_ge(cd_ready, q - 8 + 1)
                        for h in range(4):
                            o = slice(64 * (h % 2), 64 * (h % 2) + 64)
                            head = 4 * g + h
                            out = bank(4 + q % 2, (h // 2) * n, (h // 2) * n + n, o)
                            mm = pe.matmul(out, xdt[0:n, head * HD:head * HD + HD], seg[0:n, q % 2, h, 0:n], start=True, stop=(ci == 0))
                            if ci:
                                mm = pe.matmul(out, prev[:, head * HD:head * HD + HD], cd[:, q % 2, h, 0:n], start=False, stop=True)
                        if ci < 2:
                            mm = pe.matmul(bank(6 + q % 2, 0, 256), b_tok[0:n, g, :], xw[0:n, g * 256:g * 256 + 256], start=True, stop=True)
                        mm.then_inc(y_done, 1)

                    for g in range(9):
                        if g < 8:
                            spread(g)
                        if g:
                            outputs(g - 1)
                        if g in GATE_GROUPS:
                            single_tile("in_z", 8 * (ci - 1) + 1 + g, x_at, T)
                pe.wait_ge(y_out, 3 * SSM_G)
                for g in range(SSM_G):
                    pe.wait_ge(zy_sq, g + 1)
                    for i in range(2):
                        mm = pe.matmul(bank(g, 0, T), C("mean", 0, P), (u_all if g < 4 else m_all)[:, 2 * (g % 4) + i, :], start=(i == 0), stop=(i == 1))
                    mm.then_inc(zy_sums, 1)
                pe.wait_ge(zy_rstd, SSM_G // 2)
                product("out_m", lambda k: (ym_hi[:, k, :], ym_lo[:, k, :]), lambda k: pe.wait_ge(y_ready, k + 1), T, behind(5))

            for l in range(DEPTH):
                first_layer(l)
            pre_norm(0)
            griffin()
            post_norm(1)
            pre_norm(2)
            second_ffn(0)
            post_norm(3)
            pre_norm(4)
            mamba()
            post_norm(5)
            pre_norm(6)
            second_ffn(1)
            post_norm(7)

        @block.scalar
        def _(act):
            tell = Tell(act, act_chain)

            def done(g):
                act.wait_ge(tile_done, g + 1)

            def evacuate(dst, g, n, func=ACT.Copy, rows=slice(0, P), scale=1.0):
                done(g)
                tell(act.activation(dst, bank(BANK[g], 0, n, rows), func, scale=scale / W_SCALE), *evac_value(g))

            def high_part(i, half=None):
                if i >= len(slots):
                    return
                w, at, off = slots[i]["width"], (i % SPLIT) * SLOT, (i % RAW) * SLOT
                if half is not None:
                    w //= 2
                    at, off = at + half * w, off + half * w
                freed_by_pe(act, i - SPLIT)
                if i >= SPLIT:
                    act.wait_ge(split_ready, i - SPLIT + 1)
                act.wait_ge(slot_full[i % RAW], 16 * (i // RAW + 1))
                tell(act.activation(high[:, at:at + w], raw[:, off:off + w], ACT.Copy, scale=W_SCALE), high_ready if half != 0 else None)

            def product(name, evac, hold=False):
                for n, (i, tiles) in enumerate(ready_steps(name)):
                    for t in tiles:
                        evac(t)
                    if n == 1:
                        high_part(i - 1 + SPLIT)
                    if n and not (hold and i == products[name]["steps"][-1][0]):
                        high_part(i + SPLIT)
                return i + SPLIT

            def single_tile(name, j, dst, n):
                evacuate(dst, products[name]["first"] + j, n)
                if j:
                    high_part(products[name]["steps"][(j - 1) // 2][0] + SPLIT, (j - 1) % 2)

            def high_x(src, wait=None, tiles=range(KT)):
                for k in tiles:
                    if wait:
                        wait(k)
                    tell(act.activation(x_hi[:, k, 0:src.shape[2]], src[:, k, :], ACT.Copy), xh_ready)

            def warm_root(t):
                if t == KT - 2:
                    act.activation(lnv[:, 40:41], eps_rms, ACT.Sqrt)

            def root_of_mean(norm, n, eps):
                act.wait_ge(sums_done, norm + 1)
                tell(act.activation(root[:, 0:n], bank(4, 0, n), ACT.Sqrt, bias=eps), root_ready)

            def layer_norm(m, which, l):
                for k in range(0, KT, 2):
                    act.wait_ge(centred, 8 * m + k + 2)
                    tell(act.activation(sq_all[:, k:k + 2, 0:S], m_all[:, k:k + 2, 0:S], ACT.Square), sq_ready, n=2)
                root_of_mean(m, S, eps_ln)
                for k in range(KT):
                    act.wait_ge(ln_scaled, 8 * m + k + 1)
                    if m == 2 * DEPTH - 1:
                        tell(act.activation(h1[:, k, :], m_all[:, k, 0:S], ACT.Identity, bias=pcol(f"ln{which}_b{l}", k)), first_out)
                        continue
                    tell(act.activation(x_hi[:, k, 0:S], m_all[:, k, 0:S], ACT.Identity, bias=pcol(f"ln{which}_b{l}", k)), xh_ready)

            def first_layer(l):
                first = products[f"in1_{l}"]["first"]
                widths = products[f"in1_{l}"]["widths"]

                def evac(t):
                    rows = slice(0, widths[t])
                    if t == 14:
                        act.wait_ge(tb_ready, 2 * l + 2)
                        tell(act.activation(tb_hi, tb, ACT.Copy), tb_high)
                    if T_Q <= t < T_Q + NSA_J:
                        evacuate(p1[:, t, :], first + t, S, scale=float(HD) ** -0.5)
                    elif t >= T_PU:
                        if t == T_PU:
                            act.wait_ge(pool_in, l + 1)
                        evacuate(pool_u[:, t - T_PU, 16:272], first + t, S)
                    else:
                        evacuate(p1[rows, t, :], first + t, S, rows=rows)

                product(f"in1_{l}", evac)
                tell.settle()
                tell(act.activation(p1[32:50, T_LR, :], p1[32:50, T_LR, :], ACT.Sigmoid), gate_sig)
                act.wait_ge(gk_biased, l + 1)
                tell(act.activation(gk_l, gk_x, ACT.Abs))
                tell.settle()
                tell(act.activation(gk_l, gk_l, ACT.Exp, scale=-1.0))
                tell.settle()
                tell(act.activation(gk_l, gk_l, ACT.Ln, bias=1.0), gk_logged)
                act.wait_ge(v_turned, l + 1)
                act.activation(v_tok, shaped(bank(0), 4, P), ACT.Copy)
                act.wait_ge(gv_turned, l + 1)
                act.activation(gv_tok[:, 0:4, :], shaped(bank(1), 4, P), ACT.Copy)
                act.activation(gv_tok[:, 4:6, :], shaped(bank(2, 0, 256), 2, P), ACT.Copy)
                act.wait_ge(bcum_ready, l + 1)
                act.activation(ep, bc, ACT.Exp, scale=1.0 / 16.0)
                act.activation(en, bc, ACT.Exp, scale=-1.0 / 16.0)
                tell(act.activation(gk_x, gk_l, ACT.Exp, scale=1.0 / 16.0), decays_ready)
                act.wait_ge(gates_turned, l + 1)
                tell(act.activation(gates_t, shaped(bank(3, 0, 36), 2, 18), ACT.Copy), toks_ready)
                act.wait_ge(hid_summed, l + 1)
                tell(act.activation(hid[:, :, 0:CMP_N], hid[:, :, 0:CMP_N], ACT.Gelu_apprx_tanh, scale=1.0 / W_SCALE), hid_ready)
                act.wait_ge(kcvc_done, l + 1)
                for g in range(2):
                    r = slice(g * HD, g * HD + HD)
                    act.activation(kc[r, 0:CMP_N], bank(6 + g, 0, CMP_N, r), ACT.Copy)
                    ins = act.activation(vc[0:CMP_N, g, :], bank(6 + g, 64, 64 + HD, slice(0, CMP_N)), ACT.Copy)
                tell(ins, kcvc_ready)
                for which in range(2):
                    high_part(matrices[f"cmp_{l}_{which}"] + SPLIT)
                act.wait_ge(cmp_shifted, l + 1)
                tell(act.activation(sc[:, :, 0:CMP_N], sc[:, :, 0:CMP_N], ACT.Exp), cmp_exped)

                base = 12 * l

                def exps(u):
                    nk = (u // 6 + 1) * P
                    act.wait_ge(scores_max, base + u + 1)
                    if u >= 2:
                        act.wait_ge(p_turned, base + u - 1)
                    for b in range(2):
                        ins = act.activation(e_at[:, u % 2, b, 0:nk], bank(6 + u % 2, b * nk, b * nk + nk), ACT.Exp,
                                             bias=nm[:, u % 2, b:b + 1], accum_out=nm[:, u % 2, 2 + b:3 + b])
                    tell(ins, attn_exp)

                def copy_pt(u):
                    n = 2 * (u // 6 + 1) * P
                    act.wait_ge(p_turned, base + u + 1)
                    if u >= 2:
                        act.wait_ge(pv_done, base + u - 1)
                    tell(act.activation(pt_at[:, u % 2, 0:n], bank(u % 2, 0, n), ACT.Copy), pt_ready)

                def copy_out(u):
                    c, j, g = u // 6, (u % 6) // 2, u % 2
                    r = slice(g * HD, g * HD + HD)
                    act.wait_ge(pv_done, base + u + 1)
                    tell(act.activation(gmix[r, j, c * P:c * P + P], bank(2 + u % 2, 0, P, r), ACT.Copy), mix_out)

                for u in range(14):
                    if u < 12:
                        exps(u)
                    if u == 0:
                        act.wait_ge(cmp_turned, l + 1)
                        for n in range(3):
                            ins = act.activation(ptc[0:CMP_N, 4 * n:4 * n + 4, :], shaped(bank(n, rows=slice(0, CMP_N)), 4, P), ACT.Copy)
                        tell(ins, ptc_ready)
                    if 1 <= u < 13:
                        copy_pt(u - 1)
                    if u >= 2:
                        copy_out(u - 2)

                act.wait_ge(kend_turned, l + 1)
                tell(act.activation(kend_tok, shaped(bank(4), 4, P), ACT.Copy), kend_tok_ready)
                tell(act.activation(og_silu, p1[:, T_OG:T_OG + 3, :], ACT.Silu))
                act.wait_ge(o_done, l + 1)
                for q in range(4):
                    dst, src = gla_out(o_sq, q)
                    ins = act.activation(dst, src, ACT.Square)
                tell(ins, o_squared)
                act.wait_ge(pool_done, l + 1)
                for g in range(4):
                    r = slice(64 * (g % 2), 64 * (g % 2) + 64)
                    tell(act.activation(gmix[r, 6 + g // 2, :], bank(g % 2, (g // 2) * S, (g // 2) * S + S, r), ACT.Identity,
                                        scale=pcol(f"pool_scale{l}", g // 2, r)), pool_mixed)
                act.wait_ge(mix_out, 12 * l + 12)
                high_x(gmix, tiles=range(3))
                act.wait_ge(o_sums, l + 1)
                act.activation(o_rs[:, 0:2, :], shaped(bank(5), 2, S), ACT.Sqrt, bias=eps_rms)
                tell(act.activation(o_rs[:, 2, :], bank(6, 0, S), ACT.Sqrt, bias=eps_rms), o_rstd)

                act.wait_ge(pool_mixed, 4 * l + 4)
                high_x(gmix, lambda k: act.wait_ge(gla_mixed, 3 * l + k - 2) if k < 6 else None, range(3, KT))
                product(f"out1_{l}", warm_root)
                layer_norm(2 * l, 1, l)
                up = products[f"up1_{l}"]["first"]

                def relu(t):
                    if t >= 4:
                        act.wait_ge(f_ready, FT1 * l + t - 3)
                    evacuate(f_relu[:, t % 4, :], up + t, S, ACT.Relu)

                product(f"up1_{l}", relu)
                product(f"down1_{l}", warm_root)
                layer_norm(2 * l + 1, 2, l)

            def pre_norm(n):
                for k in range(0, KT, 2):
                    if n == 0:
                        act.wait_ge(first_out, k + 2)
                    else:
                        act.wait_ge(h2_ready, 8 * (n // 2 - 1) + k + 2)
                    tell(act.activation(sq_all[:, k:k + 2, :], h_all[:, k:k + 2, :], ACT.Square), sq_ready, n=2)
                root_of_mean(4 + n, T, eps_rms)
                high_x(sq_all, lambda k: act.wait_ge(u_ready, 8 * (n // 2) + k + 1))

            def out_product(name):
                first = products[name]["first"]

                def evac(t):
                    g = first + t
                    warm_root(t)
                    done(g)
                    tell(act.activation(sq_all[:, t, :], bank(BANK[g], 0, T), ACT.Square, scale=1.0 / W_SCALE), sq_ready)
                    evacuate(m_all[:, t, :], g, T)

                return product(name, evac, hold=True)

            def second_ffn(l):
                up = products[f"up2_{l}"]["first"]

                def gelu(i):
                    act.wait_ge(*evac_value(up + 2 * i))
                    tell(act.activation(cg[:, i % 2, :], cg[:, i % 2, :], ACT.Gelu_apprx_tanh), conv_act)

                def last_tap(t):
                    i, half = divmod(t, 2)
                    g, buf = up + t, (cg, cu)[half]
                    done(g)
                    if i >= 2:
                        act.wait_ge(f_ready, 2 * FT1 + FT2 * l + i - 1)
                    tell(act.activation(buf[:, i % 2, :], bank(BANK[g], 0, T), ACT.Identity, scale=pcol(f"ffn_w{l}", 2 * 2 * FT2 + t),
                                        bias=pcol(f"ffn_b{l}", t)), conv_acc)
                    if half and i:
                        gelu(i - 1)

                product(f"up2_{l}", last_tap)
                gelu(FT2 - 1)
                return out_product(f"down2_{l}")

            def griffin():
                first = products["in_g"]["first"]

                def evac(t):
                    i, g = t % 8, first + t
                    if t == 13:
                        act.wait_ge(conv_done, 1)
                        tell(act.activation(xr_hi, xr, ACT.Copy), xr_high)
                    if t == 18:
                        tell(act.activation(lnv[:, 16:24], lnv[:, 8:16], ACT.Abs))
                        tell.settle()
                        tell(act.activation(lnv[:, 16:24], lnv[:, 16:24], ACT.Exp, scale=-1.0))
                        tell.settle()
                        tell(act.activation(lnv[:, 16:24], lnv[:, 16:24], ACT.Ln, bias=1.0), lru_softplus)
                    if t < 8:
                        done(g)
                        tell(act.activation(xr[:, i, :], bank(BANK[g], 0, T), ACT.Identity, scale=pcol("lru_w", 24 + i), bias=pcol("lru_b", i)), conv_acc)
                    elif t < 16:
                        evacuate(gg[:, i, :], g, T, ACT.Gelu_apprx_tanh)
                    elif t < 24:
                        done(g)
                        act.activation(kv_t[:, 2, META * i:META * i + META], bank(BANK[g], 2 * P, T), ACT.Copy, scale=float(HD) ** -0.5 / W_SCALE)
                        evacuate(qt[:, i, :], g, T, scale=float(HD) ** -0.5)
                    else:
                        evacuate(kv_t[:, i, :], g, T)

                product("in_g", evac)
                for n in range(16):
                    act.wait_ge(lru_done, n + 1)
                    dst = (rg if n < 8 else ig)[:, n % 8, :]
                    tell(act.activation(dst, bank(4 + n % 4, 0, T), ACT.Sigmoid, bias=pcol("lru_ba" if n < 8 else "lru_bx", n % 8), scale=1.0 / W_SCALE), lru_gated)
                high_part(matrices["lru"] + SPLIT)
                act.wait_ge(lru_log, 1)
                act.activation(a_sc, la, ACT.Exp)
                act.activation(th, la, ACT.Tanh, scale=-1.0)
                tell(act.activation(sq_all, la, ACT.Exp, scale=2.0), lru_exp)
                act.wait_ge(v2_turned, 1)
                act.activation(v_swa[:, 0:2, :], shaped(bank(0, 0, 256), 2, P), ACT.Copy)
                tell(act.activation(v_swa[0:16, 2, :], bank(0, 256, 384, slice(0, 16)), ACT.Copy), v2_ready)
                act.wait_ge(lru_a2, 1)
                tell(act.activation(th, th, ACT.Sqrt), lru_root)
                for b, (c, g, half) in enumerate(SWA_BATCHES):
                    nk = SWA_KEYS[c]
                    heads = 4 if c < 2 else 1
                    if b:
                        swa_turned(b - 1)
                    act.wait_ge(sw_max, b + 1)
                    st = sm[:, b % 2]
                    for j in range(heads):
                        s = s_at[b % 2][:, j, 0:nk] if c < 2 else s_at[b % 2].rearrange("p a b -> p (a b)")[:, 0:nk]
                        act.activation(s, s, ACT.Exp, bias=st[:, 1, j:j + 1], accum_out=st[:, 2, j:j + 1])
                    tell(act.activation(st[:, 3, 0:heads], st[:, 3, 0:heads], ACT.Exp), sw_exp)
                    if b:
                        swa_mixed(b - 1)
                    if b == 2:
                        act.wait_ge(lru_out, 1)
                        tell(act.activation(ya_hi, gmix_a, ACT.Copy), ya_high)
                swa_turned(len(SWA_BATCHES) - 1)
                swa_mixed(len(SWA_BATCHES) - 1)
                tell.settle()
                tell(act.activation(yb_hi, gmix_b, ACT.Copy), ya_high)
                return out_product("out_g")

            def swa_turned(b):
                c, g, half = SWA_BATCHES[b]
                nk = SWA_KEYS[c]
                heads = 4 if c < 2 else 1
                act.wait_ge(sw_turned, b + 1)
                if b:
                    act.wait_ge(sw_pv, b)
                for k in range((nk + P - 1) // P):
                    rows = slice(0, min(P, nk - k * P))
                    ins = act.activation(pt_sw[rows, k, 0:heads * P], bank(1 + k, 0, heads * P, rows), ACT.Copy)
                tell(ins, sw_pt)

            def swa_mixed(b):
                c, g, half = SWA_BATCHES[b]
                act.wait_ge(sw_pv, b + 1)
                r = slice(g * HD, g * HD + HD)
                if c < 2:
                    ins = act.activation(gmix_b[r, 4 * half:4 * half + 4, c * P:c * P + P], shaped(bank(0, rows=r), 4, P), ACT.Copy)
                else:
                    ins = act.activation(gmix_b[r, :, 2 * P:T], shaped(bank(0, 0, P, r), 8, META), ACT.Copy)
                tell(ins, sw_out)

            def mamba():
                first = products["in_m"]["first"]

                def softplus():
                    act.wait_ge(*evac_value(first))
                    ab = dts[0:32, 3, :]
                    tell(act.activation(ab, dts[0:32, 0, :], ACT.Abs))
                    tell.settle()
                    tell(act.activation(ab, ab, ACT.Exp, scale=-1.0))
                    tell(act.activation(aneg[0:32, 0:1], pcol("a_log", 0, slice(0, 32)), ACT.Exp))
                    tell.settle()
                    tell(act.activation(ab, ab, ACT.Ln, bias=1.0), dt_logged)

                def silu(i):
                    act.wait_ge(*evac_value(first + 1 + i))
                    tell(act.activation(xbc[:, i, :], xbc[:, i, :], ACT.Silu), conv_act)

                def evac(t):
                    if t == 0:
                        return softplus()
                    i, g = t - 1, first + t
                    if i == 8:
                        act.wait_ge(cs_ready, 1)
                        tell(act.activation(dts[0:32, 4, :], dts[0:32, 4, :], ACT.Exp, scale=-1.0), ssd_end)
                    done(g)
                    tell(act.activation(xbc[:, i, :], bank(BANK[g], 0, T), ACT.Identity, scale=pcol("ssm_w", 96 + i), bias=pcol("ssm_b", i)), conv_acc)
                    if i:
                        silu(i - 1)

                product("in_m", evac)
                silu(31)
                for j in range(2):
                    single_tile("in_z", j, z_t[:, j, :], T)
                act.wait_ge(dtt_done, 1)
                act.activation(dtt[0:META, 0], shaped(bank(7, 0, 96, slice(0, META)), 3, 32), ACT.Copy)
                tell(act.activation(dtt[:, 1:3], shaped(bank(7, 96, 288), 2, 3, 32), ACT.Copy), dtt_ready)
                for ci, (t0, n) in enumerate(CHUNKS):
                    if ci < 2:
                        act.wait_ge(b_turned, ci + 1)
                        for i in range(2):
                            ins = act.activation(b_tok[0:n, 4 * i:4 * i + 4, :], shaped(bank(2 + i, rows=slice(0, n)), 4, P), ACT.Copy)
                        tell(ins, b_ready)
                    else:
                        for j in (8, 9):
                            single_tile("in_z", j, z_t[:, j, :], T)
                    if ci == 0:
                        act.wait_ge(seg_ready, SSM_G)
                        tell(act.activation(seg_all[0:n], seg_all[0:n], ACT.Exp), ssd_exp, n=SSM_G)
                        continue
                    for g in range(SSM_G):
                        q = 8 * ci + g
                        if ci:
                            act.wait_ge(seg_ready, q + 1)
                            if q - 8 >= 2:
                                act.wait_ge(cd_ready, q - 8 - 1)
                                act.wait_ge(prev_ready, min(q - 1, 16))
                            act.activation(e2[:, q % 2], shaped(bank(2 + q % 2), 4, P), ACT.Exp)
                        act.wait_ge(seg_ready, q + 1)
                        s = seg[0:n, q % 2, :, 0:n]
                        tell(act.activation(s, s, ACT.Exp), ssd_exp)
                        if g in GATE_GROUPS:
                            j = 8 * (ci - 1) + 1 + g
                            single_tile("in_z", j, z_t[:, j, :], T)
                high_part(products["in_z"]["steps"][-1][0] + SPLIT, 1)
                tell.settle()
                for g in range(0, SSM_TILES, 4):
                    tell(act.activation(z_t[:, g:g + 4, :], z_t[:, g:g + 4, :], ACT.Silu), gates_act)
                for g in range(SSM_G):
                    act.wait_ge(zy_ready, g + 1)
                    dst = (u_all if g < 4 else m_all)[:, 2 * (g % 4):2 * (g % 4) + 2, :]
                    tell(act.activation(dst, xbc[:, 2 * g:2 * g + 2, :], ACT.Square), zy_sq)

                def high_y(g):
                    act.wait_ge(zy_normed, 2 * g + 2)
                    tell(act.activation(ym_hi[:, 2 * g:2 * g + 2, :], xbc[:, 2 * g:2 * g + 2, :], ACT.Copy), ym_high)

                for g in range(SSM_G):
                    act.wait_ge(zy_sums, g + 1)
                    tell(act.activation(g_rs[:, g, :], bank(g, 0, T), ACT.Ln, bias=eps_rms, scale=float(D) / 256.0))
                tell.settle()
                for g in (0, SSM_G // 2):
                    part = g_rs[:, g:g + SSM_G // 2, :]
                    tell(act.activation(part, part, ACT.Exp, scale=-0.5), zy_rstd, n=SSM_G // 2)
                for g in range(SSM_G):
                    high_y(g)
                return out_product("out_m")

            act.wait_ge(x_in, 16)
            high_x(h1)
            for i in range(SPLIT):
                high_part(i)
            act.wait_ge(tables_in, 64)
            act.wait_ge(params_scaled, 1)
            for l in range(DEPTH):
                first_layer(l)

            pre_norm(0)
            held = griffin()
            root_of_mean(5, T, eps_rms)
            high_part(held)
            pre_norm(2)
            held = second_ffn(0)
            root_of_mean(7, T, eps_rms)
            high_part(held)
            pre_norm(4)
            held = mamba()
            root_of_mean(9, T, eps_rms)
            high_part(held)
            pre_norm(6)
            second_ffn(1)
            root_of_mean(11, T, eps_rms)

        @block.vector
        def _(dve):
            tell = Tell(dve, dve_chain)

            def low_part(i, half=None):
                if i >= len(slots):
                    return
                w, at, off = slots[i]["width"], (i % SPLIT) * SLOT, (i % RAW) * SLOT
                if half is not None:
                    w //= 2
                    at, off = at + half * w, off + half * w
                dve.wait_ge(high_ready, i + 1)
                tell(dve.scalar_tensor_tensor(low[:, at:at + w], raw[:, off:off + w], W_SCALE, high[:, at:at + w], ALU.mult,
                                              ALU.subtract), split_ready if half != 0 else None)

            def product(name, evac=lambda t: None, hold=False):
                for n, (i, tiles) in enumerate(ready_steps(name)):
                    for t in tiles:
                        evac(t)
                    if n == 1:
                        low_part(i - 1 + SPLIT)
                    if n and not (hold and i == products[name]["steps"][-1][0]):
                        low_part(i + SPLIT)
                return i + SPLIT

            def behind_tile(name, j):
                if j > 0:
                    low_part(products[name]["steps"][(j - 1) // 2][0] + SPLIT, (j - 1) % 2)

            def low_x(src, p, tiles=range(KT)):
                for k in tiles:
                    dve.wait_ge(xh_ready, 8 * p + k + 1)
                    n = src.shape[2]
                    tell(dve.tensor_tensor(x_lo[:, k, 0:n], src[:, k, :], x_hi[:, k, 0:n], ALU.subtract), x_ready)

            def residual(name, n):
                first = products[name]["first"]

                def add(t):
                    g = first + t
                    dve.wait_ge(tile_done, g + 1)
                    dve.wait_ge(m_scaled, n + 1)
                    tell(dve.scalar_tensor_tensor(m_all[:, t, 0:S], bank(BANK[g], 0, S), 1.0 / W_SCALE, m_all[:, t, 0:S], ALU.mult, ALU.add),
                         *evac_value(g))

                return product(name, add, hold=True)

            def inverse_root(norm, n):
                dve.wait_ge(root_ready, norm + 1)
                tell(dve.reciprocal(rstd[:, 0:n], root[:, 0:n]))
                tell.settle()

            def layer_norm(m, which, l, held):
                dve.wait_ge(mean_done, m + 1)
                tell.settle()
                for k in range(0, KT, 2):
                    pair = m_all[:, k:k + 2, 0:S]
                    tell(dve.tensor_tensor(pair, pair, over(bank(5, 0, S), 2), ALU.subtract), centred, n=2)
                low_part(held)
                inverse_root(m, S)

                def low(k):
                    dve.wait_ge(xh_ready, 8 * (2, 3, 5)[m] + k + 1)
                    tell(dve.scalar_tensor_tensor(x_lo[:, k, 0:S], m_all[:, k, 0:S], pcol(f"ln{which}_b{l}", k), x_hi[:, k, 0:S],
                                                  ALU.add, ALU.subtract), x_ready)

                last = m == 2 * DEPTH - 1
                for k in range(KT if last else KT + 2):
                    if k < KT:
                        tell(dve.scalar_tensor_tensor(m_all[:, k, 0:S], m_all[:, k, 0:S], pcol(f"ln{which}_g{l}", k), rstd[:, 0:S],
                                                      ALU.mult, ALU.mult), ln_scaled)
                    if k >= 2 and not last:
                        low(k - 2)

            def first_layer(l):
                first = products[f"in1_{l}"]["first"]

                def evac_wait(t):
                    dve.wait_ge(*evac_value(first + t))

                def rotate():
                    for i in range(3):
                        pair = roped[:, 2 * i:2 * i + 2, :]
                        dve.wait_ge(rope_done, 3 * l + i + 1)
                        tell(dve.tensor_tensor(pair, shaped(bank(4 + i), 2, S), over(C("sin", 0, S), 2), ALU.mult))
                        tell.settle()
                        dve.wait_ge(cos_ready, l + 1)
                        tell(dve.tensor_tensor(pair, pair, rope_cos[:, 2 * i:2 * i + 2, :], ALU.add), roped_ready)

                def compression(t):
                    if t == 12:
                        dve.wait_ge(roped_ready, 3 * l + 3)
                        evac_wait(T_VC)
                        for which, src in ((0, roped[:, T_KC, :]), (1, p1[:, T_VC, :])):
                            windows = bass.AP(src.tensor, src.offset, [list(src.ap[0]), [1, CMP_BLOCK], [CMP_STRIDE, CMP_N]])
                            pos = par[:, PAR[f"pos{l}"] + 32 * which:PAR[f"pos{l}"] + 32 * which + 32]
                            tell(dve.tensor_tensor(tb[:, which], windows, along(pos, CMP_N), ALU.add), tb_ready)
                    if t == 16:
                        dve.wait_ge(tb_high, l + 1)
                        tell(dve.tensor_tensor(tb_lo, tb, tb_hi, ALU.subtract), tb_split)

                product(f"in1_{l}", lambda t: rotate() if t == 9 else compression(t))
                dve.wait_ge(gk_done, l + 1)
                for i in range(2):
                    ins = dve.tensor_scalar(shaped(gk_x, 2, S)[:, i, :], bank(7, i * S, i * S + S), pcol(f"b_gate{l}", i), None, ALU.add)
                tell(ins, gk_biased)
                tell.settle()
                dve.wait_ge(gk_logged, l + 1)
                tell(dve.scalar_tensor_tensor(gk_l, gk_x, 0.0, gk_l, ALU.min, ALU.subtract))
                tell.settle()
                tell(dve.tensor_tensor_scan(bc, C("gla_reset", 0, 2 * S), gk_l, 0.0, ALU.mult, ALU.add))
                tell.settle()
                chunked = shaped(bc, 8, GLA_C)
                tell(dve.tensor_tensor(shaped(gk_l, 8, GLA_C), chunked[:, :, GLA_C - 1:GLA_C].to_broadcast([P, 8, GLA_C]), chunked, ALU.subtract), bcum_ready)
                dve.wait_ge(decays_ready, l + 1)
                p1q = p1[:, T_GQ:T_GQ + 2, :].rearrange("p a b -> p (a b)")
                p1k = p1[:, T_GK:T_GK + 2, :].rearrange("p a b -> p (a b)")
                dve.scalar_tensor_tensor(qd, p1q, float(np.float32(GLA_DK ** -0.5)), ep, ALU.mult, ALU.mult)
                tell(dve.tensor_tensor(kinv, p1k, en, ALU.mult), gla_in)
                tell(dve.tensor_tensor(kend, p1k, gk_x, ALU.mult), kend_ready)
                dve.wait_ge(hid_done, l + 1)
                for g in range(2):
                    r = slice(g * HD, g * HD + HD)
                    parts = shaped(bank(4 + g, 0, 64, r), 2, 32)
                    ins = dve.tensor_copy(hid[r, :, 0:CMP_N], parts[:, :, 0:CMP_N])
                tell(ins)
                tell.settle()
                for g in range(2):
                    r = slice(g * HD, g * HD + HD)
                    parts = shaped(bank(4 + g, 0, 64, r), 2, 32)
                    ins = dve.tensor_tensor(hid[r, :, 0:CMP_N], hid[r, :, 0:CMP_N], parts[:, :, CMP_N:2 * CMP_N], ALU.add)
                tell(ins, hid_summed)
                dve.wait_ge(cmp_scored, l + 1)
                s15 = sc[:, :, 0:CMP_N]
                mask = shaped(C("cmp_mask", 0, 192), 12, 16)
                for g in range(2):
                    ins = dve.tensor_tensor(sc[:, 6 * g:6 * g + 6, 0:CMP_N], shaped(bank(4 + g, 0, 96), 6, 16)[:, :, 0:CMP_N],
                                            mask[:, 6 * g:6 * g + 6, 0:CMP_N], ALU.add)
                tell(ins)
                tell.settle()
                tell(dve.tensor_reduce(sc_s[:, 0, :], s15, AX_X, ALU.max))
                tell.settle()
                tell(dve.tensor_scalar(sc_s[:, 1, :], sc_s[:, 0, :], MAX_FLOOR, None, ALU.max))
                tell.settle()
                tell(dve.tensor_tensor(s15, s15, along(sc_s[:, 1, :], CMP_N), ALU.subtract), cmp_shifted)
                dve.wait_ge(cmp_exped, l + 1)
                tell(dve.tensor_reduce(sc_s[:, 2, :], s15, AX_X, ALU.add))
                tell.settle()
                tell(dve.tensor_scalar(sc_s[:, 3, :], sc_s[:, 2, :], 1.0e-30, None, ALU.max))
                tell.settle()
                tell(dve.reciprocal(sc_s[:, 4, :], sc_s[:, 3, :]))
                tell.settle()
                dve.wait_ge(toks_ready, l + 1)
                gates = gates_t.rearrange("p c (g j b) -> p c g j b", g=2, j=3)
                for c in range(2):
                    r = sc_s[:, 4, :].rearrange("p (g c j) -> p g c j", g=2, c=2)[:, :, c, :]
                    ins = dve.tensor_tensor(sc_s[:, 0, :].rearrange("p (g c j) -> p g c j", g=2, c=2)[:, :, c, :], r, gates[:, c, :, :, 0], ALU.mult)
                tell(ins)
                tell.settle()
                tell(dve.tensor_tensor(s15, s15, along(sc_s[:, 0, :], CMP_N), ALU.mult), cmp_ready)
                low_part(matrices[f"cmp_{l}_0"] + SPLIT)

                base = 12 * l

                def maxima(u):
                    c = u // 6
                    nk = (c + 1) * P
                    b2 = shaped(bank(6 + u % 2, 0, 2 * nk), 2, nk)
                    dve.wait_ge(scores_done, base + u + 1)
                    if u >= 2:
                        dve.wait_ge(attn_exp, base + u - 1)
                    tell(dve.tensor_tensor(b2[:, :, c * P:nk], b2[:, :, c * P:nk], over(C("tri", 0, P), 2), ALU.add))
                    tell.settle()
                    tell(dve.tensor_reduce(nm[:, u % 2, 0:2], b2, AX_X, ALU.max, negate=True), scores_max)

                def weigh(u):
                    c, j, g = u // 6, (u % 6) // 2, u % 2
                    nk = (c + 1) * P
                    dve.wait_ge(attn_exp, base + u + 1)
                    tell(dve.reciprocal(nm[:, u % 2, 4:6], nm[:, u % 2, 2:4]))
                    tell.settle()
                    at = (g * 3 + j) * 3
                    tell(dve.tensor_tensor(nm[:, u % 2, 6:8], nm[:, u % 2, 4:6], gates_t[:, c, at + 1:at + 3], ALU.mult))
                    tell.settle()
                    for b in range(2):
                        e = e_at[:, u % 2, b, 0:nk]
                        ins = dve.tensor_scalar(e, e, nm[:, u % 2, 6 + b:7 + b], None, ALU.mult)
                    tell(ins, attn_p)

                for u in range(13):
                    if u:
                        weigh(u - 1)
                    if u < 12:
                        maxima(u)

                low_part(matrices[f"cmp_{l}_1"] + SPLIT)
                dve.wait_ge(a_done, l + 1)
                for b in range(4):
                    n = 4 if b < 2 else 2
                    ins = dve.tensor_tensor(at_gla[:, b, 0:n, :], shaped(bank(b, 0, n * P), n, P), over(C("gla_causal", 0, P), n), ALU.mult)
                tell(ins, a_masked)
                dve.wait_ge(ds_done, l + 1)
                epc = shaped(ep, 2, 4, GLA_C)
                for n in range(3):
                    for i in range(2):
                        rows = slice(0, P) if i == 0 else slice(0, HD)
                        ds = bank(5 + n % 2, (n // 2) * P + i * HD, (n // 2) * P + i * HD + HD, rows)
                        if n == 0:
                            ins = dve.tensor_copy(s_gla[rows, n, i, :], ds)
                        else:
                            ins = dve.scalar_tensor_tensor(s_gla[rows, n, i, :], s_gla[rows, n - 1, i, :], epc[rows, i, n, GLA_C - 1:GLA_C], ds,
                                                           ALU.mult, ALU.add)
                    tell(ins, s_ready if n == 2 else None)
                    tell.settle()
                dve.wait_ge(o_squared, l + 1)
                for q in range(4):
                    gate, _ = gla_out(og_silu, q)
                    ins = dve.tensor_tensor(gate, gla_out(og_silu, q)[1], gate, ALU.mult)
                tell(ins, og_read)
                low_x(gmix, 3 * l + 1, range(3))
                dve.wait_ge(o_rstd, l + 1)
                for i in range(3):
                    tell(dve.reciprocal(o_rs[:, i, :], o_rs[:, i, :]))
                    tell.settle()
                    tell(dve.scalar_tensor_tensor(gmix[:, 3 + i, :], og_silu[:, i, :], pcol(f"norm_g{l}", i), o_rs[:, i, :], ALU.mult, ALU.mult), gla_mixed)
                low_x(gmix, 3 * l + 1, range(3, KT))
                layer_norm(2 * l, 1, l, residual(f"out1_{l}", 2 * l))
                up = products[f"up1_{l}"]["first"]

                def square(t):
                    dve.wait_ge(*evac_value(up + t))
                    tell(dve.tensor_tensor(f1_hi[:, t, :], f_relu[:, t % 4, :], f_relu[:, t % 4, :], ALU.mult), fh_ready)

                product(f"up1_{l}", square)
                layer_norm(2 * l + 1, 2, l, residual(f"down1_{l}", 2 * l + 1))

            def pre_norm(n, name, held=None):
                if held:
                    low_part(held)
                inverse_root(4 + n, T)
                p = 6 + n // 2
                for k in range(KT + 2):
                    if k < KT:
                        tell(dve.scalar_tensor_tensor(sq_all[:, k, :], h_all[:, k, :], pcol(name, k), rstd, ALU.mult, ALU.mult), u_ready)
                    if k >= 2:
                        dve.wait_ge(xh_ready, 8 * p + k - 1)
                        tell(dve.tensor_tensor(x_lo[:, k - 2, :], sq_all[:, k - 2, :], x_hi[:, k - 2, :], ALU.subtract), x_ready)

            def post_norm(n, name):
                inverse_root(4 + n, T)
                for k in range(0, KT, 2):
                    for i in (k, k + 1):
                        tell(dve.scalar_tensor_tensor(m_all[:, i, :], m_all[:, i, :], pcol(name, i), rstd, ALU.mult, ALU.mult))
                    tell.settle()
                    tell(dve.tensor_tensor(h_all[:, k:k + 2, :], h_all[:, k:k + 2, :], m_all[:, k:k + 2, :], ALU.add), h2_ready, n=2)

            def taps(dst, g, count, acc_value, weight):
                dve.wait_ge(conv_acc, acc_value)
                for back in range(1, count):
                    ins = dve.scalar_tensor_tensor(dst[:, back:T], bank(BANK[g], 0, T - back), weight(count - 1 - back), dst[:, back:T], ALU.mult, ALU.add)
                    if back < count - 1:
                        tell(ins)
                        tell.settle()
                tell(ins, *evac_value(g))

            def second_ffn(l):
                up = products[f"up2_{l}"]["first"]
                acc0 = (8, 8 + 2 * FT2 + 32)[l]
                act0 = (0, FT2 + 32)[l]

                def gated(i):
                    dve.wait_ge(conv_act, act0 + i + 1)
                    tell(dve.tensor_tensor(f2_hi[:, i, :], cg[:, i % 2, :], cu[:, i % 2, :], ALU.mult), fh_ready)

                def other_taps(t):
                    i, half = divmod(t, 2)
                    taps((cg, cu)[half][:, i % 2, :], up + t, 3, acc0 + t + 1, lambda tap: pcol(f"ffn_w{l}", tap * 2 * FT2 + t))
                    if half and i:
                        gated(i - 1)

                product(f"up2_{l}", other_taps)
                tell.settle()
                gated(FT2 - 1)
                return product(f"down2_{l}", hold=True)

            def griffin():
                first = products["in_g"]["first"]

                def behind(t):
                    if t < 8:
                        taps(xr[:, t, :], first + t, 4, t + 1, lambda tap: pcol("lru_w", tap * 8 + t))
                    if t == 9:
                        for i in range(4, 8):
                            dve.wait_ge(*evac_value(first + i))
                        tell(dve.tensor_scalar(lnv[:, 8:16], par[:, PAR["lru_lam"]:PAR["lru_lam"] + 8], -1.0, None, ALU.mult), conv_done)
                    if t == 15:
                        dve.wait_ge(xr_high, 1)
                        tell(dve.tensor_tensor(xr_lo, xr, xr_hi, ALU.subtract), xr_split)

                product("in_g", behind)
                dve.wait_ge(lru_softplus, 1)
                tell.settle()
                tell(dve.scalar_tensor_tensor(lnv[:, 24:32], lnv[:, 8:16], 0.0, lnv[:, 16:24], ALU.max, ALU.add))
                tell.settle()
                tell(dve.tensor_scalar(lnv[:, 24:32], lnv[:, 24:32], -8.0, None, ALU.mult))
                tell.settle()
                dve.wait_ge(lru_gated, 8)
                tell(dve.tensor_tensor(la, rg, along(lnv[:, 24:32], T), ALU.mult), lru_log)
                dve.wait_ge(lru_gated, 16)
                tell(dve.tensor_tensor(ig, ig, xr, ALU.mult))
                low_part(matrices["lru"] + SPLIT)
                dve.wait_ge(lru_exp, 1)
                tell(dve.scalar_tensor_tensor(th, sq_all, 1.0, th, ALU.add, ALU.mult), lru_a2)
                dve.wait_ge(lru_root, 1)
                tell.settle()
                dve.memset(a_sc[:, :, 0:1], 0.0)
                tell(dve.tensor_tensor(th, th, ig, ALU.mult))
                tell.settle()
                flat = lambda a: a.rearrange("p k t -> p (k t)")
                tell(dve.tensor_tensor_scan(flat(gmix_a), flat(a_sc), flat(th), 0.0, ALU.mult, ALU.add))
                tell.settle()
                for b in range(len(SWA_BATCHES) + 1):
                    if b:
                        swa_weigh(b - 1)
                    if b < len(SWA_BATCHES):
                        swa_scores(b)
                    if b == 1:
                        tell(dve.tensor_tensor(gmix_a, gmix_a, gg, ALU.mult), lru_out)
                    if b == 3:
                        dve.wait_ge(ya_high, 1)
                        tell(dve.tensor_tensor(ya_lo, gmix_a, ya_hi, ALU.subtract), y_split)
                dve.wait_ge(ya_high, 2)
                tell(dve.tensor_tensor(yb_lo, gmix_b, yb_hi, ALU.subtract), y_split)
                return product("out_g", hold=True)

            def swa_scores(b):
                c, g, half = SWA_BATCHES[b]
                nk = SWA_KEYS[c]
                heads = 4 if c < 2 else 1
                st = sm[:, b % 2]
                s0 = 4 + 2 * (b % 2)
                dve.wait_ge(sw_scored, b + 1)
                if b >= 2:
                    dve.wait_ge(sw_turned, b - 1)
                per = 512 // nk
                flat = s_at[b % 2].rearrange("p a b -> p (a b)")
                for j in range(heads):
                    src = bank(s0 + j // per, (j % per) * nk, (j % per) * nk + nk)
                    slope = C("slope_last", g, g + 1) if c == 2 else -SLOPES[g * SWA_J + 4 * half + j]
                    dst = s_at[b % 2][:, j, 0:nk] if c < 2 else flat[:, 0:nk]
                    ins = dve.scalar_tensor_tensor(dst, C(f"dist{c}", 0, nk), slope, src, ALU.mult, ALU.add)
                tell(ins)
                tell.settle()
                if c < 2:
                    tell(dve.tensor_reduce(st[:, 0, 0:heads], s_at[b % 2][:, :, 0:nk], AX_X, ALU.max))
                    sink = par[:, PAR["sinks"] + g * SWA_J + 4 * half:PAR["sinks"] + g * SWA_J + 4 * half + 4]
                else:
                    tell(dve.tensor_reduce(st[:, 0, 0:1], flat[:, 0:nk], AX_X, ALU.max))
                    sink = pcol("sinks_last", g)
                tell.settle()
                tell(dve.tensor_tensor(st[:, 4, 0:heads], st[:, 0, 0:heads], sink, ALU.max))
                tell.settle()
                dve.tensor_scalar(st[:, 1, 0:heads], st[:, 4, 0:heads], -1.0, None, ALU.mult)
                tell(dve.tensor_tensor(st[:, 3, 0:heads], sink, st[:, 4, 0:heads], ALU.subtract), sw_max)

            def swa_weigh(b):
                c, g, half = SWA_BATCHES[b]
                nk = SWA_KEYS[c]
                heads = 4 if c < 2 else 1
                st = sm[:, b % 2]
                dve.wait_ge(sw_exp, b + 1)
                tell(dve.tensor_tensor(st[:, 5, 0:heads], st[:, 2, 0:heads], st[:, 3, 0:heads], ALU.add))
                tell.settle()
                tell(dve.reciprocal(st[:, 0, 0:heads], st[:, 5, 0:heads]))
                tell.settle()
                if c < 2:
                    s = s_at[b % 2][:, :, 0:nk]
                    tell(dve.tensor_tensor(s, s, along(st[:, 0, 0:heads], nk), ALU.mult), sw_p)
                else:
                    s = s_at[b % 2].rearrange("p a b -> p (a b)")[:, 0:nk]
                    tell(dve.tensor_scalar(s, s, st[:, 0, 0:1], None, ALU.mult), sw_p)

            def first_chunk():
                n = META
                rows = slice(0, n)
                seg_heads = seg_all[rows].rearrange("p a b c -> p (a b) c")
                dve.wait_ge(cs_spread, SSM_G)
                tell(dve.tensor_tensor(seg_heads, shaped(bank(2, rows=rows), 32, n), along(dtt[rows, 0, 1, :], n), ALU.subtract))
                tell.settle()
                tell(dve.tensor_tensor(seg_heads, seg_heads, over(C("ssd_causal", 0, n, rows), 32), ALU.min), seg_ready, n=SSM_G)
                dve.wait_ge(ssd_exp, SSM_G)
                tell(dve.tensor_tensor(seg_all[rows], seg_all[rows],
                                       shaped(bank(3, 0, SSM_G * n, rows), SSM_G, n).unsqueeze(2).to_broadcast([n, SSM_G, 4, n]), ALU.mult),
                     mt_ready, n=SSM_G)
                dve.wait_ge(y_done, SSM_G)
                for i in range(4):
                    ins = dve.tensor_copy(prev[:, 512 * i:512 * i + 512], bank((5, 6, 7, 2)[i]))
                tell(ins, prev_ready, n=SSM_G)
                x = xbc[:, 0:16, 0:n]
                tell(dve.tensor_tensor(x, x, along(par[:, PAR["d_skip"]:PAR["d_skip"] + 16], n), ALU.mult))
                tell.settle()
                tell(dve.tensor_tensor(x, x, shaped(bank(4, 0, 16 * n), 16, n), ALU.add), y_out, n=SSM_G)

            def mamba():
                first = products["in_m"]["first"]
                r32 = slice(0, 32)
                dt, cs, w, ab, dl = (dts[r32, i, :] for i in range(5))

                def step_sizes():
                    dve.wait_ge(tile_done, first + 1)
                    tell(dve.tensor_scalar(dt, bank(BANK[first], 0, T, r32), 1.0 / W_SCALE, pcol("dt_bias", 0, r32), ALU.mult, ALU.add),
                         *evac_value(first))
                    dve.wait_ge(dt_logged, 1)
                    tell(dve.scalar_tensor_tensor(dt, dt, 0.0, ab, ALU.max, ALU.add))
                    tell.settle()
                    tell(dve.tensor_scalar(dl, dt, aneg[r32, 0:1], -1.0, ALU.mult, ALU.mult))
                    tell.settle()
                    tell(dve.tensor_tensor_scan(cs, C("ssd_reset", 0, T, r32), dl, 0.0, ALU.mult, ALU.add))
                    tell.settle()
                    for t0, n in CHUNKS:
                        ins = dve.tensor_scalar(dts[r32, 4, t0:t0 + n], dts[r32, 1, t0:t0 + n], dts[r32, 1, t0 + n - 1:t0 + n], None, ALU.subtract)
                    tell(ins, cs_ready)

                def evac(t):
                    if t == 0:
                        return step_sizes()
                    i = t - 1
                    if i == 16:
                        dve.wait_ge(ssd_end, 1)
                        tell(dve.tensor_tensor(w, dt, dl, ALU.mult), dt_w)
                    if i < 32:
                        taps(xbc[:, i, :], first + t, 4, 8 + 2 * FT2 + t, lambda tap: pcol("ssm_w", tap * 32 + i))

                product("in_m", evac)
                tell(dve.scalar_tensor_tensor(shaped(cs_diag, 32, META), along(C("ident", 0, 32, r32), META), float(D),
                                              over(cs[:, 0:META], 32), ALU.mult, ALU.mult), diag_ready)
                dve.wait_ge(dtt_ready, 1)
                for ci, (t0, n) in enumerate(CHUNKS):
                    rows = slice(0, n)
                    for i in range(4):
                        dve.wait_ge(x_turned, 4 * ci + i + 1)
                        src = shaped(bank(4 + i, rows=rows), 8, HD)
                        ins = dve.tensor_tensor(shaped(xdt[rows, 512 * i:512 * i + 512], 8, HD), src, along(dtt[rows, ci, 0, 8 * i:8 * i + 8], HD), ALU.mult)
                        if ci < 2:
                            ins = dve.tensor_tensor(shaped(xw[rows, 512 * i:512 * i + 512], 8, HD), src, along(dtt[rows, ci, 2, 8 * i:8 * i + 8], HD), ALU.mult)
                    tell(ins, xdt_ready)

                    if ci == 0:
                        first_chunk()
                        continue

                    def segments(g):
                        q = 8 * ci + g
                        dve.wait_ge(cs_spread, q + 1)
                        if g >= 2:
                            dve.wait_ge(y_done, q - 1)
                        for h in range(4):
                            ins = dve.scalar_tensor_tensor(seg[rows, q % 2, h, 0:n], bank(2 + q % 2, h * n, h * n + n, rows),
                                                           dtt[rows, ci, 1, 4 * g + h:4 * g + h + 1], C("ssd_causal", 0, n, rows), ALU.subtract, ALU.min)
                        tell(ins, seg_ready)

                    def scores(g):
                        q = 8 * ci + g
                        dve.wait_ge(ssd_exp, q + 1)
                        s = seg[rows, q % 2, :, 0:n]
                        tell(dve.tensor_tensor(s, s, over(bank(4 + q % 2, 256, 256 + n, rows), 4), ALU.mult), mt_ready)

                    def outputs(g):
                        q = 8 * ci + g
                        dve.wait_ge(y_done, q + 1)
                        st = prev[:, 256 * g:256 * g + 256]
                        if ci == 1:
                            tell(dve.tensor_tensor(shaped(st, 4, HD), shaped(st, 4, HD), e2[:, q % 2, :, P - 1:P].to_broadcast([P, 4, HD]), ALU.mult))
                            tell.settle()
                            tell(dve.tensor_tensor(st, st, bank(6 + q % 2, 0, 256), ALU.add), prev_ready)
                        for i in range(2):
                            t = xbc[:, 2 * g + i, t0:t0 + n]
                            ins = dve.scalar_tensor_tensor(t, t, pcol("d_skip", 2 * g + i), bank(4 + q % 2, i * n, i * n + n), ALU.mult, ALU.add)
                        tell(ins, y_out)

                    for g in range(10):
                        if g >= 2:
                            outputs(g - 2)
                        if 1 <= g < 9:
                            scores(g - 1)
                        if 1 <= g < 9:
                            behind_tile("in_z", 8 * (ci - 1) + g - 2)
                        if g < 8:
                            segments(g)
                behind_tile("in_z", 15)
                behind_tile("in_z", 16)
                dve.wait_ge(y_out, 3 * SSM_G)
                for g in range(SSM_G):
                    dve.wait_ge(gates_act, g // 2 + 1)
                    t = xbc[:, 2 * g:2 * g + 2, :]
                    tell(dve.tensor_tensor(t, t, z_t[:, 2 * g:2 * g + 2, :], ALU.mult), zy_ready)
                tell.settle()

                def low_y(g):
                    dve.wait_ge(ym_high, g + 1)
                    for i in (2 * g, 2 * g + 1):
                        tell(dve.tensor_tensor(ym_lo[:, i, :], xbc[:, i, :], ym_hi[:, i, :], ALU.subtract), y_ready)

                for g in range(SSM_G):
                    dve.wait_ge(zy_rstd, g + 1)
                    dve.wait_ge(zy_sq, g + 1)
                    for i in range(2):
                        t = xbc[:, 2 * g + i, :]
                        tell(dve.scalar_tensor_tensor(t, t, pcol("gate_norm", 2 * g + i), g_rs[:, g, :], ALU.mult, ALU.mult), zy_normed)
                    if g:
                        low_y(g - 1)
                low_y(SSM_G - 1)
                return product("out_m", hold=True)

            low_x(h1, 0)
            for i in range(SPLIT):
                low_part(i)
            dve.wait_ge(tables_in, 64)
            for name, n in (("ffn_w0", 3 * 2 * FT2), ("ffn_w1", 3 * 2 * FT2), ("lru_w", 32), ("ssm_w", 4 * 32)):
                at = par[:, PAR[name]:PAR[name] + n]
                ins = dve.tensor_scalar(at, at, 1.0 / W_SCALE, None, ALU.mult)
            tell(ins, params_scaled)
            for l in range(DEPTH):
                first_layer(l)
            pre_norm(0, "mix_pre0")
            held = griffin()
            post_norm(1, "mix_post0")
            pre_norm(2, "ffn_pre0", held)
            held = second_ffn(0)
            post_norm(3, "ffn_post0")
            pre_norm(4, "mix_pre1", held)
            held = mamba()
            post_norm(5, "mix_post1")
            pre_norm(6, "ffn_pre1", held)
            second_ffn(1)
            post_norm(7, "ffn_post1")

        @block.gpsimd
        def _(pool):
            tell = Tell(pool, pool_chain)
            pool.wait_ge(tables_in, 64)
            pool.wait_ge(x_in, 16)

            def layer_norm(m, which, l):
                if m == 2 * DEPTH - 1:
                    return
                for k in range(KT):
                    pool.wait_ge(ln_scaled, 8 * m + k + 1)
                    tell(pool.tensor_scalar(h1[:, k, :], m_all[:, k, 0:S], pcol(f"ln{which}_b{l}", k), None, ALU.add), h_ready)
                if which == 1:
                    pool.wait_ge(x_ready, 8 * (3 * l + 3))
                    tell.settle()
                    tell(pool.tensor_scalar(m_all[:, :, 0:S], h1, ALPHA, None, ALU.mult), m_scaled)

            def hidden_low(n0, tiles, a, b, depth, hi, lo, tmp):
                for t in range(tiles):
                    pool.wait_ge(fh_ready, n0 + t + 1)
                    tell(pool.tensor_tensor(tmp[:, t % 2, :], a[:, t % depth, :], b[:, t % depth, :], ALU.mult))
                    tell.settle()
                    tell(pool.tensor_tensor(lo[:, t, :], tmp[:, t % 2, :], hi[:, t, :], ALU.subtract), f_ready)

            for l in range(DEPTH):
                first = products[f"in1_{l}"]["first"]
                if l:
                    pool.wait_ge(x_ready, 8 * 3 * l + 8)
                    tell.settle()
                for buf in (pool_u, pool_a, pool_b):
                    ins = pool.memset(buf[:, :, 0:16], 0.0)
                tell(ins, pool_in)
                for t in range(3, 6):
                    pool.wait_ge(*evac_value(first + t))
                pool.wait_ge(*evac_value(first + 2))
                tell(pool.tensor_tensor(rope_cos, p1[:, 0:6, :], over(C("cos", 0, S), 6), ALU.mult), cos_ready)
                pool.wait_ge(*evac_value(first + T_PU + 1))
                pool.wait_ge(*evac_value(first + T_PU))
                live, shift = pool_u, 1
                inv = shaped(C("pool_inv", 0, 2 * S), 2, S)
                for step, dst in enumerate((pool_a, pool_b, pool_a, pool_b)):
                    tell(pool.tensor_tensor(dst[:, :, 16:272], live[:, :, 16:272], live[:, :, 16 - shift:272 - shift], ALU.add))
                    tell.settle()
                    r = slice(64 * (step % 2), 64 * (step % 2) + 64)
                    i = step // 2
                    tell(pool.tensor_tensor(pool_d[r, i, :], dst[r, i, 16:272], inv[r, i, :], ALU.mult))
                    tell.settle()
                    live, shift = dst, 2 * shift
                tell(pool.tensor_tensor(pool_d, pool_d, pool_u[:, :, 16:272], ALU.subtract), pooled)
                pool.wait_ge(pool_done, l + 1)
                tell.settle()
                tell(pool.tensor_scalar(m_all[:, :, 0:S], h1, ALPHA, None, ALU.mult), m_scaled)
                layer_norm(2 * l, 1, l)
                hidden_low(FT1 * l, FT1, f_relu, f_relu, 4, f1_hi, f1_lo, f_sq)
                layer_norm(2 * l + 1, 2, l)
            hidden_low(2 * FT1, FT2, cg, cu, 2, f2_hi, f2_lo, f_prod)
            for ci, (t0, n) in enumerate(CHUNKS):
                if ci == 0:
                    continue
                for g in range(SSM_G):
                    q = 8 * ci + g
                    pool.wait_ge(ssd_exp, q + 1)
                    if g >= 2 or ci > 1:
                        pool.wait_ge(y_done, q - 1)
                    tell(pool.tensor_tensor(cd[:, q % 2], e2[:, q % 2], over(xbc[:, 24 + g, t0:t0 + n], 4), ALU.mult), cd_ready)
            hidden_low(2 * FT1 + FT2, FT2, cg, cu, 2, f2_hi, f2_lo, f_prod)


GATE_GROUPS = range(1, 7)
SWA_KEYS = [P, 2 * P, T]
SWA_BATCHES = [(c, g, half) for c in range(2) for g in range(2) for half in range(2)] + [(2, 0, 0), (2, 1, 0)]


def _columns_of(a, cols):
    out = np.zeros((a.shape[0], len(cols)), np.float32)
    at = [i for i, c in enumerate(cols) if c is not None]
    out[:, at] = a[:, [cols[i] for i in at]]
    return out


def _feature_major(v):
    v = v.reshape(-1, P)
    return v.transpose(1, 0)


def _twice(a):
    return np.concatenate([a, a], 0)


def lay_out_stream(x):
    slots, products, matrices, width, _ = plan_stream()
    stream = np.zeros((P, width), np.float32)

    def put_product(name, w, tiles, rows=None):
        if rows is not None:
            w = w[rows]
        prod = products[name]
        for i, pair, k0, ks in prod["steps"]:
            cols = [c for j in pair for c in tiles[j]]
            part = _columns_of(w[k0 * P:(k0 + ks) * P], cols).reshape(ks, P, len(cols)).transpose(1, 0, 2)
            stream[:, slots[i]["at"]:slots[i]["at"] + slots[i]["width"]] = part.reshape(P, -1)

    def put_matrix(name, parts):
        at = slots[matrices[name]]["at"]
        for a in parts:
            a = a.reshape(a.shape[0], -1)
            stream[:a.shape[0], at:at + a.shape[1]] = a
            at += a.shape[1]

    small = []
    for l in range(DEPTH):
        put_product(f"in1_{l}", x["w_in"][l], nsa_gla_pool_tiles())
        for which in range(2):
            w1 = x["cmp_w1"][l, which].reshape(CMP_BLOCK, HD, HD).transpose(1, 0, 2)
            put_matrix(f"cmp_{l}_{which}", [_twice(w1)])
        wg = np.zeros((P, 2 * P), np.float32)
        wg[:16, :GLA_H * GLA_DK] = x["gla_w_gate2"][l]
        pw = x["pool_w"][l].reshape(2, 2, HD, HD).transpose(1, 2, 0, 3).reshape(P, 2 * HD)
        small += [_twice(x["cmp_w2"][l, 0]), _twice(x["cmp_w2"][l, 1]), wg, pw]
        put_product(f"out1_{l}", x["w_out"][l], straight_tiles(KT), nsa_mix_rows())
        put_product(f"up1_{l}", x["w_up"][l], straight_tiles(FT1))
        put_product(f"down1_{l}", x["w_down"][l], straight_tiles(KT))
    put_product("in_g", x["l0_w_in_2"], griffin_tiles())
    put_matrix("lru", [x["l0_lru_w_a_2"].transpose(1, 0, 2), x["l0_lru_w_x_2"].transpose(1, 0, 2)])
    put_product("out_g", x["l0_w_out_2"], straight_tiles(KT), griffin_mix_rows())
    put_product("in_m", x["l1_w_in_2"], mamba_tiles())
    put_product("in_z", x["l1_w_in_2"], gate_tiles())
    put_product("out_m", x["l1_w_out_2"], straight_tiles(KT))
    for l in range(2):
        put_product(f"up2_{l}", x[f"l{l}_ffn_w_up_2"], ffn2_up_tiles())
        put_product(f"down2_{l}", x[f"l{l}_ffn_w_down_2"], straight_tiles(KT))
    return stream, np.concatenate(small, 1)


def lay_out_parameters(x):
    par = np.zeros((P, PAR.n), np.float32)

    def put(name, a):
        a = a.reshape(a.shape[0], -1)
        par[:a.shape[0], PAR[name]:PAR[name] + a.shape[1]] = a

    for l in range(DEPTH):
        put(f"pos{l}", _twice(x["cmp_pos"][l].transpose(2, 0, 1)))
        bg = np.zeros(2 * P, np.float32)
        bg[:GLA_H * GLA_DK] = x["gla_b_gate"][l]
        put(f"b_gate{l}", _feature_major(bg))
        put(f"norm_g{l}", _feature_major(x["gla_norm_g"][l]))
        put(f"pool_scale{l}", _feature_major(x["pool_scale"][l]))
        for name in ("ln1_g", "ln1_b", "ln2_g", "ln2_b"):
            put(f"{name}{l}", _feature_major(x[name][l]))
    order = [c for t in ffn2_up_tiles() for c in t]
    for l in range(2):
        for name in ("mix_pre", "mix_post", "ffn_pre", "ffn_post"):
            put(f"{name}{l}", _feature_major(x[f"l{l}_{name}_norm_2"]))
        put(f"ffn_w{l}", _feature_major(x[f"l{l}_ffn_conv_w_2"][:, order]))
        put(f"ffn_b{l}", _feature_major(x[f"l{l}_ffn_conv_b_2"][order]))
    put("lru_w", _feature_major(x["l0_lru_conv_w_2"]))
    put("lru_b", _feature_major(x["l0_lru_conv_b_2"]))
    put("lru_ba", _feature_major(x["l0_lru_b_a_2"]))
    put("lru_bx", _feature_major(x["l0_lru_b_x_2"]))
    put("lru_lam", _feature_major(x["l0_lru_lambda_2"]))
    sinks = x["l0_attn_sinks_2"]
    put("sinks", np.broadcast_to(sinks[None, :], (P, 16)))
    put("sinks_last", np.repeat(sinks.reshape(2, SWA_J), META, axis=1).transpose(1, 0))
    put("ssm_w", _feature_major(x["l1_ssm_conv_w_2"]))
    put("ssm_b", _feature_major(x["l1_ssm_conv_b_2"]))
    put("dt_bias", x["l1_dt_bias_2"].reshape(-1, 1))
    put("a_log", x["l1_a_log_2"].reshape(-1, 1))
    put("d_skip", _feature_major(np.repeat(x["l1_d_skip_2"], HD)))
    put("gate_norm", _feature_major(x["l1_gate_norm_2"]))
    return par


def kernel(**inputs):
    import concourse.bacc as bacc
    from concourse.bass_utils import run_bass_kernel_spmd

    x = {name: np.asarray(a) for name, a in inputs.items()}
    feature_tiles = lambda a: np.ascontiguousarray(a.reshape(a.shape[0], KT, P).transpose(2, 1, 0))
    stream, small = lay_out_stream(x)
    arrays = {
        "stream": stream,
        "small": small,
        "params": lay_out_parameters(x),
        "consts": constants(),
        "x_t": feature_tiles(x["x"][0]),
        "meta_t": feature_tiles(x["meta_tokens_2"]),
    }
    nc = bacc.Bacc("TRN2", target_bir_lowering=False, num_devices=1)
    args = [nc.dram_tensor(n, a.shape, F32, kind="ExternalInput").ap() for n, a in arrays.items()]
    args.append(nc.dram_tensor("out_t", (P, KT, S), F32, kind="ExternalOutput").ap())
    two_stacks(nc, *args)
    r = run_bass_kernel_spmd(nc, [arrays], core_ids=[0])
    out = np.asarray(r.results[0]["out_t"])
    return np.ascontiguousarray(out.transpose(2, 1, 0).reshape(1, S, D))
```
